# Optimizing a Trainium2 kernel written in Bass

```python
import math
import jax
import jax.numpy as jnp
from jax import lax
import numpy as np

D_MODEL = 1024
BATCH = 1
SEQ = 1024
DEPTH = 2

CTX_LEN = 256
GRID_W = 64
NORM_EPS = 1e-6

MLSTM_WIDTH = 512
MLSTM_HEADS = 4
MLSTM_HEAD_DIM = MLSTM_WIDTH // MLSTM_HEADS
MLSTM_CHUNK = 64

RWKV_WIDTH = 512
RWKV_HEAD_DIM = 64
RWKV_HEADS = RWKV_WIDTH // RWKV_HEAD_DIM
RWKV_DECAY_LORA = 64
RWKV_ICLR_LORA = 64
RWKV_LN_EPS = 64e-5

HGRN_WIDTH = 512
HGRN_HEADS = 4
HGRN_CHUNK = 32

HYENA_WIDTH = 512
HYENA_BANDS = 16
HYENA_POS_DIM = 1 + 2 * HYENA_BANDS
HYENA_FILTER_HIDDEN = 64
HYENA_SIN_FREQ = 1.0
HYENA_FAST_DECAY = 0.3
HYENA_SLOW_DECAY = 1.5
HYENA_TARGET = 1e-2
HYENA_MOD_SHIFT = 0.05

EVEN_SPLITS = (MLSTM_WIDTH,) * 5 + (4 * MLSTM_HEADS,) + (RWKV_WIDTH,) * 4 + (2 * RWKV_DECAY_LORA, 2 * RWKV_ICLR_LORA)
EVEN_IN = sum(EVEN_SPLITS)
ODD_SPLITS = (HGRN_WIDTH,) * 5 + (HYENA_WIDTH,) * 4
ODD_IN = sum(ODD_SPLITS)
MIX_WIDTH_EVEN = MLSTM_WIDTH + RWKV_WIDTH
MIX_WIDTH_ODD = HGRN_WIDTH + HYENA_WIDTH

kernel_name = 'hybrid_mlstm_rwkv7_hgrn2_hyena_dit'

def split_cols(u, sizes):
    return jnp.split(u, np.cumsum(sizes)[:-1].tolist(), axis=-1)

def rmsnorm(x, g):
    xf = x.astype(jnp.float32)
    y = xf * lax.rsqrt(jnp.mean(xf * xf, axis=-1, keepdims=True) + NORM_EPS)
    return (y * g.astype(jnp.float32)).astype(x.dtype)

def heads_rmsnorm(y, g, n_heads):
    B, L, W = y.shape
    yh = y.astype(jnp.float32).reshape(B, L, n_heads, W // n_heads)
    yh = yh * lax.rsqrt(jnp.mean(yh * yh, axis=-1, keepdims=True) + NORM_EPS)
    return yh.reshape(B, L, W) * g.astype(jnp.float32)

def heads_layernorm(y, w, b, n_heads, eps):
    B, L, W = y.shape
    yh = y.astype(jnp.float32).reshape(B, L, n_heads, W // n_heads)
    mu = jnp.mean(yh, axis=-1, keepdims=True)
    var = jnp.mean(jnp.square(yh - mu), axis=-1, keepdims=True)
    yh = (yh - mu) * lax.rsqrt(var + eps)
    return yh.reshape(B, L, W) * w.astype(jnp.float32) + b.astype(jnp.float32)

def adaln(cvec, w_mod, b_mod):
    m = jax.nn.silu(cvec) @ w_mod + b_mod
    return jnp.split(m, 3, axis=-1)

def to_heads(u, n_heads):
    B, L, W = u.shape
    return u.reshape(B, L, n_heads, W // n_heads).transpose(0, 2, 1, 3).astype(jnp.float32)

def from_heads(y):
    B, H, L, d = y.shape
    return y.transpose(0, 2, 1, 3).reshape(B, L, H * d)

def to_chunks(a, T):
    B, H, L = a.shape[:3]
    return jnp.moveaxis(a.reshape(B, H, L // T, T, *a.shape[3:]), 2, 0)

def from_chunks(a):
    nc, B, H, T = a.shape[:4]
    return jnp.moveaxis(a, 0, 2).reshape(B, H, nc * T, *a.shape[4:])

def conv3(u, w):
    up = jnp.pad(u, ((0, 0), (1, 1), (0, 0)))
    return up[:, :-2] * w[0] + up[:, 1:-1] * w[1] + up[:, 2:] * w[2]

def token_shift(u, mu):
    up = jnp.pad(u, ((0, 0), (1, 1), (0, 0)))
    return u + mu * (0.5 * (up[:, :-2] + up[:, 2:]) - u)

def raster_to_column(h):
    B, L, D = h.shape
    rows = L // GRID_W
    return h.reshape(B, rows, GRID_W, D).transpose(0, 2, 1, 3).reshape(B, L, D)

def column_to_raster(h):
    B, L, D = h.shape
    rows = L // GRID_W
    return h.reshape(B, GRID_W, rows, D).transpose(0, 2, 1, 3).reshape(B, L, D)

def bidirectional(scan_fn, init, ctx_shared, ctx_dirs, lat_shared, lat_dirs):
    y_ctx, y_lat = 0.0, 0.0
    for d in range(2):
        orient = (lambda a: a) if d == 0 else (lambda a: jnp.flip(a, axis=2))
        yc, state = scan_fn(tuple(orient(a) for a in ctx_shared + ctx_dirs[d]), init)
        yl, _ = scan_fn(tuple(orient(a) for a in lat_shared + lat_dirs[d]), state)
        y_ctx = y_ctx + orient(yc)
        y_lat = y_lat + orient(yl)
    return y_lat, y_ctx

def mlstm_chunk_scan(inputs, state):
    q, k, v, ig, lf = inputs
    B, H, L, d = q.shape
    mask = jnp.tril(jnp.ones((MLSTM_CHUNK, MLSTM_CHUNK), dtype=bool))

    def step(carry, blk):
        C, n, m = carry
        qc, kc, vc, ic, fc = blk
        b = jnp.cumsum(fc, axis=-1)
        logw = jnp.where(mask, b[..., :, None] - b[..., None, :] + ic[..., None, :], -jnp.inf)
        inter = b + m[..., None]
        m_t = jnp.maximum(inter, jnp.max(logw, axis=-1))
        w = jnp.exp(logw - m_t[..., None])
        s = jnp.exp(inter - m_t)
        qk = jnp.einsum('bhtd,bhsd->bhts', qc, kc) * w
        num = s[..., None] * jnp.einsum('bhtd,bhde->bhte', qc, C) + jnp.einsum('bhts,bhse->bhte', qk, vc)
        den = s * jnp.einsum('bhtd,bhd->bht', qc, n) + jnp.sum(qk, axis=-1)
        h = num / jnp.maximum(jnp.abs(den), jnp.exp(-m_t))[..., None]
        m_new = m_t[..., -1]
        g = jnp.exp(b[..., -1:] - b + ic - m_new[..., None])
        decay = jnp.exp(b[..., -1] + m - m_new)
        C = decay[..., None, None] * C + jnp.einsum('bhs,bhsd,bhse->bhde', g, kc, vc)
        n = decay[..., None] * n + jnp.einsum('bhs,bhsd->bhd', g, kc)
        return (C, n, m_new), h

    state, hs = lax.scan(step, state, tuple(to_chunks(a, MLSTM_CHUNK) for a in inputs))
    return from_chunks(hs), state

def rwkv_scan(inputs, S):
    def step(S, xs):
        r, v, kk, w, k, a = xs
        sa = jnp.einsum('bhvk,bhk->bhv', S, -kk)
        S = S * w[:, :, None, :] + sa[..., None] * (kk * a)[:, :, None, :] + v[..., None] * k[:, :, None, :]
        return S, jnp.einsum('bhvk,bhk->bhv', S, r)

    S, ys = lax.scan(step, S, tuple(jnp.moveaxis(t, 2, 0) for t in inputs))
    return jnp.moveaxis(ys, 0, 2), S

def hgrn_chunk_scan(inputs, S):
    mask = jnp.tril(jnp.ones((HGRN_CHUNK, HGRN_CHUNK), dtype=bool))[:, :, None]

    def step(S, blk):
        qc, vc, kc, gc = blk
        b = jnp.cumsum(gc, axis=2)
        o = jnp.einsum('bhtd,bhde->bhte', qc * jnp.exp(b), S)
        pair = jnp.exp(jnp.where(mask, b[:, :, :, None] - b[:, :, None], -jnp.inf))
        A = jnp.einsum('bhtd,bhtsd,bhsd->bhts', qc, pair, kc)
        o = o + jnp.einsum('bhts,bhse->bhte', A, vc)
        b_end = b[:, :, -1]
        S = jnp.exp(b_end)[..., None] * S + jnp.einsum('bhsd,bhse->bhde', kc * jnp.exp(b_end[:, :, None] - b), vc)
        return S, o

    S, os_ = lax.scan(step, S, tuple(to_chunks(a, HGRN_CHUNK) for a in inputs))
    return from_chunks(os_), S

def hyena_filters(L, p):
    f32 = jnp.float32
    pos = jnp.arange(L, dtype=f32)
    t = pos / L
    bands = jnp.linspace(1e-4, HYENA_BANDS - 1, HYENA_BANDS, dtype=f32)
    ang = (2.0 * math.pi / L) * pos[:, None] * bands
    z = jnp.concatenate([t[:, None], jnp.cos(ang), jnp.sin(ang)], axis=-1)
    hid = jnp.sin(HYENA_SIN_FREQ * (z @ p['y_w1'].astype(f32) + p['y_b1'].astype(f32)))
    hid = jnp.sin(HYENA_SIN_FREQ * (hid @ p['y_w2'].astype(f32) + p['y_b2'].astype(f32)))
    filt = (hid @ p['y_w3'].astype(f32)).reshape(L, 2, HYENA_WIDTH)
    max_decay = math.log(HYENA_TARGET) / HYENA_FAST_DECAY
    min_decay = math.log(HYENA_TARGET) / HYENA_SLOW_DECAY
    deltas = jnp.abs(jnp.linspace(min_decay, max_decay, HYENA_WIDTH, dtype=f32))
    window = jnp.exp(-t[:, None] * deltas) + HYENA_MOD_SHIFT
    filt = filt * window[:, None]
    filt = filt / jnp.sum(jnp.abs(filt), axis=(0, 1), keepdims=True)
    return filt[:, 0], filt[:, 1]

def long_conv_bidir(u, h_fwd, h_bwd, bias):
    B, L, C = u.shape
    kern = jnp.concatenate([h_fwd[:1] + h_bwd[:1], h_fwd[1:], jnp.zeros((1, C), jnp.float32),
                            jnp.flip(h_bwd[1:], axis=0)], axis=0)
    uf = u.astype(jnp.float32)
    spec = jnp.fft.rfft(uf, n=2 * L, axis=1) * jnp.fft.rfft(kern, axis=0)[None]
    y = jnp.fft.irfft(spec, n=2 * L, axis=1)[:, :L]
    return y + uf * bias.astype(jnp.float32)

def hyena_branch(v_in, g0, g1, p):
    L = v_in.shape[1]
    s = conv3(jnp.concatenate([v_in, g0, g1], axis=-1), p['y_short_w']) + p['y_short_b']
    v, x0, x1 = jnp.split(s, 3, axis=-1)
    h_fwd, h_bwd = hyena_filters(L, p)
    return x0 * long_conv_bidir(x1 * v, h_fwd, h_bwd, p['y_bias'])

def even_prep(h, p):
    B, L, _ = h.shape
    f32 = jnp.float32
    mq, mk, mv, mo, mz, mg, rr, rk, rv, rz, wd, ad = split_cols(h @ p['w_in'], EVEN_SPLITS)
    q = jax.nn.silu(conv3(mq, p['m_conv_w'][:, :MLSTM_WIDTH]))
    k = jax.nn.silu(conv3(mk, p['m_conv_w'][:, MLSTM_WIDTH:])) * (MLSTM_HEAD_DIM ** -0.5)
    g = (mg + p['m_gate_b']).astype(f32).reshape(B, L, 2, 2, MLSTM_HEADS).transpose(2, 3, 0, 4, 1)
    m_shared = (to_heads(q, MLSTM_HEADS), to_heads(k, MLSTM_HEADS), to_heads(mv, MLSTM_HEADS))
    m_dirs = tuple((g[d, 0], jax.nn.log_sigmoid(g[d, 1])) for d in range(2))
    r = token_shift(rr.astype(f32), p['r_mu'][0])
    kr = token_shift(rk.astype(f32), p['r_mu'][1])
    v = token_shift(rv.astype(f32), p['r_mu'][2])
    kk = to_heads(kr * p['r_k_k'], RWKV_HEADS)
    kk = kk / jnp.maximum(jnp.sqrt(jnp.sum(kk * kk, axis=-1, keepdims=True)), 1e-12)
    wd = jnp.tanh(wd.astype(f32)).reshape(B, L, 2, RWKV_DECAY_LORA)
    w_raw = p['r_w0'] + jnp.einsum('bldr,drc->bldc', wd, p['r_w_up'])
    decay = jnp.exp(-jnp.exp(-jax.nn.softplus(-w_raw) - 0.5))
    ad = ad.astype(f32).reshape(B, L, 2, RWKV_ICLR_LORA)
    a = jax.nn.sigmoid(p['r_a0'] + jnp.einsum('bldr,drc->bldc', ad, p['r_a_up']))
    kt = kr[:, :, None] * (1.0 + (a - 1.0) * p['r_k_a'])
    r_shared = (to_heads(r, RWKV_HEADS), to_heads(v, RWKV_HEADS), kk)
    r_dirs = tuple((to_heads(decay[:, :, d], RWKV_HEADS), to_heads(kt[:, :, d], RWKV_HEADS),
                    to_heads(a[:, :, d], RWKV_HEADS)) for d in range(2))
    coef = jnp.einsum('blhn,bldhn,hn->blh', r.reshape(B, L, RWKV_HEADS, RWKV_HEAD_DIM),
                      kt.reshape(B, L, 2, RWKV_HEADS, RWKV_HEAD_DIM), p['r_r_k'])
    bonus = (coef[..., None] * v.reshape(B, L, RWKV_HEADS, RWKV_HEAD_DIM)).reshape(B, L, RWKV_WIDTH)
    return {'m_shared': m_shared, 'm_dirs': m_dirs, 'mo': mo, 'mz': mz,
            'r_shared': r_shared, 'r_dirs': r_dirs, 'bonus': bonus, 'rz': rz}

def mixer_even(h_lat, h_ctx, p, need_ctx):
    lat = even_prep(h_lat, p)
    ctx = even_prep(h_ctx, p)
    B = h_lat.shape[0]
    f32 = jnp.float32
    m_init = (jnp.zeros((B, MLSTM_HEADS, MLSTM_HEAD_DIM, MLSTM_HEAD_DIM), f32),
              jnp.zeros((B, MLSTM_HEADS, MLSTM_HEAD_DIM), f32),
              jnp.zeros((B, MLSTM_HEADS), f32))
    r_init = jnp.zeros((B, RWKV_HEADS, RWKV_HEAD_DIM, RWKV_HEAD_DIM), f32)
    m_lat, m_ctx = bidirectional(mlstm_chunk_scan, m_init, ctx['m_shared'], ctx['m_dirs'], lat['m_shared'], lat['m_dirs'])
    r_lat, r_ctx = bidirectional(rwkv_scan, r_init, ctx['r_shared'], ctx['r_dirs'], lat['r_shared'], lat['r_dirs'])

    def finish(pre, m_h, r_h, dtype):
        m_y = heads_rmsnorm(from_heads(m_h), p['m_norm_g'], MLSTM_HEADS) * jax.nn.sigmoid(pre['mo']) * jax.nn.silu(pre['mz'])
        r_y = heads_layernorm(from_heads(r_h) + pre['bonus'], p['r_ln_w'], p['r_ln_b'], RWKV_HEADS, RWKV_LN_EPS) * jax.nn.silu(pre['rz'])
        return jnp.concatenate([m_y, r_y], axis=-1).astype(dtype) @ p['w_out']

    y_lat = finish(lat, m_lat, r_lat, h_lat.dtype)
    y_ctx = finish(ctx, m_ctx, r_ctx, h_ctx.dtype) if need_ctx else None
    return y_lat, y_ctx

def odd_prep(h, p, lb):
    gq, gi, gf_fwd, gf_bwd, gz, yv, y0, y1, yz = split_cols(h @ p['w_in'], ODD_SPLITS)

    def forget(ff):
        log_f = jnp.logaddexp(jnp.log(lb), jnp.log1p(-lb) + jax.nn.log_sigmoid(ff.astype(jnp.float32)))
        return (to_heads(-jnp.expm1(log_f), HGRN_HEADS), to_heads(log_f, HGRN_HEADS))

    return {'g_shared': (to_heads(gq, HGRN_HEADS), to_heads(gi, HGRN_HEADS)),
            'g_dirs': (forget(gf_fwd), forget(gf_bwd)), 'gz': gz,
            'yv': yv, 'y0': y0, 'y1': y1, 'yz': yz}

def mixer_odd(h_lat, h_ctx, p, li, need_ctx):
    probs = jax.nn.softmax(p['lb_all'].astype(jnp.float32), axis=0)
    lb = (jnp.cumsum(probs, axis=0) - probs[0])[li]
    lat = odd_prep(h_lat, p, lb)
    ctx = odd_prep(h_ctx, p, lb)
    B = h_lat.shape[0]
    dh = HGRN_WIDTH // HGRN_HEADS
    init = jnp.zeros((B, HGRN_HEADS, dh, dh), jnp.float32)
    g_lat, g_ctx = bidirectional(hgrn_chunk_scan, init, ctx['g_shared'], ctx['g_dirs'], lat['g_shared'], lat['g_dirs'])

    def finish(pre, g_h, dtype):
        g_y = heads_rmsnorm(from_heads(g_h), p['g_norm_g'], HGRN_HEADS) * jax.nn.silu(pre['gz'])
        y_y = hyena_branch(pre['yv'], pre['y0'], pre['y1'], p) * jax.nn.silu(pre['yz'])
        return jnp.concatenate([g_y, y_y], axis=-1).astype(dtype) @ p['w_out']

    y_lat = finish(lat, g_lat, h_lat.dtype)
    y_ctx = finish(ctx, g_ctx, h_ctx.dtype) if need_ctx else None
    return y_lat, y_ctx

def trunk_layer(x, xc, c, c_ctx, li, p, need_ctx):
    shift, scale, gate = adaln(c, p['mod_w'], p['mod_b'])
    c_shift, c_scale, c_gate = adaln(c_ctx, p['mod_w'], p['mod_b'])
    h = rmsnorm(x, p['norm_g']) * (1.0 + scale[:, None]) + shift[:, None]
    hc = rmsnorm(xc, p['norm_g']) * (1.0 + c_scale) + c_shift
    if li % 2 == 0:
        y, yc = mixer_even(h, hc, p, need_ctx)
    else:
        y, yc = mixer_odd(raster_to_column(h), hc, p, li, need_ctx)
        y = column_to_raster(y)
    x = x + gate[:, None] * y
    if need_ctx:
        xc = xc + c_gate * yc
    return x, xc

def setup_inputs(seed: int = 0) -> dict:
    key = jax.random.key(seed)
    keys = jax.random.split(key, 64)
    count = [0]
    f32 = jnp.float32

    def nrm(shape, scale=1.0):
        k = keys[count[0]]
        count[0] += 1
        return scale * jax.random.normal(k, shape, f32)

    D = D_MODEL
    H = HYENA_FILTER_HIDDEN
    ident3 = jnp.array([0.0, 1.0, 0.0], f32)[:, None]
    f_bias = jnp.linspace(3.0, 6.0, MLSTM_HEADS, dtype=f32)
    return {
        'x': nrm((BATCH, SEQ, D)),
        'c': nrm((BATCH, D)),
        'ctx': nrm((BATCH, CTX_LEN, D)),
        'c_ctx': nrm((D,)),
        'l0_norm_g': 1.0 + nrm((D,), 0.02),
        'l0_mod_w': nrm((D, 3 * D), 0.5 * D ** -0.5),
        'l0_mod_b': nrm((3 * D,), 0.01),
        'l0_w_in': nrm((D, EVEN_IN), D ** -0.5),
        'l0_w_out': nrm((MIX_WIDTH_EVEN, D), MIX_WIDTH_EVEN ** -0.5),
        'l0_mlstm_conv_w': ident3 + nrm((3, 2 * MLSTM_WIDTH), 0.2),
        'l0_mlstm_gate_b': jnp.stack([nrm((2, MLSTM_HEADS), 0.1), f_bias + nrm((2, MLSTM_HEADS), 0.1)], axis=1).reshape(-1),
        'l0_mlstm_norm_g': 1.0 + nrm((MLSTM_WIDTH,), 0.02),
        'l0_rwkv_mu': 0.5 + nrm((3, RWKV_WIDTH), 0.1),
        'l0_rwkv_w0': jnp.linspace(-6.5, -1.5, RWKV_WIDTH, dtype=f32)[None] + nrm((2, RWKV_WIDTH), 0.1),
        'l0_rwkv_w_up': nrm((2, RWKV_DECAY_LORA, RWKV_WIDTH), 0.1 * RWKV_DECAY_LORA ** -0.5),
        'l0_rwkv_a0': nrm((2, RWKV_WIDTH), 0.1),
        'l0_rwkv_a_up': nrm((2, RWKV_ICLR_LORA, RWKV_WIDTH), 0.1 * RWKV_ICLR_LORA ** -0.5),
        'l0_rwkv_k_k': 0.85 + nrm((RWKV_WIDTH,), 0.02),
        'l0_rwkv_k_a': 1.0 + nrm((RWKV_WIDTH,), 0.02),
        'l0_rwkv_r_k': nrm((RWKV_HEADS, RWKV_HEAD_DIM), 0.1),
        'l0_rwkv_ln_w': 1.0 + nrm((RWKV_WIDTH,), 0.02),
        'l0_rwkv_ln_b': nrm((RWKV_WIDTH,), 0.01),
        'hgrn_lower_bounds': nrm((DEPTH, HGRN_WIDTH), 0.1),
        'l1_norm_g': 1.0 + nrm((D,), 0.02),
        'l1_mod_w': nrm((D, 3 * D), 0.5 * D ** -0.5),
        'l1_mod_b': nrm((3 * D,), 0.01),
        'l1_w_in': nrm((D, ODD_IN), D ** -0.5),
        'l1_w_out': nrm((MIX_WIDTH_ODD, D), MIX_WIDTH_ODD ** -0.5),
        'l1_hgrn_norm_g': 1.0 + nrm((HGRN_WIDTH,), 0.02),
        'l1_hyena_short_w': ident3 + nrm((3, 3 * HYENA_WIDTH), 0.2),
        'l1_hyena_short_b': nrm((3 * HYENA_WIDTH,), 0.01),
        'l1_hyena_w1': nrm((HYENA_POS_DIM, H), HYENA_POS_DIM ** -0.5),
        'l1_hyena_b1': nrm((H,), 0.1),
        'l1_hyena_w2': nrm((H, H), H ** -0.5),
        'l1_hyena_b2': nrm((H,), 0.1),
        'l1_hyena_w3': nrm((H, 2 * HYENA_WIDTH), H ** -0.5),
        'l1_hyena_bias': nrm((HYENA_WIDTH,), 0.5),
        'final_norm_g': 1.0 + nrm((D,), 0.02),
    }

def reference(x, c, ctx, c_ctx, l0_norm_g, l0_mod_w, l0_mod_b, l0_w_in, l0_w_out,
              l0_mlstm_conv_w, l0_mlstm_gate_b, l0_mlstm_norm_g,
              l0_rwkv_mu, l0_rwkv_w0, l0_rwkv_w_up, l0_rwkv_a0, l0_rwkv_a_up,
              l0_rwkv_k_k, l0_rwkv_k_a, l0_rwkv_r_k, l0_rwkv_ln_w, l0_rwkv_ln_b,
              hgrn_lower_bounds,
              l1_norm_g, l1_mod_w, l1_mod_b, l1_w_in, l1_w_out, l1_hgrn_norm_g,
              l1_hyena_short_w, l1_hyena_short_b, l1_hyena_w1, l1_hyena_b1,
              l1_hyena_w2, l1_hyena_b2, l1_hyena_w3, l1_hyena_bias, final_norm_g):
    even_p = {'norm_g': l0_norm_g, 'mod_w': l0_mod_w, 'mod_b': l0_mod_b, 'w_in': l0_w_in, 'w_out': l0_w_out,
              'm_conv_w': l0_mlstm_conv_w, 'm_gate_b': l0_mlstm_gate_b, 'm_norm_g': l0_mlstm_norm_g,
              'r_mu': l0_rwkv_mu, 'r_w0': l0_rwkv_w0, 'r_w_up': l0_rwkv_w_up, 'r_a0': l0_rwkv_a0,
              'r_a_up': l0_rwkv_a_up, 'r_k_k': l0_rwkv_k_k, 'r_k_a': l0_rwkv_k_a, 'r_r_k': l0_rwkv_r_k,
              'r_ln_w': l0_rwkv_ln_w, 'r_ln_b': l0_rwkv_ln_b}
    odd_p = {'norm_g': l1_norm_g, 'mod_w': l1_mod_w, 'mod_b': l1_mod_b, 'w_in': l1_w_in, 'w_out': l1_w_out,
             'lb_all': hgrn_lower_bounds, 'g_norm_g': l1_hgrn_norm_g,
             'y_short_w': l1_hyena_short_w, 'y_short_b': l1_hyena_short_b,
             'y_w1': l1_hyena_w1, 'y_b1': l1_hyena_b1, 'y_w2': l1_hyena_w2, 'y_b2': l1_hyena_b2,
             'y_w3': l1_hyena_w3, 'y_bias': l1_hyena_bias}
    layer_params = (even_p, odd_p)
    xc = ctx
    for li in range(DEPTH):
        x, xc = trunk_layer(x, xc, c, c_ctx, li, layer_params[li], li < DEPTH - 1)
    return rmsnorm(x, final_norm_g)


_drawn_inputs = setup_inputs


def setup_inputs(seed=0):
    import zlib

    import numpy as np

    out = dict(_drawn_inputs(seed))
    spreads = {}
    factors = {'c_ctx': 2.988,
     'l0_norm_g': 8.0,
     'l0_mod_b': 7.23,
     'l0_mlstm_conv_w': 2.834,
     'l0_mlstm_norm_g': 8.0,
     'l0_rwkv_w_up': 8.0,
     'l0_rwkv_a0': 8.0,
     'l0_rwkv_a_up': 8.0,
     'l0_rwkv_k_k': 6.972,
     'l0_rwkv_k_a': 6.967,
     'l0_rwkv_r_k': 8.0,
     'l0_rwkv_ln_w': 8.0,
     'l0_rwkv_ln_b': 26.047,
     'hgrn_lower_bounds': 29.939,
     'l1_norm_g': 8.0,
     'l1_mod_b': 7.754,
     'l1_hgrn_norm_g': 64.0,
     'l1_hyena_short_b': 27.801,
     'l1_hyena_w1': 5.876,
     'l1_hyena_b1': 8.0,
     'l1_hyena_w2': 5.641,
     'l1_hyena_b2': 8.0,
     'l1_hyena_w3': 5.799,
     'final_norm_g': 8.178}
    for name, (base, spread) in spreads.items():
        noise = np.random.default_rng([zlib.crc32(name.encode()), seed]).standard_normal(out[name].shape)
        drawn = base * np.exp(spread * noise) if base else spread * noise
        out[name] = jnp.asarray(drawn.astype(out[name].dtype))
    for name, factor in factors.items():
        out[name] = (out[name] * factor).astype(out[name].dtype)
    return out
```

```python
from contextlib import ExitStack

import numpy as np

import concourse.bass as bass
from concourse import mybir

F32 = mybir.dt.float32
U32 = mybir.dt.uint32
ALU = mybir.AluOpType
ACT = mybir.ActivationFunctionType
AX = mybir.AxisListType

P = 128
D = 1024
KT = D // P
CTX, LAT = 256, 1024
TOK = CTX + LAT
TILES = TOK // P
CTX_TILES = CTX // P
W = 512
WT = W // P
GRID_W = 64
GRID_H = LAT // GRID_W
EPS = 1e-6
GROUPS = ((0, 256), (256, 512), (768, 512))
BANK = 512

M_HEADS, M_CHUNK = 4, 128
R_HEADS, R_DIM, R_CHUNK = 8, 64, 64
R_LN_EPS = 64e-5
GATE_ROWS = 36


def columns(spec):
    at, where = 0, {}
    for name, width in spec:
        where[name] = (at, width)
        at += width
    return where, at


PARAMS, N_PARAMS = columns([
    ("l0_norm_g", 8), ("l1_norm_g", 8), ("conv_w", 24), ("m_norm_g", 4), ("r_mu", 12), ("r_w0", 8),
    ("r_a0", 8), ("r_k_k", 4), ("r_k_a", 4), ("r_r_k", 4), ("r_ln_w", 4), ("r_ln_b", 4), ("lower", 8),
    ("g_norm_g", 4), ("short_w", 36), ("short_b", 12), ("y_bias", 4), ("b1", 1), ("b2", 1),
    ("gate_b_i", 1), ("gate_b_f", 1), ("c", 16)])
CONSTS, N_CONSTS = columns([("ident", 128), ("ones", 128), ("head_ones", 128), ("row2", 256)])


def const_common():
    a = np.zeros((P, N_CONSTS), np.float32)
    a[:, 0:128] = np.eye(128)
    a[:, 128:256] = 1
    a[:, 256:384] = np.kron(np.eye(2), np.ones((64, 64)))
    a[0, 384:512] = 1
    a[1, 512:640] = 1
    return a


def const_mlstm():
    s, t = np.arange(P)[:, None], np.arange(P)[None]
    a = np.zeros((P, 2 * P + 8 * P), np.float32)
    a[:, 0:P] = np.where(s <= t, 0, -1e30)
    a[:, P:2 * P] = np.where(s >= t, 0, -1e30)
    for d in range(2):
        for h in range(M_HEADS):
            r = d * M_HEADS + h
            a[32 * d + h, 2 * P + r * P:2 * P + (r + 1) * P] = 1
    return a


class Program:

    SEMAPHORES_KEPT_FREE = 40

    def __init__(self, nc, ctx, dram):
        self.nc, self.ctx, self.dram = nc, ctx, dram
        scratch = lambda name, shape: nc.dram_tensor(f"scratch_{name}", shape, F32).ap()
        self.scratch = {"mix": scratch("mix", [KT, P, TOK]), "spill": scratch("spill", [3, WT, P, TOK]),
                        "gate": scratch("gate", [2, P, 2, D]), "x1": scratch("x1", [TOK, D]),
                        "z": scratch("z", [P, LAT // P, W])}
        self.stages, self.in_use, self.free = 0, [], 144
        self.x1_stored = [nc.alloc_semaphore(name=f"x1_stored{i}") for i in range(2)]
        self.out_stored = [nc.alloc_semaphore(name=f"out_stored{i}") for i in range(2)]
        self.psum = ctx.enter_context(nc.psum_tensor("psum", [P, 8, BANK], F32))
        self.consts = self.keep("consts", [P, N_CONSTS])
        self.params = self.keep("params", [P, N_PARAMS])

    def keep(self, name, shape, dtype=F32):
        return self.ctx.enter_context(self.nc.sbuf_tensor(name, shape, dtype))

    def begin_stage(self):
        self.stages += 1
        if self.free < self.SEMAPHORES_KEPT_FREE:
            self.nc.clear_and_free_semaphores(self.in_use)
            self.nc.all_engine_barrier()
            self.free += len(self.in_use)
            self.in_use = []

    def semaphore(self, name):
        self.in_use.append(self.nc.alloc_semaphore(name=f"{name}_{self.stages}"))
        self.free -= 1
        return self.in_use[-1]

    def semaphores(self, name, n):
        return [self.semaphore(f"{name}{i}") for i in range(n)]

    def const(self, name, rows=P):
        at, width = CONSTS[name]
        return self.consts[0:rows, at:at + width]

    def param(self, name, i, rows=P):
        at = PARAMS[name][0] + i
        return self.params[0:rows, at:at + 1]


def stage_copies(p, copies):
    p.begin_stage()
    copied = p.semaphore("copied")
    with p.nc.Block() as block:
        @block.sync
        def _(sp):
            for dst, of in copies:
                sp.dma_start(dst, of).then_inc(copied, 16)
            sp.wait_ge(copied, 16 * len(copies))


def stage_modulation(p, layer, norm_scale, norm_shift, gate_dram):
    nc = p.nc
    SLOTS = 3
    p.begin_stage()
    weight_loaded = p.semaphores("mod_weight_loaded", SLOTS)
    bias_loaded = p.semaphore("mod_bias_loaded")
    silu_ready = p.semaphore("mod_silu_ready")
    products_ready = p.semaphore("mod_products_ready")
    rows_ready = p.semaphore("mod_rows_ready")
    columns_ready = p.semaphore("mod_columns_ready")
    gates_ready = p.semaphore("mod_gates_ready")
    gates_spread = p.semaphore("mod_gates_spread")
    gate_stored = p.semaphore("mod_gate_stored")
    scaled = p.semaphore("mod_scaled")
    mod_w = p.dram[f"l{layer}_mod_w"].rearrange("(p k) n -> p k n", k=KT)
    at_c = PARAMS["c"][0]
    with ExitStack() as local:
        sb = lambda name, shape: local.enter_context(nc.sbuf_tensor(f"{name}_{layer}", shape, F32))
        weight = sb("mod_weight", [P, SLOTS, 3 * D])
        silu = sb("mod_silu", [P, KT, 2])
        bias = sb("mod_bias", [2, 3 * D])
        rows = sb("mod_rows", [2, 3 * D])
        gate = sb("mod_gate", [P, 2, D])
        with nc.Block() as block:
            @block.sync
            def _(sp):
                sp.dma_start(bias[:, :], p.dram[f"mod_b{layer}"]).then_inc(bias_loaded, 16)
                for k in range(KT):
                    if k >= SLOTS:
                        sp.wait_ge(products_ready, k - SLOTS + 1)
                    sp.dma_start(weight[:, k % SLOTS, :], mod_w[:, k, :]).then_inc(weight_loaded[k % SLOTS], 16)
                sp.wait_ge(gates_spread, 4)
                sp.dma_start(gate_dram, gate[:, :, :]).then_inc(gate_stored, 16)
                sp.wait_ge(gate_stored, 16)

            @block.scalar
            def _(act):
                nc.scalar.activation(
                    silu[:, :, :], p.params[:, at_c:at_c + 16].rearrange("p (r k) -> p k r", r=2), ACT.Silu).then_inc(silu_ready, 1)
                for r in range(2):
                    for half in range(2):
                        act.wait_ge(gates_ready, 2 * r + half + 1)
                        nc.scalar.copy(gate[:, r, half * BANK:(half + 1) * BANK],
                                                   p.psum[:, 2 * r + half, :]).then_inc(gates_spread, 1)

            @block.tensor
            def _(pe):
                pe.wait_ge(silu_ready, 1)
                for k in range(KT):
                    pe.wait_ge(weight_loaded[k % SLOTS], 16 * (k // SLOTS + 1))
                    for g in range(6):
                        last = nc.tensor.matmul(p.psum[0:2, g, :], silu[:, k, :],
                                                weight[:, k % SLOTS, g * BANK:(g + 1) * BANK],
                                                start=(k == 0), stop=(k == KT - 1))
                    last.then_inc(products_ready, 1)
                pe.wait_ge(rows_ready, 1)
                for i in range(16):
                    last = nc.tensor.transpose(p.psum[:, 6, 2 * i:2 * i + 2], rows[:, i * P:(i + 1) * P],
                                               p.const("ident")[0:2, 0:2])
                last.then_inc(columns_ready, 1)
                for r in range(2):
                    for half in range(2):
                        nc.tensor.matmul(
                            p.psum[:, 2 * r + half, :], p.const("row2", 2)[:, r * P:(r + 1) * P],
                            rows[:, 2 * D + half * BANK:2 * D + (half + 1) * BANK], start=True, stop=True).then_inc(gates_ready, 1)

            @block.vector
            def _(dve):
                dve.wait_ge(bias_loaded, 16)
                dve.wait_ge(products_ready, KT)
                nc.vector.tensor_tensor(
                    rows[:, :], p.psum[0:2, 0:6, :].rearrange("p g n -> p (g n)"), bias[:, :], ALU.add).then_inc(rows_ready, 1)
                dve.wait_ge(columns_ready, 1)
                cols = p.psum[:, 6, 0:32].rearrange("p (s k r) -> p s k r", s=2, r=2)
                gains = p.params[:, PARAMS[f"l{layer}_norm_g"][0]:][:, 0:KT]
                nc.vector.tensor_copy(norm_shift[:, :, :], cols[:, 0])
                for r in range(2):
                    nc.vector.scalar_tensor_tensor(
                        norm_scale[:, :, r], cols[:, 1, :, r], 1.0, gains, ALU.add, ALU.mult).then_inc(scaled, 1)


def stage_norm_transpose(p, layer, x, norm_scale, norm_shift, hT):
    nc = p.nc
    SLOTS = 3
    p.begin_stage()
    x_loaded = p.semaphores("norm_x_loaded", SLOTS)
    squares_ready = p.semaphore("norm_squares_ready")
    mean_ready = p.semaphore("norm_mean_ready")
    root_ready = p.semaphore("norm_root_ready")
    inverse_ready = p.semaphore("norm_inverse_ready")
    normed = p.semaphore("norm_normed")
    turned = p.semaphore("norm_turned")
    written = p.semaphore("norm_written")
    with ExitStack() as local:
        sb = lambda name, shape: local.enter_context(nc.sbuf_tensor(f"{name}_{layer}", shape, F32))
        xt = sb("norm_x", [P, SLOTS, D])
        junk = sb("norm_junk", [P, D])
        stat = sb("norm_stat", [P, TILES, 4])
        with nc.Block() as block:
            @block.sync
            def _(sp):
                for i in range(TILES):
                    if i >= SLOTS:
                        sp.wait_ge(turned, i - SLOTS + 1)
                    sp.dma_start(xt[:, i % SLOTS, :], x(i)).then_inc(x_loaded[i % SLOTS], 16)

            @block.scalar
            def _(act):
                for i in range(TILES):
                    act.wait_ge(x_loaded[i % SLOTS], 16 * (i // SLOTS + 1))
                    if i:
                        if i:
                            act.wait_ge(squares_ready, i)
                    nc.scalar.activation(junk[:, :], xt[:, i % SLOTS, :], ACT.Square,
                                                            accum_out=stat[:, i, 0:1]).then_inc(squares_ready, 1)
                    act.wait_ge(mean_ready, i + 1)
                    nc.scalar.activation(stat[:, i, 2:3], stat[:, i, 1:2], ACT.Sqrt).then_inc(root_ready, 1)

            @block.tensor
            def _(pe):
                for i in range(TILES):
                    pe.wait_ge(normed, i + 1)
                    if i >= 2:
                        pe.wait_ge(written, i - 1)
                    for k in range(KT):
                        last = nc.tensor.transpose(
                            p.psum[:, 2 * (i % 2) + k // 4, (k % 4) * P:(k % 4 + 1) * P],
                            xt[:, i % SLOTS, k * P:(k + 1) * P], p.const("ident"))
                    last.then_inc(turned, 1)

            @block.vector
            def _(dve):
                for i in range(TILES):
                    dve.wait_ge(squares_ready, i + 1)
                    nc.vector.tensor_scalar(stat[:, i, 1:2], stat[:, i, 0:1], 1.0 / D, EPS,
                                                            ALU.mult, ALU.add).then_inc(mean_ready, 1)
                    dve.wait_ge(root_ready, i + 1)
                    nc.vector.reciprocal(stat[:, i, 3:4], stat[:, i, 2:3]).then_inc(inverse_ready, 1)
                    dve.wait_ge(inverse_ready, i + 1)
                    nc.vector.tensor_scalar(xt[:, i % SLOTS, :], xt[:, i % SLOTS, :],
                                                        stat[:, i, 3:4], None, ALU.mult).then_inc(normed, 1)
                    dve.wait_ge(turned, i + 1)
                    r = 1 if i < CTX_TILES else 0
                    for k in range(KT):
                        src = p.psum[:, 2 * (i % 2) + k // 4, (k % 4) * P:(k % 4 + 1) * P]
                        if layer == 0 or i < CTX_TILES:
                            dst = hT[:, k, i * P:(i + 1) * P]
                        else:
                            rows = P // GRID_W
                            first = (i - CTX_TILES) * rows
                            dst = hT[:, k, CTX:TOK].rearrange("p (c r) -> p r c", r=GRID_H)[:, first:first + rows, :]
                            src = src.rearrange("p (r c) -> p r c", r=rows)
                        last = nc.vector.tensor_scalar(dst, src, norm_scale[:, k, r:r + 1],
                                                       norm_shift[:, k, r:r + 1], ALU.mult, ALU.add)
                    last.then_inc(written, 1)


def stage_project(p, name, hT, w_dram, jobs):
    nc = p.nc
    SLOTS = 2
    p.begin_stage()
    weight_loaded = p.semaphores("project_weight_loaded", SLOTS)
    products_ready = p.semaphore("project_products_ready")
    copied = p.semaphore("project_copied")
    w_view = w_dram.rearrange("(k p) n -> p k n", p=P)

    def units(job):
        col, width, func, dst, token_major, groups = job
        if token_major:
            first, end, offset = (*groups, 0)[:3]
            for i in range(first, end):
                yield P, width, (lambda k, w, i=i: (hT[:, k, i * P:(i + 1) * P], w[:, k, 0:width])), dst[:, i - offset]
        else:
            for j in range((width + P - 1) // P):
                m = min(P, width - j * P)
                for at, n, *to in groups:
                    to = to[0] if to else at
                    yield m, n, (lambda k, w, j=j, m=m, at=at, n=n: (w[:, k, j * P:j * P + m], hT[:, k, at:at + n])), \
                        (dst[:, j, to:to + n] if width > P else dst[0:m, to:to + n])

    ends = np.cumsum([sum(1 for _ in units(job)) for job in jobs]).tolist()
    with ExitStack() as local:
        weight = local.enter_context(nc.sbuf_tensor(f"project_weight_{name}", [P, SLOTS, KT, W], F32))
        with nc.Block() as block:
            @block.sync
            def _(sp):
                for b, (col, width, *_) in enumerate(jobs):
                    if b >= SLOTS:
                        sp.wait_ge(products_ready, ends[b - SLOTS])
                    src = (p.dram[col].rearrange("(k p) n -> p k n", p=P) if isinstance(col, str)
                           else w_view[:, :, col:col + width])
                    sp.dma_start(weight[:, b % SLOTS, :, 0:width], src).then_inc(weight_loaded[b % SLOTS], 16)

            @block.tensor
            def _(pe):
                u = 0
                for b, job in enumerate(jobs):
                    pe.wait_ge(weight_loaded[b % SLOTS], 16 * (b // SLOTS + 1))
                    for rows, n, operands, _ in units(job):
                        if u >= 8:
                            pe.wait_ge(copied, u - 7)
                        for k in range(KT):
                            lhsT, rhs = operands(k, weight[:, b % SLOTS])
                            last = nc.tensor.matmul(p.psum[0:rows, u % 8, 0:n], lhsT, rhs,
                                                    start=(k == 0), stop=(k == KT - 1))
                        last.then_inc(products_ready, 1)
                        u += 1

            @block.scalar
            def _(act):
                u = 0
                for job in jobs:
                    for rows, n, _, dst in units(job):
                        act.wait_ge(products_ready, u + 1)
                        src = p.psum[0:rows, u % 8, 0:n]
                        if len(dst.shape) == 3:
                            src = src.rearrange("p (a b) -> p a b", a=dst.shape[1])
                        nc.scalar.activation(dst, src, job[2]).then_inc(copied, 1)
                        u += 1


def conv3_steps(nc, then, dst, src, taps, ready):
    before, here, after = taps
    then(nc.vector.tensor_scalar(dst, src, here, None, ALU.mult))
    for a, n in ((0, CTX), (CTX, LAT)):
        out = dst[:, a + 1:a + n]
        then(nc.vector.scalar_tensor_tensor(out, src[:, a:a + n - 1], before, out, ALU.mult, ALU.add))
    for a, n in ((0, CTX), (CTX, LAT)):
        out = dst[:, a:a + n - 1]
        nc.vector.scalar_tensor_tensor(out, src[:, a + 1:a + n], after, out, ALU.mult, ALU.add).then_inc(ready, 1)


def stage_conv_qk(p, raw, out, which):
    nc = p.nc
    p.begin_stage()
    chain = p.semaphore("dve_chain")
    conv_ready = p.semaphore("conv_ready")
    silu_done = p.semaphore("conv_silu_done")
    with nc.Block() as block:
        @block.vector
        def _(dve):
            made = [0]

            def then(instruction):
                made[0] += 1
                instruction.then_inc(chain, 1)
                dve.wait_ge(chain, made[0])

            for j in range(WT):
                conv3_steps(nc, then, out[:, j, :], raw[:, j, :],
                            [p.param("conv_w", 8 * tap + WT * which + j) for tap in range(3)], conv_ready)

        @block.scalar
        def _(act):
            for j in range(WT):
                act.wait_ge(conv_ready, 2 * (j + 1))
                nc.scalar.activation(out[:, j, :], out[:, j, :], ACT.Silu).then_inc(silu_done, 1)
                if which == 1:
                    act.wait_ge(silu_done, 2 * j + 1)
                    nc.scalar.mul(out[:, j, :], out[:, j, :], float(P) ** -0.5).then_inc(silu_done, 1)


def stage_gate_rows(p, gate_i, gate_f, rows, carry):
    nc = p.nc
    p.begin_stage()
    chain = p.semaphore("dve_chain")
    biased = p.semaphore("gate_biased")
    soft = p.semaphore("gate_soft")
    logs_ready = p.semaphore("gate_logs_ready")
    exps_ready = p.semaphore("gate_exps_ready")
    R = GATE_ROWS
    with ExitStack() as local:
        sb = lambda name, shape: local.enter_context(nc.sbuf_tensor(name, shape, F32))
        soft_t = sb("gate_soft_t", [R, TOK])
        decay = sb("gate_decay", [R, TOK])
        peak = sb("gate_peak", [R, TOK])
        carry_on = sb("gate_carry_on", [R, TOK])
        small = sb("gate_small", [R, 3, TILES])
        chunked = lambda a: a.rearrange("r (c t) -> r c t", t=M_CHUNK)
        with nc.Block() as block:
            @block.scalar
            def _(act):
                act.wait_ge(biased, 1)
                nc.scalar.activation(soft_t[:, :], gate_f[:, :], ACT.Abs).then_inc(soft, 1)
                act.wait_ge(soft, 1)
                nc.scalar.activation(soft_t[:, :], soft_t[:, :], ACT.Exp, scale=-1.0).then_inc(soft, 1)
                act.wait_ge(soft, 2)
                nc.scalar.activation(soft_t[:, :], soft_t[:, :], ACT.Ln, bias=1.0).then_inc(soft, 1)
                act.wait_ge(logs_ready, 1)
                for name in ("query_scale", "floor", "key_scale"):
                    nc.scalar.activation(rows[name], rows[name], ACT.Exp,
                                                         scale=-1.0 if name == "floor" else 1.0).then_inc(exps_ready, 1)
                nc.scalar.activation(carry[:, :], carry[:, :], ACT.Exp).then_inc(exps_ready, 1)

            @block.vector
            def _(dve):
                made = [0]

                def then(instruction):
                    made[0] += 1
                    instruction.then_inc(chain, 1)
                    dve.wait_ge(chain, made[0])

                then(nc.vector.memset(carry_on[:, :], 1.0))
                then(nc.vector.memset(chunked(carry_on[0:32, :])[:, :, 0], 0.0))
                then(nc.vector.memset(chunked(carry_on[32:R, :])[:, :, M_CHUNK - 1], 0.0))
                then(nc.vector.tensor_scalar(gate_i[:, :], gate_i[:, :], p.param("gate_b_i", 0, R), None, ALU.add))
                nc.vector.tensor_scalar(gate_f[:, :], gate_f[:, :], p.param("gate_b_f", 0, R), None, ALU.add).then_inc(biased, 1)
                dve.wait_ge(biased, 1)
                dve.wait_ge(soft, 1)
                then(nc.vector.tensor_scalar(gate_f[:, :], gate_f[:, :], 0.0, None, ALU.min))
                dve.wait_ge(soft, 3)
                then(nc.vector.tensor_tensor(gate_f[:, :], gate_f[:, :], soft_t[:, :], ALU.subtract))
                fwd, bwd = slice(0, 32), slice(32, R)
                then(nc.vector.tensor_tensor_scan(decay[fwd, :], carry_on[fwd, :], gate_f[fwd, :], 0.0, ALU.mult, ALU.add))
                then(nc.vector.tensor_tensor_scan(decay[bwd, ::-1], carry_on[bwd, ::-1], gate_f[bwd, ::-1], 0.0, ALU.mult, ALU.add))
                then(nc.vector.tensor_tensor_scan(peak[fwd, :], gate_f[fwd, :], gate_i[fwd, :], 0.0, ALU.add, ALU.max))
                then(nc.vector.tensor_tensor_scan(peak[bwd, 0:CTX][:, ::-1], gate_f[bwd, 0:CTX][:, ::-1],
                                                  gate_i[bwd, 0:CTX][:, ::-1], 0.0, ALU.add, ALU.max))
                then(nc.vector.tensor_tensor_scan(peak[bwd, CTX:TOK][:, ::-1], gate_f[bwd, CTX:TOK][:, ::-1],
                                                  gate_i[bwd, CTX:TOK][:, ::-1], peak[bwd, 0:1], ALU.add, ALU.max))
                before, at_end, whole = small[:, 0, :], small[:, 1, :], small[:, 2, :]
                then(nc.vector.memset(small[:, :, :], 0.0))
                peaks, decays = chunked(peak[:, :]), chunked(decay[:, :])
                then(nc.vector.tensor_copy(before[fwd, 1:TILES], peaks[fwd, 0:TILES - 1, M_CHUNK - 1]))
                then(nc.vector.tensor_copy(before[bwd, 0:1], peaks[bwd, 1:2, 0]))
                then(nc.vector.tensor_copy(before[bwd, CTX_TILES:TILES - 1], peaks[bwd, CTX_TILES + 1:TILES, 0]))
                then(nc.vector.tensor_copy(before[bwd, TILES - 1:TILES], peaks[bwd, 0:1, 0]))
                for rws, at in ((fwd, M_CHUNK - 1), (bwd, 0)):
                    then(nc.vector.tensor_copy(at_end[rws, :], peaks[rws, :, at]))
                    then(nc.vector.tensor_copy(whole[rws, :], decays[rws, :, at]))
                wide = lambda a: a.unsqueeze(2).broadcast_to([R, TILES, M_CHUNK])
                then(nc.vector.tensor_tensor(rows["query_log"], decay[:, :], peak[:, :], ALU.subtract))
                then(nc.vector.tensor_tensor(rows["key_log"], gate_i[:, :], decay[:, :], ALU.subtract))
                then(nc.vector.tensor_copy(rows["floor"], peak[:, :]))
                then(nc.vector.tensor_tensor(chunked(rows["query_scale"]), chunked(rows["query_log"]), wide(before), ALU.add))
                then(nc.vector.tensor_tensor(whole, whole, at_end, ALU.subtract))
                then(nc.vector.tensor_tensor(chunked(rows["key_scale"]), chunked(rows["key_log"]), wide(whole), ALU.add))
                nc.vector.tensor_tensor(carry[:, :], whole, before, ALU.add).then_inc(logs_ready, 1)


def stage_gate_columns(p, rows, carry, sel, cols, carry_wide):
    nc = p.nc
    R = GATE_ROWS
    p.begin_stage()
    turned = p.semaphore("gate_turned")
    copied = p.semaphore("gate_columns_copied")
    kinds = ("key_log", "query_scale", "floor", "key_scale")
    with nc.Block() as block:
        @block.tensor
        def _(pe):
            for n, name in enumerate(kinds):
                for c in range(TILES):
                    last = nc.tensor.transpose(p.psum[:, n, c * R:(c + 1) * R], rows[name][:, c * P:(c + 1) * P],
                                               p.const("ident")[0:R, 0:R])
                last.then_inc(turned, 1)
            for r in range(2 * M_HEADS):
                last = nc.tensor.matmul(p.psum[:, 4, r * TILES:(r + 1) * TILES], sel[0:R, r * P:(r + 1) * P],
                                        carry[:, :], start=True, stop=True)
            last.then_inc(turned, 1)

        @block.vector
        def _(dve):
            for n in range(4):
                dve.wait_ge(turned, n + 1)
                nc.vector.tensor_copy(cols[:, n], p.psum[:, n, 0:TILES * R].rearrange("p (c r) -> p c r", r=R)).then_inc(copied, 1)
            dve.wait_ge(turned, 5)
            nc.vector.tensor_copy(carry_wide[:, :, :],
                                              p.psum[:, 4, 0:8 * TILES].rearrange("p (r c) -> p r c", c=TILES)).then_inc(copied, 1)


def stage_turn(p, kT, k_tok):
    nc = p.nc
    p.begin_stage()
    turned = p.semaphore("turn_turned")
    copied = p.semaphore("turn_copied")
    with nc.Block() as block:
        @block.tensor
        def _(pe):
            for i in range(TILES):
                if i >= 8:
                    pe.wait_ge(copied, i - 7)
                for h in range(WT):
                    last = nc.tensor.transpose(p.psum[:, i % 8, h * P:(h + 1) * P], kT[:, h, i * P:(i + 1) * P],
                                               p.const("ident"))
                last.then_inc(turned, 1)

        @block.scalar
        def _(act):
            for i in range(TILES):
                act.wait_ge(turned, i + 1)
                nc.scalar.copy(k_tok[:, i, :, :], p.psum[:, i % 8, :].rearrange("p (h n) -> p h n", h=WT)).then_inc(copied, 1)


def scan_order(direction, chunks, ctx_chunks):
    if direction == 0:
        return list(range(chunks))
    return list(range(ctx_chunks))[::-1] + list(range(ctx_chunks, chunks))[::-1]


def stage_mlstm_scan(p, qT, kT, k_tok, v_aug, rows, cols, carry_wide, sel, caps, y):
    nc = p.nc
    H, C = M_HEADS, M_CHUNK
    names = ("weights_logs_ready", "scores_ready", "capped", "weights_exp", "weighted", "inside_ready",
             "across_ready", "keys_scaled", "update_ready", "state_decayed", "state_ready", "y_ready")
    p.begin_stage()
    sig = {n: p.semaphore("m_" + n) for n in names}
    chain = p.semaphore("dve_chain")
    cleared = p.semaphore("m_cleared")
    steps = [(d, c) for pair in zip(scan_order(0, TILES, CTX_TILES), scan_order(1, TILES, CTX_TILES))
             for d, c in enumerate(pair)]
    N = len(steps)
    logs, scores, inside, across, update = 0, 1, (2, 4), (4, 6), (6, 8)
    two = lambda banks: p.psum[:, banks[0]:banks[1], 0:2 * (P + 1)].rearrange("p b (h n) -> p b h n", h=2)
    col = lambda n, c, d: cols[:, n, c, 32 * d:32 * d + H]
    with ExitStack() as local:
        sb = lambda name, shape: local.enter_context(nc.sbuf_tensor("m_" + name, shape, F32))
        state = sb("state", [P, 2, H, P + 1])
        decayed = sb("decayed", [P, 2, H, P + 1])
        capped = sb("capped", [P, 2, H, C])
        weight = sb("weight", [P, 2, H, C])
        keys = sb("keys", [P, 2, H, P])
        num = sb("num", [P, 2, H, P + 1])
        den = sb("den", [P, 2, 3, H])
        with nc.Block() as block:
            @block.tensor
            def _(pe):
                pe.wait_ge(cleared, 1)
                for i, (d, c) in enumerate(steps):
                    tokens = slice(c * C, (c + 1) * C)
                    if i:
                        pe.wait_ge(sig["capped"], H * i)
                    for h in range(H):
                        r = d * H + h
                        last = nc.tensor.matmul(p.psum[:, logs, h * C:(h + 1) * C],
                                                sel[0:GATE_ROWS, r * P:(r + 1) * P], rows["query_log"][:, tokens],
                                                start=True, stop=True)
                    last.then_inc(sig["weights_logs_ready"], 1)
                    if i:
                        pe.wait_ge(sig["weighted"], i)
                    for h in range(H):
                        last = nc.tensor.matmul(p.psum[:, scores, h * C:(h + 1) * C], kT[:, h, tokens],
                                                qT[:, h, tokens], start=True, stop=True)
                    last.then_inc(sig["scores_ready"], 1)
                    if i >= 2:
                        pe.wait_ge(sig["state_ready"], i - 1)
                    if i:
                        pe.wait_ge(sig["y_ready"], i)
                    for h in range(H):
                        last = nc.tensor.matmul(p.psum[:, across[0] + h // 2, (h % 2) * (P + 1):(h % 2 + 1) * (P + 1)],
                                                qT[:, h, tokens], state[:, d, h, :], start=True, stop=True)
                    last.then_inc(sig["across_ready"], 1)
                    pe.wait_ge(sig["weighted"], i + 1)
                    for h in range(H):
                        last = nc.tensor.matmul(p.psum[:, inside[0] + h // 2, (h % 2) * (P + 1):(h % 2 + 1) * (P + 1)],
                                                weight[:, i % 2, h, :], v_aug[:, c, h, :], start=True, stop=True)
                    last.then_inc(sig["inside_ready"], 1)
                    pe.wait_ge(sig["keys_scaled"], i + 1)
                    if i:
                        pe.wait_ge(sig["state_ready"], i)
                    for h in range(H):
                        last = nc.tensor.matmul(p.psum[:, update[0] + h // 2, (h % 2) * (P + 1):(h % 2 + 1) * (P + 1)],
                                                keys[:, i % 2, h, :], v_aug[:, c, h, :], start=True, stop=True)
                    last.then_inc(sig["update_ready"], 1)

            @block.scalar
            def _(act):
                for i, (d, c) in enumerate(steps):
                    act.wait_ge(sig["capped"], H * (i + 1))
                    if i >= 2:
                        act.wait_ge(sig["inside_ready"], i - 1)
                    nc.scalar.activation(weight[:, i % 2], capped[:, i % 2], ACT.Exp).then_inc(sig["weights_exp"], 1)

            @block.gpsimd
            def _(pool):
                for i, (d, c) in enumerate(steps):
                    if i >= 2:
                        pool.wait_ge(sig["update_ready"], i - 1)
                    nc.gpsimd.tensor_tensor(
                        keys[:, i % 2], k_tok[:, c], col(3, c, d).unsqueeze(2).broadcast_to([P, H, P]), ALU.mult).then_inc(sig["keys_scaled"], 1)
                    if i == 0:
                        pool.wait_ge(cleared, 1)
                    if i >= 2:
                        pool.wait_ge(sig["state_ready"], i - 1)
                    nc.gpsimd.tensor_tensor(
                        decayed[:, d], state[:, d],
                        carry_wide[:, d * H:(d + 1) * H, c].unsqueeze(2).broadcast_to([P, H, P + 1]), ALU.mult).then_inc(sig["state_decayed"], 1)

            @block.vector
            def _(dve):
                made = [0]

                def then(instruction):
                    made[0] += 1
                    instruction.then_inc(chain, 1)
                    dve.wait_ge(chain, made[0])

                nc.vector.memset(state[:, :, :, :], 0.0).then_inc(cleared, 1)
                for i, (d, c) in enumerate(steps):
                    b = i % 2
                    dve.wait_ge(sig["weights_logs_ready"], i + 1)
                    if i >= 2:
                        dve.wait_ge(sig["weights_exp"], i - 1)
                    for h in range(H):
                        nc.vector.scalar_tensor_tensor(
                            capped[:, b, h, :], p.psum[:, logs, h * C:(h + 1) * C], cols[:, 0, c, 32 * d + h:32 * d + h + 1],
                            caps[:, d * P:(d + 1) * P], ALU.add, ALU.min).then_inc(sig["capped"], 1)
                    dve.wait_ge(sig["scores_ready"], i + 1)
                    dve.wait_ge(sig["weights_exp"], i + 1)
                    nc.vector.tensor_tensor(
                        weight[:, b], weight[:, b], p.psum[:, scores, :].rearrange("p (h n) -> p h n", h=H), ALU.mult).then_inc(sig["weighted"], 1)
                    four = num[:, b].rearrange("p (b h) n -> p b h n", b=2)
                    dve.wait_ge(sig["across_ready"], i + 1)
                    then(nc.vector.tensor_tensor(
                        four, two(across), col(1, c, d).rearrange("p (b h) -> p b h", b=2).unsqueeze(3).broadcast_to([P, 2, 2, P + 1]), ALU.mult))
                    dve.wait_ge(sig["inside_ready"], i + 1)
                    then(nc.vector.tensor_tensor(four, four, two(inside), ALU.add))
                    then(nc.vector.tensor_scalar(den[:, b, 0, :], num[:, b, :, P], -1.0, None, ALU.mult))
                    then(nc.vector.tensor_tensor(den[:, b, 0, :], den[:, b, 0, :], num[:, b, :, P], ALU.max))
                    then(nc.vector.tensor_tensor(den[:, b, 1, :], den[:, b, 0, :], col(2, c, d), ALU.max))
                    then(nc.vector.reciprocal(den[:, b, 2, :], den[:, b, 1, :]))
                    inv = den[:, b, 2, :].unsqueeze(2).broadcast_to([P, H, P])
                    y_c = y[:, c, :].rearrange("p (h n) -> p h n", h=H)
                    first = all(cc != c for _, cc in steps[:i])
                    if first:
                        nc.vector.tensor_tensor(y_c, num[:, b, :, 0:P], inv, ALU.mult).then_inc(sig["y_ready"], 1)
                    else:
                        then(nc.vector.tensor_tensor(num[:, b, :, 0:P], num[:, b, :, 0:P], inv, ALU.mult))
                        nc.vector.tensor_tensor(y_c, y_c, num[:, b, :, 0:P], ALU.add).then_inc(sig["y_ready"], 1)
                    dve.wait_ge(sig["update_ready"], i + 1)
                    dve.wait_ge(sig["state_decayed"], i + 1)
                    nc.vector.tensor_tensor(
                        state[:, d].rearrange("p (b h) n -> p b h n", b=2),
                        decayed[:, d].rearrange("p (b h) n -> p b h n", b=2), two(update), ALU.add).then_inc(sig["state_ready"], 1)


def stage_heads_rmsnorm(p, y, gate, tiles, heads_eps):
    nc = p.nc
    H = WT
    p.begin_stage()
    squares = p.semaphore("hn_squares")
    sums = p.semaphore("hn_sums")
    roots = p.semaphore("hn_roots")
    done = p.semaphore("hn_done")
    with ExitStack() as local:
        sq = local.enter_context(nc.sbuf_tensor(f"hn_squares_t{len(tiles)}", [P, 2, W], F32))
        st = local.enter_context(nc.sbuf_tensor(f"hn_stat{len(tiles)}", [P, TILES, 3, H], F32))
        with nc.Block() as block:
            @block.scalar
            def _(act):
                for i, t in enumerate(tiles):
                    if i >= 2:
                        act.wait_ge(sums, 2 * i - 2)
                    nc.scalar.activation(sq[:, i % 2, :], y[:, t, :], ACT.Square).then_inc(squares, 1)
                for i, t in enumerate(tiles):
                    act.wait_ge(sums, 2 * i + 2)
                    nc.scalar.activation(st[:, i, 1, :], st[:, i, 1, :], ACT.Sqrt).then_inc(roots, 1)

            @block.gpsimd
            def _(pool):
                for i, t in enumerate(tiles):
                    pool.wait_ge(squares, i + 1)
                    nc.gpsimd.tensor_tensor(y[:, t, :], y[:, t, :], gate[:, t, :], ALU.mult).then_inc(done, 1)

            @block.vector
            def _(dve):
                for i, t in enumerate(tiles):
                    dve.wait_ge(squares, i + 1)
                    nc.vector.tensor_reduce(st[:, i, 0, :], sq[:, i % 2, :].rearrange("p (h n) -> p h n", h=H), AX.X, ALU.add).then_inc(sums, 1)
                    dve.wait_ge(sums, 2 * i + 1)
                    nc.vector.tensor_scalar(st[:, i, 1, :], st[:, i, 0, :], 1.0 / P, heads_eps, ALU.mult, ALU.add).then_inc(sums, 1)
                for i, t in enumerate(tiles):
                    dve.wait_ge(roots, i + 1)
                    nc.vector.reciprocal(st[:, i, 2, :], st[:, i, 1, :]).then_inc(sums, 1)
                    dve.wait_ge(sums, 2 * len(tiles) + 2 * i + 1)
                    dve.wait_ge(done, i + 1)
                    yt = y[:, t, :].rearrange("p (h n) -> p h n", h=H)
                    nc.vector.tensor_tensor(yt, yt, st[:, i, 2, :].unsqueeze(2).broadcast_to([P, H, P]), ALU.mult).then_inc(sums, 1)


def stage_turn_back(p, y, tiles, scale, shift, factor, mix, first, offset=0):
    nc = p.nc
    p.begin_stage()
    turned = p.semaphore("back_turned")
    copied = p.semaphore("back_copied")
    multiplied = p.semaphore("back_multiplied")
    stored = p.semaphore("back_stored")
    with ExitStack() as local:
        mixT = local.enter_context(nc.sbuf_tensor(f"back_mixT{first}_{len(tiles)}", [P, WT, TOK], F32))
        with nc.Block() as block:
            @block.tensor
            def _(pe):
                for i, t in enumerate(tiles):
                    if i >= 8:
                        pe.wait_ge(copied, WT * (i - 7))
                    for h in range(WT):
                        last = nc.tensor.transpose(p.psum[:, i % 8, h * P:(h + 1) * P], y[:, t, h * P:(h + 1) * P],
                                                   p.const("ident"))
                    last.then_inc(turned, 1)

            @block.scalar
            def _(act):
                for i, t in enumerate(tiles):
                    act.wait_ge(turned, i + 1)
                    for h in range(WT):
                        nc.scalar.activation(mixT[:, h, offset + t * P:offset + (t + 1) * P],
                                                         p.psum[:, i % 8, h * P:(h + 1) * P], ACT.Identity,
                                                         scale=scale(h), bias=shift(h) if shift else 0.0).then_inc(copied, 1)

            @block.gpsimd
            def _(pool):
                if factor is not None:
                    for i, t in enumerate(tiles):
                        pool.wait_ge(copied, WT * (i + 1))
                        out = mixT[:, :, t * P:(t + 1) * P]
                        nc.gpsimd.tensor_tensor(out, out, factor[:, :, t * P:(t + 1) * P], ALU.mult).then_inc(multiplied, 1)

            @block.sync
            def _(sp):
                sp.wait_ge(copied, WT * len(tiles))
                if factor is not None:
                    sp.wait_ge(multiplied, len(tiles))
                at = offset + tiles[0] * P
                sp.dma_start(mix[first:first + WT, :, at:TOK].rearrange("k p t -> p k t"), mixT[:, :, at:TOK]).then_inc(stored, 16)
                sp.wait_ge(stored, 16)


def mlstm_branch(p, free, hT, mix):
    nc = p.nc
    w_in = p.dram["l0_w_in"]
    with ExitStack() as outer:
        so = lambda name, shape: outer.enter_context(nc.sbuf_tensor(name, shape, F32))
        y = so("m_y", [P, TILES, W])
        with ExitStack() as inner:
            si = lambda name, shape: inner.enter_context(nc.sbuf_tensor(name, shape, F32))
            qT, kT = (free[:, i * WT * TOK:(i + 1) * WT * TOK].rearrange("p (j t) -> p j t", j=WT) for i in range(2))
            v_aug = si("m_v", [P, TILES, M_HEADS, P + 1])
            query_log = si("m_query_log", [GATE_ROWS, TOK])
            masks = si("m_masks", [P, 2 * P + 8 * P])
            cols = si("m_cols", [P, 4, TILES, GATE_ROWS])
            carry_wide = si("m_carry_wide", [P, 2 * M_HEADS, TILES])
            caps, sel = masks[:, 0:2 * P], masks[:, 2 * P:]
            for i, out in enumerate((qT, kT)):
                with ExitStack() as raws:
                    raw = raws.enter_context(nc.sbuf_tensor(f"m_raw{i}", [P, WT, TOK], F32))
                    stage_project(p, f"m{i}", hT, w_in, [(i * W, W, ACT.Copy, raw, False, GROUPS)])
                    stage_conv_qk(p, raw, out, i)
            with ExitStack() as gates:
                sg = lambda name, shape: gates.enter_context(nc.sbuf_tensor(name, shape, F32))
                gate_rows = sg("m_gates", [GATE_ROWS, 2, TOK])
                stage_project(p, "mv", hT, w_in, [
                    (2 * W, W, ACT.Copy, v_aug[:, :, :, 0:P], True, (0, TILES)),
                    ("gate_i", GATE_ROWS, ACT.Copy, gate_rows[:, 0], False, GROUPS),
                    ("gate_f", GATE_ROWS, ACT.Copy, gate_rows[:, 1], False, GROUPS)])
                stage_copies(p, [(masks[:, :], p.dram["const_mlstm"])])
                with nc.Block() as block:
                    @block.gpsimd
                    def _(pool):
                        nc.gpsimd.memset(v_aug[:, :, :, P:P + 1], 1.0)
                carry = sg("m_carry", [GATE_ROWS, TILES])
                row_buf = sg("m_rows", [GATE_ROWS, 4, TOK])
                rows = {n: row_buf[:, i, :] for i, n in enumerate(("key_log", "query_scale", "floor", "key_scale"))}
                rows["query_log"] = query_log[:, :]
                stage_gate_rows(p, gate_rows[:, 0], gate_rows[:, 1], rows, carry)
                stage_gate_columns(p, rows, carry, sel, cols, carry_wide)
            k_tok = si("m_k_tok", [P, TILES, M_HEADS, P])
            stage_turn(p, kT, k_tok)
            stage_mlstm_scan(p, qT, kT, k_tok, v_aug, rows, cols, carry_wide, sel, caps, y)
        gate_o, gate_z = so("m_o", [P, TILES, W]), so("m_z", [P, TILES, W])
        stage_project(p, "mo", hT, w_in, [
            (3 * W, W, ACT.Sigmoid, gate_o, True, (0, TILES)), (4 * W, W, ACT.Silu, gate_z, True, (0, TILES))])
        with nc.Block() as block:
            @block.gpsimd
            def _(pool):
                nc.gpsimd.tensor_tensor(gate_o[:, :, :], gate_o[:, :, :], gate_z[:, :, :], ALU.mult)
        stage_heads_rmsnorm(p, y, gate_o, range(TILES), EPS)
        stage_turn_back(p, y, range(TILES), lambda h: p.param("m_norm_g", h), None, None, mix, 0)


R_CHUNKS = TOK // R_CHUNK
R_PAIRS = R_HEADS // 2
R_LEVELS = 6
M_IN = 5 * W + 4 * M_HEADS


R_MASKS = 2 * 2 * R_CHUNK + R_CHUNK + R_LEVELS * 2 * P + 2 * P


def const_rwkv():
    C = R_CHUNK
    s, t = np.arange(C)[:, None], np.arange(C)[None]
    out = []
    for d in range(2):
        before = (s < t) if d == 0 else (s > t)
        upto = (s <= t) if d == 0 else (s >= t)
        cols = [before, upto, upto, before, before.T]
        out.append(np.tile(np.concatenate(cols, axis=1), (2, 1)))
        cols = []
        for n in range(R_LEVELS):
            added = before & ((s >> (n + 1)) == (t >> (n + 1))) & ((s >> n) != (t >> n))
            cols += [added, added.T]
        cols += [s == t, np.ones((C, C))]
        out += [np.kron(np.eye(2), m) for m in cols]
    return np.concatenate(out, axis=1).astype(np.float32)


def stage_shift_taps(p, taps):
    nc = p.nc
    p.begin_stage()
    made = p.semaphore("taps_made")
    at = PARAMS["r_mu"][0]
    with nc.Block() as block:
        @block.vector
        def _(dve):
            mu = p.params[:, at:at + 12]
            nc.vector.tensor_scalar(taps[:, 0, :], mu, 0.5, None, ALU.mult).then_inc(made, 1)
            nc.vector.tensor_scalar(taps[:, 1, :], mu, -1.0, 1.0, ALU.mult, ALU.add).then_inc(made, 1)


def stage_token_shift(p, raw, outs, taps, which):
    nc = p.nc
    p.begin_stage()
    chain = p.semaphore("dve_chain")
    shifted = p.semaphore("shift_done")
    with nc.Block() as block:
        @block.vector
        def _(dve):
            made = [0]

            def then(instruction):
                made[0] += 1
                instruction.then_inc(chain, 1)
                dve.wait_ge(chain, made[0])

            for j in range(WT):
                n = which * WT + j
                for rows, out in outs:
                    side, here = taps[rows, 0, n:n + 1], taps[rows, 1, n:n + 1]
                    conv3_steps(nc, then, out[:, j, :], raw[rows, j, :], [side, here, side], shifted)


def lora_products(nc, p, up, down, d, j, bank):
    for n, (at, width) in enumerate(GROUPS):
        last = nc.tensor.matmul(p.psum[:, bank + n, 0:width], up[64 * d:64 * d + 64, j * P:(j + 1) * P],
                                down[64 * d:64 * d + 64, at:at + width], start=True, stop=True)
    return last


def stage_rwkv_prepare(p, d, r_dram, kr_dram, down, up, mix_k, queries, keys, chunk_decay):
    nc = p.nc
    p.begin_stage()
    chain = p.semaphore("dve_chain")
    lora_ready = p.semaphore("rp_lora_ready")
    lora_read = p.semaphore("rp_lora_read")
    logs_ready = p.semaphore("rp_logs_ready")
    exps_ready = p.semaphore("rp_exps_ready")
    squares_ready = p.semaphore("rp_squares_ready")
    norms_ready = p.semaphore("rp_norms_ready")
    norms_read = p.semaphore("rp_norms_read")
    raw_keys_ready = p.semaphore("rp_raw_keys_ready")
    pair_done = p.semaphore("rp_pair_done")
    r_loaded, kr_loaded = p.semaphores("rp_r_loaded", 2), p.semaphores("rp_kr_loaded", 2)
    half_e = -float(np.exp(-0.5))
    with ExitStack() as local:
        sb = lambda name, shape: local.enter_context(nc.sbuf_tensor(f"rp_{name}{d}", shape, F32))
        log_w, rate, decay = sb("log_w", [P, TOK]), sb("rate", [P, TOK]), sb("decay", [P, TOK])
        kk, norm, grown = sb("kk", [P, TOK]), sb("norm", [P, TOK]), sb("grown", [P, TOK])
        carry_on = sb("carry_on", [P, TOK])
        r_in, kr_in = sb("r_in", [P, 2, TOK]), sb("kr_in", [P, 2, TOK])
        chunked = lambda a: a.rearrange("p (c t) -> p c t", t=R_CHUNK)
        order = slice(None) if d == 0 else slice(None, None, -1)
        first, last_of_chunk = (0, R_CHUNK - 1) if d == 0 else (R_CHUNK - 1, 0)
        with nc.Block() as block:
            @block.sync
            def _(sp):
                for j in range(R_PAIRS):
                    if j >= 2:
                        sp.wait_ge(pair_done, j - 1)
                    sp.dma_start(r_in[:, j % 2, :], r_dram[j]).then_inc(r_loaded[j % 2], 16)
                    sp.dma_start(kr_in[:, j % 2, :], kr_dram[j]).then_inc(kr_loaded[j % 2], 16)

            @block.tensor
            def _(pe):
                for j in range(R_PAIRS):
                    if j:
                        pe.wait_ge(lora_read, 6 * j)
                    lora_products(nc, p, up[:, 0], down[:, 0], d, j, 0)
                    lora_products(nc, p, up[:, 1], down[:, 1], d, j, 3).then_inc(lora_ready, 1)
                    pe.wait_ge(squares_ready, j + 1)
                    for n, (at, width) in enumerate(GROUPS):
                        pe.wait_ge(lora_read, 6 * j + 3)
                        last = nc.tensor.matmul(p.psum[:, n, 0:width], p.const("head_ones"),
                                                norm[:, at:at + width], start=True, stop=True)
                    last.then_inc(norms_ready, 1)
                    pe.wait_ge(norms_read, 3 * (j + 1))

            @block.scalar
            def _(act):
                for j in range(R_PAIRS):
                    act.wait_ge(lora_ready, j + 1)
                    if j:
                        act.wait_ge(pair_done, j)
                    for n, (at, width) in enumerate(GROUPS):
                        nc.scalar.activation(log_w[:, at:at + width], p.psum[:, n, 0:width], ACT.Sigmoid,
                                                            bias=p.param("r_w0", WT * d + j)).then_inc(lora_read, 1)
                    for n, (at, width) in enumerate(GROUPS):
                        nc.scalar.activation(rate[:, at:at + width], p.psum[:, 3 + n, 0:width], ACT.Sigmoid,
                                                            bias=p.param("r_a0", WT * d + j)).then_inc(lora_read, 1)
                    act.wait_ge(raw_keys_ready, j + 1)
                    nc.scalar.activation(norm[:, :], kk[:, :], ACT.Square).then_inc(squares_ready, 1)
                    act.wait_ge(norms_ready, j + 1)
                    for n, (at, width) in enumerate(GROUPS):
                        nc.scalar.activation(norm[:, at:at + width], p.psum[:, n, 0:width], ACT.Sqrt).then_inc(norms_read, 1)
                    act.wait_ge(logs_ready, j + 1)
                    nc.scalar.activation(log_w[:, :], log_w[:, :], ACT.Exp).then_inc(exps_ready, 1)
                    nc.scalar.activation(grown[:, :], decay[:, :], ACT.Exp).then_inc(exps_ready, 1)
                    act.wait_ge(exps_ready, 3 * j + 2)
                    nc.scalar.activation(decay[:, :], decay[:, :], ACT.Exp, scale=-1.0).then_inc(exps_ready, 1)

            @block.vector
            def _(dve):
                made = [0]

                def then(instruction):
                    made[0] += 1
                    instruction.then_inc(chain, 1)
                    dve.wait_ge(chain, made[0])

                then(nc.vector.memset(carry_on[:, :], 1.0))
                then(nc.vector.memset(chunked(carry_on[:, :])[:, :, first], 0.0))
                for j in range(R_PAIRS):
                    dve.wait_ge(r_loaded[j % 2], 16 * (j // 2 + 1))
                    dve.wait_ge(kr_loaded[j % 2], 16 * (j // 2 + 1))
                    rT, krT = r_in[:, j % 2, :], kr_in[:, j % 2, :]
                    nc.vector.tensor_scalar(kk[:, :], krT, p.param("r_k_k", j), None, ALU.mult).then_inc(raw_keys_ready, 1)
                    dve.wait_ge(lora_read, 6 * (j + 1))
                    then(nc.vector.tensor_scalar(log_w[:, :], log_w[:, :], half_e, None, ALU.mult))
                    then(nc.vector.tensor_tensor_scan(decay[:, order], carry_on[:, order], log_w[:, order], 0.0, ALU.mult, ALU.add))
                    nc.vector.tensor_tensor(log_w[:, :], decay[:, :], log_w[:, :], ALU.subtract).then_inc(logs_ready, 1)
                    dve.wait_ge(norms_read, 3 * (j + 1))
                    then(nc.vector.tensor_scalar(norm[:, :], norm[:, :], 1e-12, None, ALU.max))
                    then(nc.vector.reciprocal(norm[:, :], norm[:, :]))
                    then(nc.vector.tensor_tensor(kk[:, :], kk[:, :], norm[:, :], ALU.mult))
                    dve.wait_ge(exps_ready, 3 * (j + 1))
                    for q in range(2):
                        rows = slice(R_DIM * q, R_DIM * q + R_DIM)
                        nc.vector.tensor_tensor(queries[rows, j, :, q, :], chunked(kk[rows, :]), chunked(log_w[rows, :]), ALU.mult)
                        nc.vector.tensor_tensor(queries[rows, j, :, 1 - q, :], chunked(grown[rows, :]), chunked(rT[rows, :]), ALU.mult)
                    then(nc.vector.tensor_copy(chunk_decay[:, j, :], chunked(grown[:, :])[:, :, last_of_chunk]))
                    then(nc.vector.tensor_tensor(kk[:, :], kk[:, :], rate[:, :], ALU.mult))
                    for q in range(2):
                        rows = slice(R_DIM * q, R_DIM * q + R_DIM)
                        last = nc.vector.scalar_tensor_tensor(keys[rows, j, :, q, :], chunked(kk[rows, :]), -1.0, chunked(decay[rows, :]),
                                                              ALU.mult, ALU.mult)
                    then(last)
                    then(nc.vector.tensor_scalar(rate[:, :], rate[:, :], p.param("r_k_a", j), mix_k[:, j:j + 1], ALU.mult, ALU.add))
                    then(nc.vector.tensor_tensor(rate[:, :], rate[:, :], krT, ALU.mult))
                    for q in range(2):
                        rows = slice(R_DIM * q, R_DIM * q + R_DIM)
                        last = nc.vector.tensor_tensor(keys[rows, j, :, 1 - q, :], chunked(rate[rows, :]), chunked(decay[rows, :]), ALU.mult)
                    last.then_inc(pair_done, 1)
                    dve.wait_ge(pair_done, j + 1)


def stage_rwkv_scan(p, d, queries, keys, vT, chunk_decay, y):
    nc = p.nc
    C, J = R_CHUNK, R_PAIRS
    HALF = J * C
    LEVELS = R_LEVELS - 1
    steps = scan_order(d, R_CHUNKS, CTX // R_CHUNK)
    N = len(steps)
    p.begin_stage()
    sig = {n: p.semaphore("r_" + n) for n in (
        "products_ready", "inverse_ready", "half_ready", "half_copied", "whole_ready", "turned_ready",
        "turned_copied", "v_copied", "pulled_ready", "pulled_copied", "u_start_ready", "from_state_copied",
        "u_sums_ready", "u_ready", "outputs_ready", "y_copied", "state_ready")}
    chain = p.semaphore("dve_chain")
    masks_loaded = p.semaphore("r_masks_loaded")
    part = lambda q: slice(C * q, C * q + C)
    both = [(j, q) for j in range(J) for q in range(2)]
    with ExitStack() as local:
        sb = lambda name, shape: local.enter_context(nc.sbuf_tensor(f"r_{name}{d}", shape, F32))
        prod = sb("prod", [P, 2, 2, J, 2 * C])
        strict_t = sb("strict_t", [P, 2, J, P])
        inv = sb("inv", [P, 2, 2, J, P])
        half = sb("half", [P, 2, J, P])
        pulled = sb("pulled", [P, 2, J, C])
        q_tok, k_tok = sb("q_tok", [P, 2, J, P]), sb("k_tok", [P, 2, J, P])
        from_state = sb("from_state", [P, 2, J, P])
        uv = sb("uv", [P, 2, 2, J, C])
        state = sb("state", [P, J, C])
        own = sb("masks", [P, R_MASKS])
        product_mask = lambda q: own[:, 2 * C * q:2 * C * (q + 1)].unsqueeze(1).broadcast_to([P, J, 2 * C])
        column = lambda n: own[:, n * C:(n + 1) * C].unsqueeze(1)
        strict = column(4).broadcast_to([P, J, C])
        block_column = lambda n: own[:, 5 * C + n * P:5 * C + (n + 1) * P].unsqueeze(1)
        added = lambda n, z: block_column(2 * n + z).bitcast(U32).broadcast_to([P, J, P])
        identity = block_column(2 * R_LEVELS).broadcast_to([P, 2 * J, P])
        blocks = block_column(2 * R_LEVELS + 1).broadcast_to([P, J, P])
        bank = lambda lane, b: p.psum[:, 4 * lane + b, :]
        narrow = lambda a: a.rearrange("p (j n) -> p j n", n=C)
        paired = lambda a: a.rearrange("p (j n) -> p j n", n=P)
        with nc.Block() as block:
            @block.sync
            def _(sp):
                sp.dma_start(own[:, :], p.dram["const_rwkv"][:, d * R_MASKS:(d + 1) * R_MASKS]).then_inc(masks_loaded, 16)

            @block.tensor
            def _(pe):
                for i in range(0, N, 2):
                    for lane in range(2):
                        s, c = i + lane, steps[i + lane]
                        if s >= 2:
                            pe.wait_ge(sig["state_ready"], s)
                            pe.wait_ge(sig["y_copied"], s - 1)
                        for j, q in both:
                            nc.tensor.matmul(bank(lane, q)[:, j * P:(j + 1) * P], keys[part(q), j, c, :, :],
                                             queries[part(q), j, c, :, :], start=True, stop=True)
                        for j, q in both:
                            last = nc.tensor.matmul(bank(lane, 2)[part(q), j * C:(j + 1) * C], queries[part(q), j, c, q, :],
                                                    keys[part(q), j, c, q, :], start=True, stop=True)
                        last.then_inc(sig["products_ready"], 1)
                    for n in range(LEVELS):
                        zs = (0, 1) if n < LEVELS - 1 else (0,)
                        for lane in range(2):
                            pe.wait_ge(sig["inverse_ready"], i * R_LEVELS + 2 * n + lane + 1)
                            for j in range(J):
                                last = nc.tensor.matmul(bank(lane, 0)[:, j * P:(j + 1) * P], strict_t[:, lane, j, :],
                                                        inv[:, lane, 0, j, :], start=True, stop=True)
                            last.then_inc(sig["half_ready"], 1)
                        for lane in range(2):
                            pe.wait_ge(sig["half_copied"], i * LEVELS + 2 * n + lane + 1)
                            for z in zs:
                                for j in range(J):
                                    h, other = half[:, lane, j, :], inv[:, lane, 1, j, :]
                                    last = nc.tensor.matmul(bank(lane, 1 + z)[:, j * P:(j + 1) * P],
                                                            *((other, h) if z == 0 else (h, other)), start=True, stop=True)
                            last.then_inc(sig["whole_ready"], 1)
                    for lane in range(2):
                        c = steps[i + lane]
                        for j in range(J):
                            nc.tensor.transpose(bank(lane, 2)[:, j * P:(j + 1) * P],
                                                queries[:, j, c, :, :].rearrange("p k t -> p (k t)"), p.const("ident"))
                            nc.tensor.transpose(bank(lane, 3)[:, j * P:(j + 1) * P],
                                                keys[:, j, c, :, :].rearrange("p k t -> p (k t)"), p.const("ident"))
                        pe.wait_ge(sig["inverse_ready"], i * R_LEVELS + 2 * LEVELS + lane + 1)
                        for j in range(J):
                            last = nc.tensor.transpose(bank(lane, 1)[:, j * P:(j + 1) * P],
                                                       vT[:, j, c * C:c * C + 2 * C], p.const("ident"))
                        last.then_inc(sig["turned_ready"], 1)
                    for lane in range(2):
                        pe.wait_ge(sig["v_copied"], i + lane + 1)
                        for j, q in both:
                            last = nc.tensor.matmul(bank(lane, 0)[part(q), j * C:(j + 1) * C], prod[part(1 - q), lane, q, j, part(q)],
                                                    uv[part(1 - q), lane, q, j, :], start=True, stop=True)
                        last.then_inc(sig["pulled_ready"], 1)
                    for lane in range(2):
                        pe.wait_ge(sig["turned_copied"], i + lane + 1)
                        for j in range(J):
                            last = nc.tensor.matmul(bank(lane, 2)[:, j * P:(j + 1) * P], q_tok[:, lane, j, :],
                                                    inv[:, lane, 0, j, :], start=True, stop=True)
                        last.then_inc(sig["u_start_ready"], 1)
                    for lane in range(2):
                        s, c = i + lane, steps[i + lane]
                        pe.wait_ge(sig["pulled_copied"], s + 1)
                        pe.wait_ge(sig["from_state_copied"], s + 1)
                        pe.wait_ge(sig["state_ready"], s + 1)
                        for j in range(J):
                            out = bank(lane, 0)[:, HALF + j * C:HALF + (j + 1) * C]
                            nc.tensor.matmul(out, inv[:, lane, 0, j, :], pulled[:, lane, j, :], start=True, stop=False)
                            last = nc.tensor.matmul(out, from_state[:, lane, j, :], state[:, j, :], start=False, stop=True)
                        last.then_inc(sig["u_sums_ready"], 1)
                        pe.wait_ge(sig["u_ready"], s + 1)
                        for j, q in both:
                            nc.tensor.matmul(bank(lane, 2)[part(q), HALF + j * C:HALF + (j + 1) * C], k_tok[:, lane, j, part(q)],
                                             uv[:, lane, q, j, :], start=True, stop=True)
                        for j, q in both:
                            out = bank(lane, 3 if q == 0 else 1)[part(c % 2), j * C:(j + 1) * C]
                            nc.tensor.matmul(out, queries[part(q), j, c, 1 - q, :], state[part(q), j, :], start=True, stop=False)
                            last = nc.tensor.matmul(out, prod[:, lane, q, j, part(1 - q)], uv[:, lane, q, j, :], start=False, stop=True)
                        last.then_inc(sig["outputs_ready"], 1)

            @block.scalar
            def _(act):
                for i in range(0, N, 2):
                    for n in range(LEVELS):
                        for lane in range(2):
                            act.wait_ge(sig["half_ready"], i * LEVELS + 2 * n + lane + 1)
                            if n:
                                act.wait_ge(sig["whole_ready"], i * LEVELS + 2 * (n - 1) + lane + 1)
                            nc.scalar.copy(half[:, lane], paired(bank(lane, 0))).then_inc(sig["half_copied"], 1)
                    for lane in range(2):
                        act.wait_ge(sig["turned_ready"], i + lane + 1)
                        nc.scalar.copy(q_tok[:, lane], paired(bank(lane, 2)))
                        nc.scalar.copy(k_tok[:, lane], paired(bank(lane, 3))).then_inc(sig["turned_copied"], 1)
                    for lane in range(2):
                        act.wait_ge(sig["pulled_ready"], i + lane + 1)
                        nc.scalar.copy(pulled[:, lane], narrow(bank(lane, 0)[:, 0:HALF])).then_inc(sig["pulled_copied"], 1)
                    for lane in range(2):
                        s, c = i + lane, steps[i + lane]
                        if d == 0:
                            act.wait_ge(sig["outputs_ready"], s + 1)
                            for q in range(2):
                                out = y[part(c % 2), c // 2, :].rearrange("p (j q n) -> p q j n", q=2, n=C)[:, q]
                                last = nc.scalar.copy(out, narrow(bank(lane, 3 if q == 0 else 1)[part(c % 2), 0:HALF]))
                            last.then_inc(sig["y_copied"], 1)

            @block.vector
            def _(dve):
                made = [0]

                def then(instruction):
                    made[0] += 1
                    instruction.then_inc(chain, 1)
                    dve.wait_ge(chain, made[0])

                nc.vector.memset(state[:, :, :], 0.0).then_inc(sig["state_ready"], 1)
                then(nc.vector.memset(strict_t[:, :, :, :], 0.0))
                dve.wait_ge(masks_loaded, 16)
                for i in range(0, N, 2):
                    for lane in range(2):
                        s = i + lane
                        dve.wait_ge(sig["products_ready"], s + 1)
                        if s >= 2:
                            dve.wait_ge(sig["outputs_ready"], s - 1)
                        for q in range(2):
                            nc.vector.tensor_tensor(prod[:, lane, q], paired(bank(lane, q)), product_mask(q), ALU.mult)
                            nc.vector.tensor_tensor(strict_t[part(q), lane, :, part(q)], narrow(bank(lane, 2)[part(q), 0:HALF]),
                                                    strict[part(q)], ALU.mult)
                        then(nc.vector.tensor_copy(inv[:, lane].rearrange("p z j n -> p (z j) n"), identity))
                        for q in range(2):
                            nc.vector.copy_predicated(inv[part(q), lane, 0, :, part(q)], added(0, 0)[part(q), :, part(q)],
                                                      prod[part(q), lane, q, :, part(q)])
                        nc.vector.copy_predicated(inv[:, lane, 1], added(0, 1), strict_t[:, lane]).then_inc(sig["inverse_ready"], 1)
                    for n in range(LEVELS):
                        for lane in range(2):
                            dve.wait_ge(sig["whole_ready"], i * LEVELS + 2 * n + lane + 1)
                            for z in range(2 if n < LEVELS - 1 else 1):
                                last = nc.vector.copy_predicated(inv[:, lane, z], added(n + 1, z),
                                                                 paired(bank(lane, 1 + z)))
                            last.then_inc(sig["inverse_ready"], 1)
                    for lane in range(2):
                        dve.wait_ge(sig["turned_ready"], i + lane + 1)
                        for q in range(2):
                            last = nc.vector.tensor_copy(uv[part(1 - q), lane, q], paired(bank(lane, 1))[part(1 - q), :, part(q)])
                        last.then_inc(sig["v_copied"], 1)
                    for lane in range(2):
                        dve.wait_ge(sig["u_start_ready"], i + lane + 1)
                        nc.vector.tensor_tensor(from_state[:, lane], paired(bank(lane, 2)), blocks, ALU.mult).then_inc(sig["from_state_copied"], 1)
                    for lane in range(2):
                        s, c = i + lane, steps[i + lane]
                        dve.wait_ge(sig["u_sums_ready"], s + 1)
                        for q in range(2):
                            last = nc.vector.tensor_copy(uv[part(q), lane, q], narrow(bank(lane, 0)[part(q), HALF:]))
                        last.then_inc(sig["u_ready"], 1)
                        dve.wait_ge(sig["outputs_ready"], s + 1)
                        then(nc.vector.tensor_tensor(state[:, :, :], state[:, :, :], narrow(bank(lane, 2)[:, HALF:]), ALU.add))
                        nc.vector.tensor_tensor(
                            state[:, :, :], state[:, :, :], chunk_decay[:, :, c].unsqueeze(2).broadcast_to([P, J, C]), ALU.mult).then_inc(sig["state_ready"], 1)
                        if d == 1:
                            for q in range(2):
                                out = y[part(c % 2), c // 2, :].rearrange("p (j q n) -> p q j n", q=2, n=C)[:, q]
                                last = nc.vector.tensor_tensor(out, out, narrow(bank(lane, 3 if q == 0 else 1)[part(c % 2), 0:HALF]), ALU.add)
                            last.then_inc(sig["y_copied"], 1)


def stage_rwkv_bonus(p, r_dram, kr_dram, vT, down, up, mix_k, bonus):
    nc = p.nc
    p.begin_stage()
    chain = p.semaphore("dve_chain")
    rates_ready = p.semaphore("rb_rates_ready")
    rates_read = p.semaphore("rb_rates_read")
    products_ready = p.semaphore("rb_products_ready")
    sums_ready = p.semaphore("rb_sums_ready")
    sums_read = p.semaphore("rb_sums_read")
    r_loaded, kr_loaded = p.semaphores("rp_r_loaded", 2), p.semaphores("rp_kr_loaded", 2)
    with ExitStack() as local:
        sb = lambda name, shape: local.enter_context(nc.sbuf_tensor(f"rb_{name}", shape, F32))
        rates = sb("rates", [P, 2, TOK])
        double = sb("double", [P, WT])
        r_in, kr_in = sb("r_in", [P, 2, TOK]), sb("kr_in", [P, 2, TOK])
        with nc.Block() as block:
            @block.sync
            def _(sp):
                for j in range(R_PAIRS):
                    if j >= 2:
                        sp.wait_ge(products_ready, j - 1)
                    sp.dma_start(r_in[:, j % 2, :], r_dram[j]).then_inc(r_loaded[j % 2], 16)
                    sp.dma_start(kr_in[:, j % 2, :], kr_dram[j]).then_inc(kr_loaded[j % 2], 16)

            @block.tensor
            def _(pe):
                for j in range(R_PAIRS):
                    if j:
                        pe.wait_ge(rates_read, 6 * j)
                    if j:
                        pe.wait_ge(sums_read, 3 * j)
                    lora_products(nc, p, up[:, 1], down[:, 1], 0, j, 0)
                    lora_products(nc, p, up[:, 1], down[:, 1], 1, j, 3).then_inc(rates_ready, 1)
                    pe.wait_ge(products_ready, j + 1)
                    for n, (at, width) in enumerate(GROUPS):
                        nc.tensor.matmul(p.psum[:, n, 0:width], p.const("head_ones"),
                                                         rates[:, 0, at:at + width], start=True, stop=True).then_inc(sums_ready, 1)

            @block.scalar
            def _(act):
                for j in range(R_PAIRS):
                    act.wait_ge(rates_ready, j + 1)
                    if j:
                        act.wait_ge(sums_ready, 3 * j)
                    for d in range(2):
                        for n, (at, width) in enumerate(GROUPS):
                            nc.scalar.activation(rates[:, d, at:at + width], p.psum[:, 3 * d + n, 0:width],
                                                                 ACT.Sigmoid, bias=p.param("r_a0", WT * d + j)).then_inc(rates_read, 1)

            @block.vector
            def _(dve):
                made = [0]

                def then(instruction):
                    made[0] += 1
                    instruction.then_inc(chain, 1)
                    dve.wait_ge(chain, made[0])

                then(nc.vector.tensor_scalar(double[:, :], mix_k[:, :], 2.0, None, ALU.mult))
                for j in range(R_PAIRS):
                    dve.wait_ge(rates_read, 6 * (j + 1))
                    r0 = rates[:, 0, :]
                    dve.wait_ge(r_loaded[j % 2], 16 * (j // 2 + 1))
                    dve.wait_ge(kr_loaded[j % 2], 16 * (j // 2 + 1))
                    then(nc.vector.tensor_tensor(r0, r0, rates[:, 1, :], ALU.add))
                    then(nc.vector.tensor_scalar(r0, r0, p.param("r_k_a", j), double[:, j:j + 1], ALU.mult, ALU.add))
                    then(nc.vector.tensor_tensor(r0, r0, kr_in[:, j % 2, :], ALU.mult))
                    nc.vector.scalar_tensor_tensor(r0, r0, p.param("r_r_k", j), r_in[:, j % 2, :], ALU.mult, ALU.mult).then_inc(products_ready, 1)
                    for n, (at, width) in enumerate(GROUPS):
                        dve.wait_ge(sums_ready, 3 * j + n + 1)
                        for rows, late in ((slice(0, R_DIM), R_CHUNK), (slice(R_DIM, P), 0)):
                            last = nc.vector.tensor_tensor(bonus[rows, j, at:at + width], p.psum[rows, n, 0:width],
                                                           vT[rows, j, late + at:late + at + width], ALU.mult)
                        last.then_inc(sums_read, 1)


def stage_rwkv_layernorm(p, y, bonus):
    nc = p.nc
    H = R_HEADS
    p.begin_stage()
    turned = p.semaphore("rl_turned")
    added = p.semaphore("rl_added")
    centred = p.semaphore("rl_centred")
    squared = p.semaphore("rl_squared")
    sums = p.semaphore("rl_sums")
    roots = p.semaphore("rl_roots")
    chain = p.semaphore("dve_chain")
    with ExitStack() as local:
        sq = local.enter_context(nc.sbuf_tensor("rl_squares", [P, 2, W], F32))
        st = local.enter_context(nc.sbuf_tensor("rl_stat", [P, TILES, 4, H], F32))
        by_head = lambda a: a.rearrange("p (h n) -> p h n", h=H)
        wide = lambda a: a.unsqueeze(2).broadcast_to([P, H, R_DIM])
        with nc.Block() as block:
            @block.tensor
            def _(pe):
                for t in range(TILES):
                    if t >= 8:
                        pe.wait_ge(added, t - 7)
                    for j in range(WT):
                        last = nc.tensor.transpose(p.psum[:, t % 8, j * P:(j + 1) * P], bonus[:, j, t * P:(t + 1) * P], p.const("ident"))
                    last.then_inc(turned, 1)

            @block.scalar
            def _(act):
                for t in range(TILES):
                    act.wait_ge(centred, t + 1)
                    if t >= 2:
                        act.wait_ge(sums, t - 1)
                    nc.scalar.activation(sq[:, t % 2, :], y[:, t, :], ACT.Square).then_inc(squared, 1)
                act.wait_ge(sums, TILES)
                nc.scalar.activation(st[:, :, 2, :], st[:, :, 2, :], ACT.Sqrt).then_inc(roots, 1)

            @block.vector
            def _(dve):
                made = [0]

                def then(instruction):
                    made[0] += 1
                    instruction.then_inc(chain, 1)
                    dve.wait_ge(chain, made[0])

                for t in range(TILES + 1):
                    if t < TILES:
                        yt = by_head(y[:, t, :])
                        dve.wait_ge(turned, t + 1)
                        nc.vector.tensor_tensor(y[:, t, :], y[:, t, :], p.psum[:, t % 8, :], ALU.add).then_inc(added, 1)
                        dve.wait_ge(added, t + 1)
                        then(nc.vector.tensor_reduce(st[:, t, 0, :], yt, AX.X, ALU.add))
                        then(nc.vector.tensor_scalar(st[:, t, 1, :], st[:, t, 0, :], 1.0 / R_DIM, None, ALU.mult))
                        nc.vector.tensor_tensor(yt, yt, wide(st[:, t, 1, :]), ALU.subtract).then_inc(centred, 1)
                    if t:
                        dve.wait_ge(squared, t)
                        then(nc.vector.tensor_reduce(st[:, t - 1, 3, :], by_head(sq[:, (t - 1) % 2, :]), AX.X, ALU.add))
                        nc.vector.tensor_scalar(st[:, t - 1, 2, :], st[:, t - 1, 3, :], 1.0 / R_DIM, R_LN_EPS, ALU.mult, ALU.add).then_inc(sums, 1)
                dve.wait_ge(roots, 1)
                then(nc.vector.reciprocal(st[:, :, 3, :], st[:, :, 2, :]))
                for t in range(TILES):
                    yt = by_head(y[:, t, :])
                    nc.vector.tensor_tensor(yt, yt, wide(st[:, t, 3, :]), ALU.mult).then_inc(centred, 1)


def rwkv_branch(p, arena, hT, mix, spill):
    nc = p.nc
    w_in = p.dram["l0_w_in"]
    free = arena[:, KT * TOK:]
    operands = lambda a: a.rearrange("p (j c k t) -> p j c k t", j=R_PAIRS, c=R_CHUNKS, k=2)
    wide = lambda a: a.rearrange("p (j t) -> p j t", j=WT)
    with ExitStack() as outer:
        so = lambda name, shape: outer.enter_context(nc.sbuf_tensor(name, shape, F32))
        vT = so("r_vT", [P, WT, R_CHUNK + TOK])
        down, up = so("r_down", [P, 2, TOK]), so("r_up", [P, 2, W])
        taps, mix_k = so("r_taps", [P, 2, 12]), so("r_mix_k", [P, WT])
        chunk_decay = so("r_chunk_decay", [P, R_PAIRS, R_CHUNKS])
        raw, shifted = wide(free[:, 0:WT * TOK]), wide(free[:, WT * TOK:])
        stage_shift_taps(p, taps)
        spilled = lambda n: spill[n].rearrange("k p t -> p k t")
        every, even, odd = slice(0, P), slice(0, R_DIM), slice(R_DIM, P)
        for which, outs in enumerate(([(every, shifted)], [(every, shifted)],
                                      [(even, vT[even, :, R_CHUNK:]), (odd, vT[odd, :, 0:TOK])])):
            stage_project(p, f"r{which}", hT, w_in, [(M_IN + which * W, W, ACT.Copy, raw, False, GROUPS)])
            stage_token_shift(p, raw, outs, taps, which)
            if which < 2:
                stage_copies(p, [(spilled(1 + which), shifted)])
        stage_project(p, "rz", hT, w_in, [
            (M_IN + 3 * W, W, ACT.Silu, raw, False, GROUPS),
            (M_IN + 4 * W, P, ACT.Tanh, down[:, 0], False, GROUPS), (M_IN + 4 * W + P, P, ACT.Copy, down[:, 1], False, GROUPS)])
        stage_copies(p, [(spilled(0), raw), (up[:, 0, :], p.dram["w_up"]), (up[:, 1, :], p.dram["a_up"])])
        with nc.Block() as block:
            @block.vector
            def _(dve):
                nc.vector.memset(vT[even, :, 0:R_CHUNK], 0.0)
                nc.vector.memset(vT[odd, :, TOK:], 0.0)
                at = PARAMS["r_k_a"][0]
                nc.vector.tensor_scalar(mix_k[:, :], p.params[:, at:at + WT], -1.0, 1.0, ALU.mult, ALU.add)
        y = so("r_y", [P, TILES, W])
        queries, keys = operands(arena[:, 0:KT * TOK]), operands(free)
        for d in range(2):
            stage_rwkv_prepare(p, d, spill[1], spill[2], down, up, mix_k, queries, keys, chunk_decay)
            stage_rwkv_scan(p, d, queries, keys, vT, chunk_decay, y)
        bonus, factor = wide(arena[:, 0:WT * TOK]), wide(free[:, 0:WT * TOK])
        stage_rwkv_bonus(p, spill[1], spill[2], vT, down, up, mix_k, bonus)
        stage_rwkv_layernorm(p, y, bonus)
        stage_copies(p, [(factor, spilled(0))])
        stage_turn_back(p, y, range(TILES), lambda h: p.param("r_ln_w", h), lambda h: p.param("r_ln_b", h), factor, mix, WT)


LAT_GROUPS = ((256, 512, 0), (768, 512, 512))
LAT_TILES = range(CTX_TILES, TILES)
FILTER_HIDDEN, FILTER_POS, BANDS = 64, 33, 16


def stage_output(p, layer, arena, mix, gate_dram, x, tiles, x_out, stored, final_gain=None):
    nc = p.nc
    p.begin_stage()
    loaded = p.semaphore("out_loaded")
    x_loaded = p.semaphores("out_x_loaded", 2)
    products_ready = p.semaphore("out_products_ready")
    gated = p.semaphore("out_gated")
    summed = p.semaphore("out_summed")
    squares_ready = p.semaphore("out_squares_ready")
    roots_ready = p.semaphore("out_roots_ready")
    chain = p.semaphore("dve_chain")
    normed = p.semaphore("out_normed")
    mixT = arena[:, 0:KT * TOK].rearrange("p (k t) -> p k t", k=KT)
    at = tiles[0] * P
    with ExitStack() as local:
        sb = lambda name, shape: local.enter_context(nc.sbuf_tensor(f"out_{name}{layer}", shape, F32))
        weight = sb("weight", [P, KT, D])
        gate = sb("gate", [P, 2, D])
        xt = sb("x", [P, 2, D])
        res = sb("res", [P, 2, D])
        junk = sb("junk", [P, D])
        gain = sb("gain", [P, D])
        stat = sb("stat", [P, TILES, 4])
        assert len(tiles) % 2 == 0
        finished = normed if final_gain is not None else summed
        with nc.Block() as block:
            @block.sync
            def _(sp):
                sp.dma_start(mixT[:, :, at:TOK], mix[:, :, at:TOK].rearrange("k p t -> p k t")).then_inc(loaded, 16)
                sp.dma_start(weight[:, :, :], p.dram[f"l{layer}_w_out"].rearrange("(k p) n -> p k n", p=P)).then_inc(loaded, 16)
                sp.dma_start(gate[:, :, :], gate_dram).then_inc(loaded, 16)
                if final_gain is not None:
                    sp.dma_start(gain[:, :], final_gain).then_inc(loaded, 16)
                for i, t in enumerate(tiles):
                    if i >= 2:
                        sp.wait_ge(finished, i - 1)
                    sp.dma_start(xt[:, i % 2, :], x(t)).then_inc(x_loaded[i % 2], 16)
                    if i:
                        sp.wait_ge(finished, i)
                        sp.dma_start(x_out(tiles[i - 1]), res[:, (i - 1) % 2, :]).then_inc(stored[(i - 1) % 2], 16)
                sp.wait_ge(finished, len(tiles))
                sp.dma_start(x_out(tiles[-1]), res[:, 1, :]).then_inc(stored[1], 16)
                sp.wait_ge(stored[0], 16 * len(tiles) // 2)
                sp.wait_ge(stored[1], 16 * len(tiles) // 2)

            @block.tensor
            def _(pe):
                pe.wait_ge(loaded, 16 * (3 + (final_gain is not None)))
                for i, t in enumerate(tiles):
                    if i >= 4:
                        pe.wait_ge(gated, i - 3)
                    for k in range(KT):
                        lhsT = mixT[:, k, t * P:(t + 1) * P]
                        for n in range(2):
                            last = nc.tensor.matmul(p.psum[:, 2 * (i % 4) + n, :], lhsT, weight[:, k, n * BANK:(n + 1) * BANK],
                                                    start=(k == 0), stop=(k == KT - 1))
                    last.then_inc(products_ready, 1)

            @block.scalar
            def _(act):
                if final_gain is not None:
                    for i in range(len(tiles)):
                        act.wait_ge(summed, i + 1)
                        if i:
                            act.wait_ge(squares_ready, i)
                        nc.scalar.activation(junk[:, :], res[:, i % 2, :], ACT.Square,
                                                                accum_out=stat[:, i, 0:1]).then_inc(squares_ready, 1)
                        act.wait_ge(roots_ready, 2 * i + 1)
                        nc.scalar.activation(stat[:, i, 2:3], stat[:, i, 1:2], ACT.Sqrt).then_inc(roots_ready, 1)

            @block.vector
            def _(dve):
                made = [0]

                def then(instruction):
                    made[0] += 1
                    instruction.then_inc(chain, 1)
                    dve.wait_ge(chain, made[0])

                for i, t in enumerate(tiles):
                    dve.wait_ge(products_ready, i + 1)
                    dve.wait_ge(x_loaded[i % 2], 16 * (i // 2 + 1))
                    if i >= 2:
                        dve.wait_ge(stored[i % 2], 16 * (i // 2))
                    out = res[:, i % 2, :]
                    nc.vector.tensor_tensor(
                        out, p.psum[:, 2 * (i % 4):2 * (i % 4) + 2, :].rearrange("p b n -> p (b n)"),
                        gate[:, 1 if t < CTX_TILES else 0, :], ALU.mult).then_inc(gated, 1)
                    dve.wait_ge(gated, i + 1)
                    nc.vector.tensor_tensor(out, out, xt[:, i % 2, :], ALU.add).then_inc(summed, 1)
                    if final_gain is not None:
                        dve.wait_ge(squares_ready, i + 1)
                        nc.vector.tensor_scalar(stat[:, i, 1:2], stat[:, i, 0:1], 1.0 / D, EPS, ALU.mult, ALU.add).then_inc(roots_ready, 1)
                        dve.wait_ge(roots_ready, 2 * i + 2)
                        then(nc.vector.reciprocal(stat[:, i, 3:4], stat[:, i, 2:3]))
                        nc.vector.scalar_tensor_tensor(out, out, stat[:, i, 3:4], gain[:, :], ALU.mult, ALU.mult).then_inc(normed, 1)


G_HEADS, G_CHUNK, G_LEVELS = 4, 128, 7
G_LAT_CHUNKS = LAT // G_CHUNK


def const_hgrn():
    s, t = np.arange(P)[:, None], np.arange(P)[None]
    out = []
    for d in range(2):
        before = (s < t) if d == 0 else (s > t)
        for n in range(G_LEVELS):
            out.append(before & ((s >> (n + 1)) == (t >> (n + 1))) & ((s >> n) != (t >> n)))
    out.append(s == t)
    return np.concatenate(out, axis=1).astype(np.float32)


def stage_lower_bound(p, bound):
    nc = p.nc
    p.begin_stage()
    chain = p.semaphore("dve_chain")
    exps = p.semaphore("lower_exps")
    raw = lambda i: p.params[:, PARAMS["lower"][0] + WT * i:PARAMS["lower"][0] + WT * (i + 1)]
    with ExitStack() as local:
        t = local.enter_context(nc.sbuf_tensor("lower_t", [P, 5, WT], F32))
        with nc.Block() as block:
            @block.scalar
            def _(act):
                act.wait_ge(chain, 3)
                nc.scalar.activation(t[:, 1:3, :], t[:, 1:3, :], ACT.Exp).then_inc(exps, 1)

            @block.vector
            def _(dve):
                made = [0]

                def then(instruction):
                    made[0] += 1
                    instruction.then_inc(chain, 1)
                    dve.wait_ge(chain, made[0])

                then(nc.vector.tensor_tensor(t[:, 0, :], raw(0), raw(1), ALU.max))
                for i in range(2):
                    then(nc.vector.tensor_tensor(t[:, 1 + i, :], raw(i), t[:, 0, :], ALU.subtract))
                dve.wait_ge(exps, 1)
                then(nc.vector.tensor_tensor(t[:, 3, :], t[:, 1, :], t[:, 2, :], ALU.add))
                then(nc.vector.reciprocal(t[:, 4, :], t[:, 3, :]))
                for i in range(2):
                    then(nc.vector.tensor_tensor(t[:, 1 + i, :], t[:, 1 + i, :], t[:, 4, :], ALU.mult))
                then(nc.vector.tensor_tensor(t[:, 3, :], t[:, 1, :], t[:, 2, :], ALU.add))
                then(nc.vector.tensor_tensor(bound[:, 0, :], t[:, 3, :], t[:, 1, :], ALU.subtract))
                then(nc.vector.tensor_scalar(bound[:, 1, :], bound[:, 0, :], -1.0, 1.0, ALU.mult, ALU.add))
                then(nc.vector.tensor_scalar(bound[:, 2, :], bound[:, 1, :], -1.0, None, ALU.mult))


def stage_hgrn(p, arena, qT, gates, v, bound, y):
    nc = p.nc
    H, C, L = G_HEADS, G_CHUNK, G_LEVELS
    units = [(d, h) for d in range(2) for h in range(H)]
    U = len(units)
    UP = L + 2
    p.begin_stage()
    sig = {n: p.semaphore("g_" + n) for n in (
        "floored", "logs_ready", "decay_ready", "k_ready", "gaps_ready", "exps_ready", "keyed", "queried", "level_ready",
        "scores_ready", "merged", "across_copied", "keys_turned", "keys_copied", "update_ready", "state_ready", "outputs_ready", "y_copied",
        "pair_cleared")}
    chain = p.semaphore("dve_chain")
    masks_loaded = p.semaphore("g_masks_loaded")
    SLOT = L * LAT + LAT + TOK
    slot = lambda u: arena[:, (u % 2) * SLOT:(u % 2 + 1) * SLOT]
    level = lambda u, n: slot(u)[:, n * LAT:(n + 1) * LAT]
    q_decayed = lambda u: slot(u)[:, L * LAT:(L + 1) * LAT]
    k_decayed = lambda u: slot(u)[:, (L + 1) * LAT:]
    chunked = lambda a: a.rearrange("p (c t) -> p c t", t=C)

    def halves(a, n, d):
        v4 = a.rearrange("p (b k t) -> p b k t", k=2, t=1 << n)
        return v4[:, :, 1 - d, :], v4[:, :, d, :]

    with ExitStack() as local:
        sb = lambda name, shape: local.enter_context(nc.sbuf_tensor(f"g_{name}", shape, F32))
        decay = sb("decay", [P, TOK])
        carry_on = sb("carry_on", [P, TOK])
        k = sb("k", [P, 2, TOK])
        gap = arena[:, 2 * SLOT:2 * SLOT + TOK]
        pairs = sb("pairs", [P, 2, G_LAT_CHUNKS, C])
        ends = sb("ends", [P, 2, TILES])
        state = sb("state", [P, P])
        keys = sb("keys", [P, 2, P])
        masks = local.enter_context(nc.sbuf_tensor("g_masks", [P, (2 * L + 1) * P], mybir.dt.uint8))
        mask = lambda d, n: masks[:, (2 * L if n == L else d * L + n) * P:][:, 0:P].unsqueeze(1).broadcast_to([P, 4, P])
        with nc.Block() as block:
            @block.sync
            def _(sp):
                sp.dma_start(slot(1)[:, 0:(2 * L + 1) * P], p.dram["const_hgrn"]).then_inc(masks_loaded, 16)

            @block.scalar
            def _(act):
                def prepare(u, n):
                    d, h = units[u]
                    if n == 0:
                        act.wait_ge(sig["floored"], u + 1)
                        nc.scalar.activation(gates[d][:, h, :], gates[d][:, h, :], ACT.Ln,
                                                                    bias=bound[:, 0, h:h + 1]).then_inc(sig["logs_ready"], 1)
                        act.wait_ge(sig["decay_ready"], u + 1)
                        at = C - 1 if d == 0 else 0
                        nc.scalar.activation(ends[:, u % 2, :], chunked(decay[:, :])[:, :, at], ACT.Exp).then_inc(sig["exps_ready"], 1)
                    if n <= L:
                        act.wait_ge(sig["gaps_ready"], (L + 1) * u + n + 1)
                    out = level(u, n) if n < L else k_decayed(u) if n == L else q_decayed(u)
                    src = decay[:, CTX:TOK] if n == L + 1 else gap[:, 0:TOK if n == L else LAT]
                    nc.scalar.activation(out, src, ACT.Exp).then_inc(sig["exps_ready"], 1)

                for n in range(UP):
                    prepare(0, n)
                for u, (d, h) in enumerate(units):
                    for n in range(UP):
                        if u + 1 < U:
                            if n == 0:
                                if u:
                                    act.wait_ge(sig["outputs_ready"], u * G_LAT_CHUNKS)
                                if u:
                                    act.wait_ge(sig["update_ready"], u * TILES)
                            prepare(u + 1, n)
                    for i, c in enumerate(scan_order(d, TILES, CTX_TILES)):
                        act.wait_ge(sig["keys_turned"], u * TILES + i + 1)
                        if u or i >= 2:
                            act.wait_ge(sig["update_ready"], u * TILES + i - 1)
                        nc.scalar.copy(keys[:, i % 2, :], p.psum[:, 4 + i % 2, 0:P]).then_inc(sig["keys_copied"], 1)

            @block.gpsimd
            def _(pool):
                def prepare(u, n):
                    d, h = units[u]
                    if n == 0:
                        pool.wait_ge(sig["k_ready"], u + 1)
                    pool.wait_ge(sig["exps_ready"], u * (UP + 1) + n + 2)
                    if n < L:
                        out, _ = halves(level(u, n), n, d)
                        q, _ = halves(qT[:, h, :], n, d)
                    elif n == L:
                        out, q = k_decayed(u), k[:, u % 2, :]
                    else:
                        out, q = q_decayed(u), qT[:, h, :]
                    nc.gpsimd.tensor_tensor(out, out, q, ALU.mult).then_inc(sig["queried"], 1)

                for u in range(U):
                    for n in range(UP):
                        prepare(u, n)

            @block.vector
            def _(dve):
                made = [0]

                def then(instruction):
                    made[0] += 1
                    instruction.then_inc(chain, 1)
                    dve.wait_ge(chain, made[0])

                def prepare(u, n):
                    d, h = units[u]
                    gate, b = gates[d][:, h, :], decay[:, :]
                    if n == 0:
                        if h == 0:
                            then(nc.vector.memset(carry_on[:, :], 1.0))
                            then(nc.vector.memset(chunked(carry_on[:, :])[:, :, 0 if d == 0 else C - 1], 0.0))
                        if u >= 2:
                            dve.wait_ge(sig["scores_ready"], 2 * (L + 1) * (u - 1))
                        if u >= 2:
                            dve.wait_ge(sig["queried"], UP * (u - 1))
                        nc.vector.tensor_scalar(k[:, u % 2, :], gate, bound[:, 2, h:h + 1], bound[:, 1, h:h + 1],
                                                                    ALU.mult, ALU.add).then_inc(sig["k_ready"], 1)
                        dve.wait_ge(sig["k_ready"], u + 1)
                        nc.vector.tensor_scalar(gate, gate, bound[:, 1, h:h + 1], 2.0 ** -62, ALU.mult, ALU.max).then_inc(sig["floored"], 1)
                        dve.wait_ge(sig["logs_ready"], u + 1)
                        order = slice(None) if d == 0 else slice(None, None, -1)
                        if u:
                            dve.wait_ge(sig["exps_ready"], u * (UP + 1))
                        nc.vector.tensor_tensor_scan(b[:, order], carry_on[:, order], gate[:, order], 0.0,
                                                                             ALU.mult, ALU.add).then_inc(sig["decay_ready"], 1)
                        dve.wait_ge(sig["decay_ready"], u + 1)
                    dve.wait_ge(sig["exps_ready"], u * (UP + 1) + n + 1)
                    if n < L:
                        bq, bk = halves(b[:, CTX:TOK], n, d)
                        gq, gk = halves(gap[:, 0:LAT], n, d)
                        at = (1 << n) - 1 if d == 0 else 0
                        anchor = bk[:, :, at:at + 1].broadcast_to(list(bk.shape))
                        nc.vector.tensor_tensor(gq, bq, anchor, ALU.subtract)
                        nc.vector.tensor_tensor(gk, anchor, bk, ALU.subtract).then_inc(sig["gaps_ready"], 1)
                        _, keyed = halves(level(u, n), n, d)
                        _, kk = halves(k[:, u % 2, CTX:TOK], n, d)
                        dve.wait_ge(sig["exps_ready"], u * (UP + 1) + n + 2)
                        nc.vector.tensor_tensor(keyed, keyed, kk, ALU.mult).then_inc(sig["keyed"], 1)
                    elif n == L:
                        at = C - 1 if d == 0 else 0
                        end = chunked(b)[:, :, at:at + 1].broadcast_to([P, TILES, C])
                        nc.vector.tensor_tensor(chunked(gap[:, :]), end, chunked(b), ALU.subtract).then_inc(sig["gaps_ready"], 1)

                dve.wait_ge(masks_loaded, 16)
                then(nc.vector.tensor_copy(masks[:, :], slot(1)[:, 0:(2 * L + 1) * P]))
                for n in range(UP):
                    prepare(0, n)
                for u, (d, h) in enumerate(units):
                    if h < 2:
                        then(nc.vector.memset(pairs[:, u % 2], 0.0))
                    for n in range(UP):
                        if u + 1 < U:
                            prepare(u + 1, n)
                        if n <= L:
                            for g in range(2):
                                m = u * 2 * (L + 1) + 2 * n + g
                                dve.wait_ge(sig["scores_ready"], m + 1)
                                if m >= 2:
                                    dve.wait_ge(sig["merged"], m - 1)
                                nc.vector.copy_predicated(
                                    pairs[:, u % 2, 4 * g:4 * g + 4, :], mask(d, n), chunked(p.psum[:, m % 4, :])).then_inc(sig["merged"], 1)
                    nc.vector.memset(state[:, :], 0.0).then_inc(sig["state_ready"], 1)
                    dve.wait_ge(sig["state_ready"], u * (TILES + 1) + 1)
                    done = 0
                    for i, c in enumerate(scan_order(d, TILES, CTX_TILES)):
                        dve.wait_ge(sig["update_ready"], u * TILES + i + 1)
                        if c >= CTX_TILES:
                            dve.wait_ge(sig["outputs_ready"], u * G_LAT_CHUNKS + done + 1)
                            out, src = y[:, c - CTX_TILES, h * P:(h + 1) * P], p.psum[:, 6 + i % 2, 0:P]
                            if d == 0:
                                nc.vector.tensor_copy(out, src).then_inc(sig["y_copied"], 1)
                            else:
                                nc.vector.tensor_tensor(out, out, src, ALU.add).then_inc(sig["y_copied"], 1)
                            done += 1
                        nc.vector.scalar_tensor_tensor(
                            state[:, :], state[:, :], ends[:, u % 2, c:c + 1], p.psum[:, 4 + i % 2, P:2 * P], ALU.mult, ALU.add).then_inc(sig["state_ready"], 1)
                        dve.wait_ge(sig["state_ready"], u * (TILES + 1) + i + 2)

            @block.tensor
            def _(pe):
                for u, (d, h) in enumerate(units):
                    for n in range(L + 1):
                        if n < L:
                            pe.wait_ge(sig["keyed"], u * L + n + 1)
                            pe.wait_ge(sig["queried"], u * UP + n + 1)
                        else:
                            pe.wait_ge(sig["k_ready"], u + 1)
                        for g in range(2):
                            m = u * 2 * (L + 1) + 2 * n + g
                            if m >= 4:
                                pe.wait_ge(sig["merged"], m - 3)
                            for c in range(4 * g, 4 * g + 4):
                                at = slice(c * C, (c + 1) * C)
                                left = level(u, n)[:, at] if n < L else k[:, u % 2, CTX:TOK][:, at]
                                right = level(u, n)[:, at] if n < L else qT[:, h, at]
                                last = nc.tensor.matmul(p.psum[:, m % 4, (c - 4 * g) * C:(c - 4 * g + 1) * C], left, right,
                                                        start=True, stop=True)
                            last.then_inc(sig["scores_ready"], 1)
                    pe.wait_ge(sig["merged"], (u + 1) * 2 * (L + 1))
                    pe.wait_ge(sig["queried"], (u + 1) * UP)
                    done = 0
                    for i, c in enumerate(scan_order(d, TILES, CTX_TILES)):
                        states = u * (TILES + 1) + i + 1
                        if states > 1:
                            pe.wait_ge(sig["state_ready"], states - 1)
                        nc.tensor.transpose(p.psum[:, 4 + i % 2, 0:P], k_decayed(u)[:, c * C:(c + 1) * C],
                                                                    p.const("ident")).then_inc(sig["keys_turned"], 1)
                        if c >= CTX_TILES:
                            lat = c - CTX_TILES
                            if u or done >= 2:
                                pe.wait_ge(sig["y_copied"], u * G_LAT_CHUNKS + done - 1)
                            nc.tensor.matmul(p.psum[:, 6 + i % 2, 0:P], pairs[:, u % 2, lat, :], v[:, c, h * P:(h + 1) * P],
                                             start=True, stop=False)
                            pe.wait_ge(sig["state_ready"], states)
                            nc.tensor.matmul(
                                p.psum[:, 6 + i % 2, 0:P], q_decayed(u)[:, lat * C:(lat + 1) * C], state[:, :], start=False, stop=True).then_inc(sig["outputs_ready"], 1)
                            done += 1
                        pe.wait_ge(sig["keys_copied"], u * TILES + i + 1)
                        nc.tensor.matmul(p.psum[:, 4 + i % 2, P:2 * P], keys[:, i % 2, :],
                                                                  v[:, c, h * P:(h + 1) * P], start=True, stop=True).then_inc(sig["update_ready"], 1)


def hgrn_branch(p, arena, hT, mix):
    nc = p.nc
    w_in = p.dram["l1_w_in"]
    with ExitStack() as outer:
        so = lambda name, shape: outer.enter_context(nc.sbuf_tensor(name, shape, F32))
        y = so("g_y", [P, G_LAT_CHUNKS, W])
        bound = so("g_bound", [P, 3, WT])
        with ExitStack() as inner:
            si = lambda name, shape: inner.enter_context(nc.sbuf_tensor(name, shape, F32))
            gates = [si(f"g_gates{d}", [P, WT, TOK]) for d in range(2)]
            v = si("g_v", [P, TILES, W])
            qT = si("g_qT", [P, WT, LAT])
            z_tok = arena[:, KT * TOK:][:, 0:G_LAT_CHUNKS * W].rearrange("p (t n) -> p t n", n=W)
            stage_lower_bound(p, bound)
            stage_project(p, "g", hT, w_in, [
                (2 * W, W, ACT.Sigmoid, gates[0], False, GROUPS), (3 * W, W, ACT.Sigmoid, gates[1], False, GROUPS),
                (W, W, ACT.Copy, v, True, (0, TILES)),
                (0, W, ACT.Copy, qT, False, LAT_GROUPS),
                (4 * W, W, ACT.Silu, z_tok, True, (CTX_TILES, TILES, CTX_TILES))])
            z_dram = p.scratch["z"]
            stage_copies(p, [(z_dram, z_tok)])
            stage_hgrn(p, arena, qT, gates, v, bound, y)
        gate = arena[:, 0:G_LAT_CHUNKS * W].rearrange("p (t n) -> p t n", n=W)
        stage_copies(p, [(gate, z_dram)])
        stage_heads_rmsnorm(p, y, gate, range(G_LAT_CHUNKS), EPS)
        stage_turn_back(p, y, range(G_LAT_CHUNKS), lambda h: p.param("g_norm_g", h), None, None, mix, 0, CTX)


F_TILES = LAT // 2 // P


def const_hyena():
    f32 = np.float32
    pos = np.arange(LAT, dtype=f32)
    t = pos / f32(LAT)
    bands = np.linspace(1e-4, BANDS - 1, BANDS, dtype=f32)
    ang = (f32(2.0 * np.pi / LAT) * pos[:, None] * bands).astype(f32)
    z = np.concatenate([t[:, None], np.cos(ang), np.sin(ang)], axis=-1).astype(f32)
    top, low = np.log(1e-2) / 0.3, np.log(1e-2) / 1.5
    deltas = np.abs(np.linspace(low, top, W, dtype=f32))
    window = (np.exp(-t[:, None] * deltas) + f32(0.05)).astype(f32)
    order = np.concatenate([np.arange(0, LAT, 2), np.arange(1, LAT, 2)])
    turn = (order[:, None] * (2 * np.arange(LAT // 2)[None] + 1)) % (4 * LAT)
    cos, sin = (fn(np.pi * turn / (2 * LAT)).astype(f32) for fn in (np.cos, np.sin))
    down = np.stack([m.reshape(KT, P, F_TILES, P).transpose(2, 1, 0, 3).reshape(F_TILES, P, LAT) for m in (cos, sin)], axis=2)
    up = np.stack([m.T.reshape(F_TILES, P, LAT) for m in (cos, sin)], axis=2)
    return {"positions": np.ascontiguousarray(z[order].T), "window": window[order].reshape(KT, P, W),
            "transform": np.ascontiguousarray(down), "transform_back": np.ascontiguousarray(up)}


def stage_filters(p, sums, differences, magnitudes):
    nc = p.nc
    TWO_PI = 2 * np.pi
    HIGH = float(np.float32(np.round(TWO_PI * 4096) / 4096))
    MIDDLE = float(np.float32(TWO_PI - HIGH))
    ROUND = 1.5 * 2.0 ** 23
    PI = 3.14159250259
    F = FILTER_HIDDEN
    p.begin_stage()
    loaded = p.semaphore("f_loaded")
    window_loaded = p.semaphores("f_window_loaded", 2)
    product_ready = p.semaphore("f_product_ready")
    reduced = p.semaphore("f_reduced")
    hidden_ready = p.semaphore("f_hidden_ready")
    taps_ready = p.semaphore("f_taps_ready")
    windowed = p.semaphore("f_windowed")
    absolute = p.semaphore("f_absolute")
    summed = p.semaphore("f_summed")
    chain = p.semaphore("dve_chain")
    with ExitStack() as local:
        sb = lambda name, shape: local.enter_context(nc.sbuf_tensor(f"f_{name}", shape, F32))
        positions, w1, w2, w3 = sb("positions", [FILTER_POS, LAT]), sb("w1", [FILTER_POS, F]), sb("w2", [F, F]), sb("w3", [F, 2 * W])
        angle, turns, hidden = sb("angle", [F, LAT]), sb("turns", [F, LAT]), sb("hidden", [F, LAT])
        window = sb("window", [P, 2, W])
        taps = sb("taps", [P, 2, 2, W])
        size = sb("size", [P, 2, 2, W])
        with nc.Block() as block:
            @block.sync
            def _(sp):
                for dst, name in ((positions, "positions"), (w1, "l1_hyena_w1"), (w2, "l1_hyena_w2"), (w3, "l1_hyena_w3")):
                    sp.dma_start(dst[:, :], p.dram[name]).then_inc(loaded, 16)
                for t in range(KT):
                    if t >= 2:
                        sp.wait_ge(windowed, 2 * (t - 1))
                    sp.dma_start(window[:, t % 2, :], p.dram["window"][t]).then_inc(window_loaded[t % 2], 16)

            @block.tensor
            def _(pe):
                pe.wait_ge(loaded, 64)
                for layer in range(2):
                    if layer:
                        pe.wait_ge(hidden_ready, layer)
                    for n in range(2):
                        at = slice(n * BANK, (n + 1) * BANK)
                        last = nc.tensor.matmul(p.psum[0:F, n, :], (w1, w2)[layer][:, :], (positions, hidden)[layer][:, at],
                                                start=True, stop=True)
                    last.then_inc(product_ready, 1)
                pe.wait_ge(hidden_ready, 2)
                for t in range(KT):
                    if t >= 2:
                        pe.wait_ge(windowed, 2 * (t - 1))
                    for n in range(2):
                        nc.tensor.matmul(p.psum[:, 2 + 2 * (t % 2) + n, :], hidden[:, t * P:(t + 1) * P],
                                                         w3[:, n * W:(n + 1) * W], start=True, stop=True).then_inc(taps_ready, 1)

            @block.scalar
            def _(act):
                for layer in range(2):
                    act.wait_ge(reduced, layer + 1)
                    nc.scalar.activation(hidden[:, :], angle[:, :], ACT.Sin).then_inc(hidden_ready, 1)
                for t in range(KT):
                    act.wait_ge(windowed, 2 * (t + 1))
                    if t >= 2:
                        act.wait_ge(summed, 2 * (t - 1))
                    nc.scalar.activation(size[:, t % 2], taps[:, t % 2], ACT.Abs).then_inc(absolute, 1)

            @block.gpsimd
            def _(pool):
                for t in range(KT):
                    pool.wait_ge(absolute, t + 1)
                    for n in range(2):
                        if t + n:
                            pool.wait_ge(summed, 2 * t + n)
                        if t + n:
                            nc.gpsimd.tensor_tensor(magnitudes[:, :], magnitudes[:, :], size[:, t % 2, n], ALU.add).then_inc(summed, 1)
                        else:
                            nc.gpsimd.tensor_copy(magnitudes[:, :], size[:, 0, 0]).then_inc(summed, 1)

            @block.vector
            def _(dve):
                made = [0]

                def then(instruction):
                    made[0] += 1
                    instruction.then_inc(chain, 1)
                    dve.wait_ge(chain, made[0])

                for layer in range(2):
                    dve.wait_ge(product_ready, layer + 1)
                    if layer:
                        dve.wait_ge(hidden_ready, layer)
                    bias = p.param(("b1", "b2")[layer], 0, F)
                    then(nc.vector.tensor_scalar(angle[:, :], p.psum[0:F, 0:2, :].rearrange("p b n -> p (b n)"), bias, None, ALU.add))
                    then(nc.vector.tensor_scalar(turns[:, :], angle[:, :], 1 / TWO_PI, ROUND, ALU.mult, ALU.add))
                    then(nc.vector.tensor_scalar(turns[:, :], turns[:, :], ROUND, None, ALU.subtract))
                    then(nc.vector.scalar_tensor_tensor(angle[:, :], turns[:, :], -HIGH, angle[:, :], ALU.mult, ALU.add))
                    then(nc.vector.scalar_tensor_tensor(angle[:, :], turns[:, :], -MIDDLE, angle[:, :], ALU.mult, ALU.add))
                    nc.vector.tensor_scalar(angle[:, :], angle[:, :], -PI, PI, ALU.max, ALU.min).then_inc(reduced, 1)
                for t in range(KT):
                    dve.wait_ge(window_loaded[t % 2], 16 * (t // 2 + 1))
                    if t >= 2:
                        dve.wait_ge(absolute, t - 1)
                    for n in range(2):
                        dve.wait_ge(taps_ready, 2 * t + n + 1)
                        nc.vector.tensor_tensor(taps[:, t % 2, n], p.psum[:, 2 + 2 * (t % 2) + n, :],
                                                              window[:, t % 2, :], ALU.mult).then_inc(windowed, 1)
                    dve.wait_ge(windowed, 2 * (t + 1))
                    nc.vector.tensor_tensor(sums[:, t, :], taps[:, t % 2, 0], taps[:, t % 2, 1], ALU.add)
                    then(nc.vector.tensor_tensor(differences[:, t, :], taps[:, t % 2, 0], taps[:, t % 2, 1], ALU.subtract))


def stage_conv_product(p, raw, uT, out, which):
    nc = p.nc
    p.begin_stage()
    chain = p.semaphore("dve_chain")
    dst = (uT, out, out)[which]
    with nc.Block() as block:
        @block.vector
        def _(dve):
            made = [0]

            def then(instruction):
                made[0] += 1
                instruction.then_inc(chain, 1)
                dve.wait_ge(chain, made[0])

            for j in range(WT):
                n = which * WT + j
                before, here, after = (p.param("short_w", 3 * WT * tap + n) for tap in range(3))
                o, r = dst[:, j, :], raw[:, j, :]
                then(nc.vector.tensor_scalar(o, r, here, p.param("short_b", n), ALU.mult, ALU.add))
                then(nc.vector.scalar_tensor_tensor(o[:, 1:LAT], r[:, 0:LAT - 1], before, o[:, 1:LAT], ALU.mult, ALU.add))
                then(nc.vector.scalar_tensor_tensor(o[:, 0:LAT - 1], r[:, 1:LAT], after, o[:, 0:LAT - 1], ALU.mult, ALU.add))
                if which == 2:
                    then(nc.vector.tensor_tensor(uT[:, j, :], uT[:, j, :], o, ALU.mult))


def stage_turn_u(p, uT, u_tok, x0T, zT):
    nc = p.nc
    p.begin_stage()
    turned = p.semaphore("turn_turned")
    copied = p.semaphore("turn_copied")
    with nc.Block() as block:
        @block.tensor
        def _(pe):
            for t in range(KT):
                at = slice((t % 4) * P, (t % 4 + 1) * P)
                for j in range(WT):
                    by_parity = uT[:, j, :].rearrange("p (n e) -> p e n", e=2)
                    last = nc.tensor.transpose(p.psum[:, t, j * P:(j + 1) * P], by_parity[:, t // 4, at], p.const("ident"))
                last.then_inc(turned, 1)

        @block.scalar
        def _(act):
            for t in range(KT):
                act.wait_ge(turned, t + 1)
                nc.scalar.copy(u_tok[:, t, :], p.psum[:, t, :]).then_inc(copied, 1)

        @block.gpsimd
        def _(pool):
            nc.gpsimd.tensor_tensor(x0T[:, :, :], x0T[:, :, :], zT[:, :, :], ALU.mult)


def stage_transform(p, u_tok, sums, differences, real, imag, spectrum, whole):
    nc = p.nc
    p.begin_stage()
    loaded = p.semaphores("t_loaded", 2)
    sums_ready = p.semaphore("t_sums_ready")
    odd_copied = p.semaphore("t_odd_copied")
    combined = p.semaphore("t_combined")
    chain = p.semaphore("dve_chain")
    with ExitStack() as local:
        sb = lambda name, shape: local.enter_context(nc.sbuf_tensor(f"t_{name}", shape, F32))
        matrix = sb("matrix", [P, 2, 2, LAT])
        cross, odd = sb("cross", [P, 2, W]), sb("odd", [P, 2, W])
        with nc.Block() as block:
            @block.sync
            def _(sp):
                for f in range(F_TILES):
                    if f >= 2:
                        sp.wait_ge(sums_ready, 2 * (f - 1))
                    sp.dma_start(matrix[:, f % 2], p.dram["transform"][f]).then_inc(loaded[f % 2], 16)

            @block.tensor
            def _(pe):
                for f in range(F_TILES):
                    pe.wait_ge(loaded[f % 2], 16 * (f // 2 + 1))
                    for part, taps in ((0, sums), (1, differences)):
                        if f:
                            pe.wait_ge(combined, 2 * (f - 1) + part + 1)
                        for t in range(KT):
                            left = matrix[:, f % 2, part, t * P:(t + 1) * P]
                            for n, right in enumerate((u_tok, taps)):
                                last = nc.tensor.matmul(p.psum[:, 4 * part + 2 * (t // 4) + n, :], left, right[:, t, :],
                                                        start=(t % 4 == 0), stop=(t % 4 == 3))
                        last.then_inc(sums_ready, 1)

            @block.scalar
            def _(act):
                for m in range(2 * F_TILES):
                    act.wait_ge(sums_ready, m + 1)
                    if m:
                        act.wait_ge(combined, m)
                    nc.scalar.copy(odd[:, :, :], p.psum[:, 4 * (m % 2) + 2:4 * (m % 2) + 4, :]).then_inc(odd_copied, 1)

            @block.vector
            def _(dve):
                made = [0]

                def then(instruction):
                    made[0] += 1
                    instruction.then_inc(chain, 1)
                    dve.wait_ge(chain, made[0])

                for f in range(F_TILES):
                    for part in range(2):
                        dve.wait_ge(odd_copied, 2 * f + part + 1)
                        even = p.psum[:, 4 * part:4 * part + 2, :]
                        nc.vector.tensor_tensor(spectrum[:, part, 0], even, odd[:, :, :], ALU.add)
                        first, second = (even, odd[:, :, :]) if part == 0 else (odd[:, :, :], even)
                        nc.vector.tensor_tensor(spectrum[:, part, 1], first, second, ALU.subtract).then_inc(combined, 1)
                    dve.wait_ge(combined, 2 * f + 2)
                    u_cos, u_sin = (spectrum[:, part, :, 0] for part in range(2))
                    k_cos, k_sin = (spectrum[:, part, :, 1] for part in range(2))
                    nc.vector.tensor_tensor(whole[:, 0], u_cos, k_cos, ALU.mult)
                    nc.vector.tensor_tensor(whole[:, 1], u_cos, k_sin, ALU.mult)
                    then(nc.vector.tensor_tensor(cross[:, :, :], u_sin, k_sin, ALU.mult))
                    then(nc.vector.tensor_tensor(whole[:, 0], whole[:, 0], cross[:, :, :], ALU.subtract))
                    then(nc.vector.tensor_tensor(cross[:, :, :], u_sin, k_cos, ALU.mult))
                    then(nc.vector.tensor_tensor(whole[:, 1], whole[:, 1], cross[:, :, :], ALU.add))
                    for out, n, signs in ((real, 0, (ALU.add, ALU.subtract)), (imag, 1, (ALU.subtract, ALU.add))):
                        for parity in range(2):
                            last = nc.vector.tensor_tensor(out[:, f, parity, :], whole[:, n, 0], whole[:, n, 1], signs[parity])
                    then(last)


def stage_transform_back(p, real, imag, magnitudes, uT, x0T, mix):
    nc = p.nc
    p.begin_stage()
    loaded = p.semaphores("t_loaded", 2)
    norms_ready = p.semaphore("b_norms_ready")
    used = p.semaphore("b_used")
    products_ready = p.semaphore("b_products_ready")
    biased = p.semaphore("b_biased")
    done = p.semaphore("b_done")
    stored = p.semaphore("b_stored")
    chain = p.semaphore("dve_chain")
    with ExitStack() as local:
        matrix = local.enter_context(nc.sbuf_tensor("b_matrix", [P, 2, 2, LAT], F32))
        norm = local.enter_context(nc.sbuf_tensor("b_norm", [P, 2, WT], F32))
        with nc.Block() as block:
            @block.sync
            def _(sp):
                for f in range(F_TILES):
                    if f >= 2:
                        sp.wait_ge(used, f - 1)
                    sp.dma_start(matrix[:, f % 2], p.dram["transform_back"][f]).then_inc(loaded[f % 2], 16)
                sp.wait_ge(done, WT)
                sp.dma_start(mix[WT:2 * WT, :, CTX:TOK].rearrange("k p t -> p k t"), uT[:, :, :]).then_inc(stored, 16)
                sp.wait_ge(stored, 16)

            @block.tensor
            def _(pe):
                for j in range(WT):
                    last = nc.tensor.matmul(p.psum[:, 0, j:j + 1], magnitudes[:, j * P:(j + 1) * P], p.const("ones")[:, 0:1],
                                            start=True, stop=True)
                last.then_inc(norms_ready, 1)
                pe.wait_ge(norms_ready, 2)
                for f in range(F_TILES):
                    pe.wait_ge(loaded[f % 2], 16 * (f // 2 + 1))
                    for j in range(WT):
                        for part, spectrum in ((0, real), (1, imag)):
                            for parity in range(2):
                                last = nc.tensor.matmul(p.psum[:, 2 * j + parity, :], spectrum[:, f, parity, j * P:(j + 1) * P],
                                                        matrix[:, f % 2, part, parity * BANK:(parity + 1) * BANK],
                                                        start=(f == 0 and part == 0), stop=(f == F_TILES - 1 and part == 1))
                        if f == F_TILES - 1:
                            last.then_inc(products_ready, 1)
                    if f < F_TILES - 1:
                        last.then_inc(used, 1)

            @block.vector
            def _(dve):
                dve.wait_ge(norms_ready, 1)
                nc.vector.tensor_scalar(norm[:, 0, :], p.psum[:, 0, 0:WT], float(LAT), None, ALU.mult).then_inc(chain, 1)
                dve.wait_ge(chain, 1)
                nc.vector.reciprocal(norm[:, 1, :], norm[:, 0, :]).then_inc(norms_ready, 1)
                for j in range(WT):
                    nc.vector.tensor_scalar(uT[:, j, :], uT[:, j, :], p.param("y_bias", j), None, ALU.mult).then_inc(biased, 1)
                dve.wait_ge(norms_ready, 2)
                for j in range(WT):
                    dve.wait_ge(products_ready, j + 1)
                    dve.wait_ge(biased, j + 1)
                    by_parity = uT[:, j, :].rearrange("p (n e) -> p e n", e=2)
                    nc.vector.scalar_tensor_tensor(by_parity, p.psum[:, 2 * j:2 * j + 2, :], norm[:, 1, j:j + 1], by_parity,
                                                   ALU.mult, ALU.add).then_inc(chain, 1)
                    dve.wait_ge(chain, j + 2)
                    nc.vector.tensor_tensor(uT[:, j, :], uT[:, j, :], x0T[:, j, :], ALU.mult).then_inc(done, 1)


def hyena_branch(p, arena, hT, mix):
    nc = p.nc
    w_in = p.dram["l1_w_in"]
    free = arena[:, KT * TOK:]
    lat = lambda i: free[:, i * WT * LAT:(i + 1) * WT * LAT].rearrange("p (j t) -> p j t", j=WT)
    with ExitStack() as outer:
        so = lambda name, shape: outer.enter_context(nc.sbuf_tensor(name, shape, F32))
        uT, x0T, zT = (so(f"y_{n}T", [P, WT, LAT]) for n in ("u", "x0", "z"))
        raw, x1T = lat(0), lat(1)
        for which, out in ((0, None), (1, x0T), (2, x1T)):
            jobs = [(5 * W + which * W, W, ACT.Copy, raw, False, LAT_GROUPS)]
            if which == 2:
                jobs.append((8 * W, W, ACT.Silu, zT, False, LAT_GROUPS))
            stage_project(p, f"y{which}", hT, w_in, jobs)
            stage_conv_product(p, raw, uT, out, which)
        sums, differences = so("y_sums", [P, KT, W]), so("y_differences", [P, KT, W])
        magnitudes = so("y_magnitudes", [P, W])
        stage_filters(p, sums, differences, magnitudes)
        u_tok = so("y_u_tok", [P, KT, W])
        stage_turn_u(p, uT, u_tok, x0T, zT)
        real, imag = (free[:, i * KT * W:(i + 1) * KT * W].rearrange("p (f e n) -> p f e n", f=F_TILES, e=2)
                      for i in range(2))
        spectrum = zT.rearrange("p j (a n) -> p (j a) n", a=2).rearrange("p (c f u) n -> p c f u n", c=2, f=2)
        whole = free[:, 2 * KT * W:2 * KT * W + 4 * W].rearrange("p (c f n) -> p c f n", c=2, f=2)
        stage_transform(p, u_tok, sums, differences, real, imag, spectrum, whole)
        stage_transform_back(p, real, imag, magnitudes, uT, x0T, mix)


def grid_columns(a):
    columns_per_tile = P // GRID_H

    def rows(t):
        first = (t - CTX_TILES) * columns_per_tile
        return a.rearrange("(r c) n -> c r n", c=GRID_W)[first:first + columns_per_tile]

    return rows


def build_program(nc, dram, out):
    with ExitStack() as ctx:
        p = Program(nc, ctx, dram)
        norm_scale, norm_shift = p.keep("norm_scale", [P, KT, 2]), p.keep("norm_shift", [P, KT, 2])
        arena = p.keep("arena", [P, 2 * KT * TOK])
        hT = arena[:, 0:KT * TOK].rearrange("p (k t) -> p k t", k=KT)
        free = arena[:, KT * TOK:]
        tile = lambda a: (lambda t: a[t * P:(t + 1) * P, :])
        mix, gate, x0, x1 = p.scratch["mix"], p.scratch["gate"], tile(dram["x_tok"]), tile(p.scratch["x1"])
        stage_copies(p, [(p.consts[:, :], dram["consts"]), (p.params[:, :], dram["params"])])
        stage_modulation(p, 0, norm_scale, norm_shift, gate[0])
        stage_norm_transpose(p, 0, x0, norm_scale, norm_shift, hT)
        mlstm_branch(p, free, hT, mix)
        rwkv_branch(p, arena, hT, mix, p.scratch["spill"])
        stage_output(p, 0, arena, mix, gate[0], x0, range(TILES), x1, p.x1_stored)
        stage_modulation(p, 1, norm_scale, norm_shift, gate[1])
        stage_norm_transpose(p, 1, x1, norm_scale, norm_shift, hT)
        hyena_branch(p, arena, hT, mix)
        hgrn_branch(p, arena, hT, mix)
        stage_output(p, 1, arena, mix, gate[1], grid_columns(p.scratch["x1"][CTX:TOK]), LAT_TILES, grid_columns(out),
                     p.out_stored, dram["final_gain"])


def host_arrays(inputs):
    a = {k: np.ascontiguousarray(v) for k, v in inputs.items()}
    f = np.float32

    def tiles(v):
        return v.reshape(-1, P).T

    def rows(v, n=P):
        out = np.zeros((P, 1), f)
        out[:v.size, 0] = v.reshape(-1)
        return out

    gate_b = a["l0_mlstm_gate_b"].reshape(2, 2, M_HEADS)
    gate_cols = np.zeros((D, 2, GATE_ROWS), f)
    gate_bias = np.zeros((2, P, 1), f)
    first = 5 * W
    for kind in range(2):
        for d in range(2):
            at = first + (d * 2 + kind) * M_HEADS
            gate_cols[:, kind, 32 * d:32 * d + M_HEADS] = a["l0_w_in"][:, at:at + M_HEADS]
            gate_bias[kind, 32 * d:32 * d + M_HEADS, 0] = gate_b[d, kind]
    parts = {
        "l0_norm_g": tiles(a["l0_norm_g"]), "l1_norm_g": tiles(a["l1_norm_g"]),
        "conv_w": tiles(a["l0_mlstm_conv_w"].reshape(-1)), "m_norm_g": tiles(a["l0_mlstm_norm_g"]),
        "r_mu": tiles(a["l0_rwkv_mu"].reshape(-1)), "r_w0": tiles(a["l0_rwkv_w0"].reshape(-1)),
        "r_a0": tiles(a["l0_rwkv_a0"].reshape(-1)), "r_k_k": tiles(a["l0_rwkv_k_k"]), "r_k_a": tiles(a["l0_rwkv_k_a"]),
        "r_r_k": tiles(a["l0_rwkv_r_k"].reshape(-1)), "r_ln_w": tiles(a["l0_rwkv_ln_w"]), "r_ln_b": tiles(a["l0_rwkv_ln_b"]),
        "lower": tiles(a["hgrn_lower_bounds"].reshape(-1)), "g_norm_g": tiles(a["l1_hgrn_norm_g"]),
        "short_w": tiles(a["l1_hyena_short_w"].reshape(-1)), "short_b": tiles(a["l1_hyena_short_b"]),
        "y_bias": tiles(a["l1_hyena_bias"]), "b1": rows(a["l1_hyena_b1"]), "b2": rows(a["l1_hyena_b2"]),
        "gate_b_i": gate_bias[0], "gate_b_f": gate_bias[1],
        "c": np.concatenate([a["c"].reshape(P, KT), a["c_ctx"].reshape(P, KT)], axis=1),
    }
    assert all(parts[n].shape[1] == PARAMS[n][1] for n in PARAMS)
    out = {
        "x_tok": np.concatenate([a["ctx"][0], a["x"][0]], axis=0),
        "params": np.ascontiguousarray(np.concatenate([parts[n] for n in PARAMS], axis=1)),
        "consts": const_common(), "const_mlstm": const_mlstm(), "const_rwkv": const_rwkv(),
        "w_up": a["l0_rwkv_w_up"].reshape(P, W), "a_up": a["l0_rwkv_a_up"].reshape(P, W),
        "gate_i": np.ascontiguousarray(gate_cols[:, 0]), "gate_f": np.ascontiguousarray(gate_cols[:, 1]),
        "mod_b0": np.stack([a["l0_mod_b"]] * 2), "mod_b1": np.stack([a["l1_mod_b"]] * 2),
    }
    out["const_hgrn"] = const_hgrn()
    out["final_gain"] = np.tile(a["final_norm_g"], (P, 1))
    out.update(const_hyena())
    for n in ("l1_hyena_w1", "l1_hyena_w2", "l1_hyena_w3", "l0_mod_w", "l1_mod_w", "l0_w_in", "l0_w_out", "l1_w_in", "l1_w_out"):
        out[n] = a[n]
    return out


def kernel(**inputs):
    import concourse.bacc as bacc
    from concourse.bass_utils import run_bass_kernel_spmd

    nc = bacc.Bacc("TRN2", target_bir_lowering=False, num_devices=1)
    arrays, dram = {}, {}
    for name, a in host_arrays(inputs).items():
        arrays[f"in_{name}"] = a
        dram[name] = nc.dram_tensor(f"in_{name}", a.shape, mybir.dt.from_np(a.dtype), kind="ExternalInput").ap()
    out = nc.dram_tensor("out_x", (LAT, D), F32, kind="ExternalOutput").ap()
    build_program(nc, dram, out)
    r = run_bass_kernel_spmd(nc, [arrays], core_ids=[0])
    return r.results[0]["out_x"].reshape(1, LAT, D)
```

```python
from contextlib import ExitStack

import numpy as np

import concourse.bass as bass
from concourse import mybir

F32 = mybir.dt.float32
U32 = mybir.dt.uint32
ALU = mybir.AluOpType
ACT = mybir.ActivationFunctionType
AX = mybir.AxisListType

P = 128
D = 1024
KT = D // P
CTX, LAT = 256, 1024
TOK = CTX + LAT
TILES = TOK // P
CTX_TILES = CTX // P
W = 512
WT = W // P
GRID_W = 64
GRID_H = LAT // GRID_W
EPS = 1e-6
GROUPS = ((0, 256), (256, 512), (768, 512))
BANK = 512

M_HEADS, M_CHUNK = 4, 128
R_HEADS, R_DIM, R_CHUNK = 8, 64, 64
R_LN_EPS = 64e-5
GATE_ROWS = 36


def columns(spec):
    at, where = 0, {}
    for name, width in spec:
        where[name] = (at, width)
        at += width
    return where, at


PARAMS, N_PARAMS = columns([
    ("l0_norm_g", 8), ("l1_norm_g", 8), ("conv_w", 24), ("m_norm_g", 4), ("r_mu", 12), ("r_w0", 8),
    ("r_a0", 8), ("r_k_k", 4), ("r_k_a", 4), ("r_r_k", 4), ("r_ln_w", 4), ("r_ln_b", 4), ("lower", 8),
    ("g_norm_g", 4), ("short_w", 36), ("short_b", 12), ("y_bias", 4), ("b1", 1), ("b2", 1),
    ("gate_b_i", 1), ("gate_b_f", 1), ("c", 16)])
CONSTS, N_CONSTS = columns([("ident", 128), ("ones", 128), ("head_ones", 128), ("row2", 256)])


def const_common():
    a = np.zeros((P, N_CONSTS), np.float32)
    a[:, 0:128] = np.eye(128)
    a[:, 128:256] = 1
    a[:, 256:384] = np.kron(np.eye(2), np.ones((64, 64)))
    a[0, 384:512] = 1
    a[1, 512:640] = 1
    return a


def const_mlstm():
    s, t = np.arange(P)[:, None], np.arange(P)[None]
    a = np.zeros((P, 2 * P + 8 * P), np.float32)
    a[:, 0:P] = np.where(s <= t, 0, -1e30)
    a[:, P:2 * P] = np.where(s >= t, 0, -1e30)
    for d in range(2):
        for h in range(M_HEADS):
            r = d * M_HEADS + h
            a[32 * d + h, 2 * P + r * P:2 * P + (r + 1) * P] = 1
    return a


class Program:

    SEMAPHORES_KEPT_FREE = 40

    def __init__(self, nc, ctx, dram):
        self.nc, self.ctx, self.dram = nc, ctx, dram
        scratch = lambda name, shape: nc.dram_tensor(f"scratch_{name}", shape, F32).ap()
        self.scratch = {"mix": scratch("mix", [KT, P, TOK]), "spill": scratch("spill", [4, WT, P, TOK]),
                        "gate": scratch("gate", [2, P, 2, D]), "x1": scratch("x1", [TOK, D]),
                        "z": scratch("z", [P, LAT // P, W])}
        self.stages, self.in_use, self.free = 0, [], 144
        self.x1_stored = [nc.alloc_semaphore(name=f"x1_stored{i}") for i in range(2)]
        self.out_stored = [nc.alloc_semaphore(name=f"out_stored{i}") for i in range(2)]
        self.psum = ctx.enter_context(nc.psum_tensor("psum", [P, 8, BANK], F32))
        self.consts = self.keep("consts", [P, N_CONSTS])
        self.params = self.keep("params", [P, N_PARAMS])

    def keep(self, name, shape, dtype=F32):
        return self.ctx.enter_context(self.nc.sbuf_tensor(name, shape, dtype))

    def begin_stage(self):
        self.stages += 1
        if self.free < self.SEMAPHORES_KEPT_FREE:
            self.nc.clear_and_free_semaphores(self.in_use)
            self.nc.all_engine_barrier()
            self.free += len(self.in_use)
            self.in_use = []

    def semaphore(self, name):
        self.in_use.append(self.nc.alloc_semaphore(name=f"{name}_{self.stages}"))
        self.free -= 1
        return self.in_use[-1]

    def semaphores(self, name, n):
        return [self.semaphore(f"{name}{i}") for i in range(n)]

    def const(self, name, rows=P):
        at, width = CONSTS[name]
        return self.consts[0:rows, at:at + width]

    def param(self, name, i, rows=P):
        at = PARAMS[name][0] + i
        return self.params[0:rows, at:at + 1]


def stage_copies(p, copies):
    p.begin_stage()
    copied = p.semaphore("copied")
    with p.nc.Block() as block:
        @block.sync
        def _(sp):
            for dst, of in copies:
                sp.dma_start(dst, of).then_inc(copied, 16)
            sp.wait_ge(copied, 16 * len(copies))


def stage_modulated_norm(p, layer, x, gate_dram, hT):
    nc = p.nc
    SLOTS = 3
    p.begin_stage()
    weight_loaded = p.semaphores("mod_weight_loaded", SLOTS)
    bias_loaded = p.semaphore("mod_bias_loaded")
    silu_ready = p.semaphore("mod_silu_ready")
    products_ready = p.semaphore("mod_products_ready")
    rows_ready = p.semaphore("mod_rows_ready")
    columns_ready = p.semaphore("mod_columns_ready")
    gates_ready = p.semaphore("mod_gates_ready")
    gates_spread = p.semaphore("mod_gates_spread")
    gate_stored = p.semaphore("mod_gate_stored")
    scale_ready = p.semaphore("mod_scale_ready")
    x_loaded = p.semaphores("norm_x_loaded", SLOTS)
    squares_ready = p.semaphore("norm_squares_ready")
    mean_ready = p.semaphore("norm_mean_ready")
    root_ready = p.semaphore("norm_root_ready")
    inverse_ready = p.semaphore("norm_inverse_ready")
    normed = p.semaphore("norm_normed")
    turned = p.semaphore("norm_turned")
    copied = p.semaphore("norm_copied")
    mod_w = p.dram[f"l{layer}_mod_w"].rearrange("(p k) n -> p k n", k=KT)
    at_c = PARAMS["c"][0]
    BY_VECTOR = 5
    regions = ((1, slice(0, CTX)), (0, slice(CTX, TOK)))
    with ExitStack() as local:
        sb = lambda name, shape: local.enter_context(nc.sbuf_tensor(f"{name}_{layer}", shape, F32))
        weight = sb("mod_weight", [P, SLOTS, 3 * D])
        silu = sb("mod_silu", [P, KT, 2])
        bias = sb("mod_bias", [2, 3 * D])
        rows = sb("mod_rows", [2, 3 * D])
        gate = sb("mod_gate", [P, 2, D])
        scale, shift = sb("mod_scale", [P, KT, 2]), sb("mod_shift", [P, KT, 2])
        xt = sb("norm_x", [P, SLOTS, D])
        junk = sb("norm_junk", [P, D])
        stat = sb("norm_stat", [P, TILES, 4])
        with nc.Block() as block:
            @block.sync
            def _(sp):
                sp.dma_start(bias[:, :], p.dram[f"mod_b{layer}"]).then_inc(bias_loaded, 16)
                for i in range(TILES):
                    if i >= SLOTS:
                        sp.wait_ge(turned, i - SLOTS + 1)
                    sp.dma_start(xt[:, i % SLOTS, :], x(i)).then_inc(x_loaded[i % SLOTS], 16)
                    if i < KT:
                        if i >= SLOTS:
                            sp.wait_ge(products_ready, i - SLOTS + 1)
                        sp.dma_start(weight[:, i % SLOTS, :], mod_w[:, i, :]).then_inc(weight_loaded[i % SLOTS], 16)
                sp.wait_ge(gates_spread, 4)
                sp.dma_start(gate_dram, gate[:, :, :]).then_inc(gate_stored, 16)
                sp.wait_ge(gate_stored, 16)

            @block.tensor
            def _(pe):
                pe.wait_ge(silu_ready, 1)
                for i in range(TILES):
                    if i < KT:
                        pe.wait_ge(weight_loaded[i % SLOTS], 16 * (i // SLOTS + 1))
                        for g in range(6):
                            last = nc.tensor.matmul(p.psum[0:2, g, :], silu[:, i, :],
                                                    weight[:, i % SLOTS, g * BANK:(g + 1) * BANK],
                                                    start=(i == 0), stop=(i == KT - 1))
                        last.then_inc(products_ready, 1)
                    pe.wait_ge(normed, i + 1)
                    if i:
                        pe.wait_ge(copied, i)
                    for k in range(KT):
                        last = nc.tensor.transpose(p.psum[:, 6 + k // 4, (k % 4) * P:(k % 4 + 1) * P],
                                                   xt[:, i % SLOTS, k * P:(k + 1) * P], p.const("ident"))
                    last.then_inc(turned, 1)
                pe.wait_ge(rows_ready, 1)
                pe.wait_ge(copied, TILES)
                for i in range(16):
                    last = nc.tensor.transpose(p.psum[:, 6, 2 * i:2 * i + 2], rows[:, i * P:(i + 1) * P],
                                               p.const("ident")[0:2, 0:2])
                last.then_inc(columns_ready, 1)
                for r in range(2):
                    for half in range(2):
                        nc.tensor.matmul(
                            p.psum[:, 2 * r + half, :], p.const("row2", 2)[:, r * P:(r + 1) * P],
                            rows[:, 2 * D + half * BANK:2 * D + (half + 1) * BANK], start=True, stop=True).then_inc(gates_ready, 1)

            @block.scalar
            def _(act):
                nc.scalar.activation(
                    silu[:, :, :], p.params[:, at_c:at_c + 16].rearrange("p (r k) -> p k r", r=2), ACT.Silu).then_inc(silu_ready, 1)
                for i in range(TILES):
                    act.wait_ge(x_loaded[i % SLOTS], 16 * (i // SLOTS + 1))
                    if i:
                        act.wait_ge(squares_ready, i)
                    nc.scalar.activation(junk[:, :], xt[:, i % SLOTS, :], ACT.Square,
                                         accum_out=stat[:, i, 0:1]).then_inc(squares_ready, 1)
                    act.wait_ge(mean_ready, i + 1)
                    nc.scalar.activation(stat[:, i, 2:3], stat[:, i, 1:2], ACT.Sqrt).then_inc(root_ready, 1)
                act.wait_ge(copied, TILES)
                act.wait_ge(scale_ready, 2)
                for k in range(BY_VECTOR, KT):
                    for r, at in regions:
                        nc.scalar.activation(hT[:, k, at], hT[:, k, at], ACT.Identity, scale=scale[:, k, r:r + 1],
                                             bias=shift[:, k, r:r + 1])
                for r in range(2):
                    for half in range(2):
                        act.wait_ge(gates_ready, 2 * r + half + 1)
                        nc.scalar.copy(gate[:, r, half * BANK:(half + 1) * BANK],
                                       p.psum[:, 2 * r + half, :]).then_inc(gates_spread, 1)

            @block.vector
            def _(dve):
                def norm(i):
                    dve.wait_ge(squares_ready, i + 1)
                    nc.vector.tensor_scalar(stat[:, i, 1:2], stat[:, i, 0:1], 1.0 / D, EPS,
                                            ALU.mult, ALU.add).then_inc(mean_ready, 1)
                    dve.wait_ge(root_ready, i + 1)
                    nc.vector.reciprocal(stat[:, i, 3:4], stat[:, i, 2:3]).then_inc(inverse_ready, 1)
                    dve.wait_ge(inverse_ready, i + 1)
                    nc.vector.tensor_scalar(xt[:, i % SLOTS, :], xt[:, i % SLOTS, :],
                                            stat[:, i, 3:4], None, ALU.mult).then_inc(normed, 1)

                norm(0)
                for i in range(TILES):
                    if i + 1 < TILES:
                        norm(i + 1)
                    dve.wait_ge(turned, i + 1)
                    for half in range(2):
                        src = p.psum[:, 6 + half, :].rearrange("p (k t) -> p k t", k=4)
                        k4 = slice(4 * half, 4 * half + 4)
                        if layer == 0 or i < CTX_TILES:
                            last = nc.vector.tensor_copy(hT[:, k4, i * P:(i + 1) * P], src)
                        else:
                            grid_rows = P // GRID_W
                            first = (i - CTX_TILES) * grid_rows
                            dst = hT[:, k4, CTX:TOK].rearrange("p k (c r) -> p k r c", r=GRID_H)[:, :, first:first + grid_rows, :]
                            last = nc.vector.tensor_copy(dst, src.rearrange("p k (r c) -> p k r c", r=grid_rows))
                    last.then_inc(copied, 1)
                dve.wait_ge(bias_loaded, 16)
                dve.wait_ge(products_ready, KT)
                nc.vector.tensor_tensor(
                    rows[:, :], p.psum[0:2, 0:6, :].rearrange("p g n -> p (g n)"), bias[:, :], ALU.add).then_inc(rows_ready, 1)
                dve.wait_ge(columns_ready, 1)
                cols = p.psum[:, 6, 0:32].rearrange("p (s k r) -> p s k r", s=2, r=2)
                gains = p.params[:, PARAMS[f"l{layer}_norm_g"][0]:][:, 0:KT]
                nc.vector.tensor_copy(shift[:, :, :], cols[:, 0])
                for r in range(2):
                    nc.vector.scalar_tensor_tensor(
                        scale[:, :, r], cols[:, 1, :, r], 1.0, gains, ALU.add, ALU.mult).then_inc(scale_ready, 1)
                dve.wait_ge(scale_ready, 2)
                for k in range(BY_VECTOR):
                    for r, at in regions:
                        nc.vector.tensor_scalar(hT[:, k, at], hT[:, k, at], scale[:, k, r:r + 1], shift[:, k, r:r + 1],
                                                ALU.mult, ALU.add)


def stage_project(p, name, hT, w_dram, jobs, finish={}, silu={}, store={}, loads=(), norm=None, save=None):
    nc = p.nc
    SLOTS = 2
    p.begin_stage()
    chain = p.semaphore("dve_chain")
    finished = p.semaphore("project_finished")
    silu_done = p.semaphore("project_silu_done")
    stored = p.semaphores("project_stored", WT)
    side_loaded = p.semaphore("project_side_loaded")
    saved = p.semaphore("project_saved")
    means_ready = p.semaphore("project_means_ready")
    roots_ready = p.semaphore("project_roots_ready")
    normed = p.semaphore("project_normed")
    gated = p.semaphore("project_gated")
    weight_loaded = p.semaphores("project_weight_loaded", SLOTS)
    products_ready = p.semaphore("project_products_ready")
    copied = p.semaphore("project_copied")
    w_view = w_dram.rearrange("(k p) n -> p k n", p=P)

    def units(job):
        col, width, func, dst, token_major, groups = job
        if token_major:
            first, end, offset = (*groups, 0)[:3]
            for i in range(first, end):
                yield P, width, (lambda k, w, i=i: (hT[:, k, i * P:(i + 1) * P], w[:, k, 0:width])), dst[:, i - offset]
        else:
            for j in range((width + P - 1) // P):
                m = min(P, width - j * P)
                for at, n, *to in groups:
                    to = to[0] if to else at
                    yield m, n, (lambda k, w, j=j, m=m, at=at, n=n: (w[:, k, j * P:j * P + m], hT[:, k, at:at + n])), \
                        (dst[:, j, to:to + n] if width > P else dst[0:m, to:to + n])

    ends = np.cumsum([sum(1 for _ in units(job)) for job in jobs]).tolist()
    units_by_tile = lambda b: len(jobs[b][5])
    first_unit = lambda b: ends[b - 1] if b else 0
    finished_by = lambda b, j: WT * sum(1 for other in finish if other < b) + j + 1
    stores_before = lambda b: sum(1 for other in store if other < b)

    def sharing(b):
        return max((other for other in finish if other < b and jobs[other][3] is jobs[b][3]), default=None)

    with ExitStack() as local:
        weight = local.enter_context(nc.sbuf_tensor(f"project_weight_{name}", [P, SLOTS, KT, W], F32))
        if norm is not None:
            assert not finish
            squares = local.enter_context(nc.sbuf_tensor(f"project_squares_{name}", [P, 2, W], F32))
            stat = local.enter_context(nc.sbuf_tensor(f"project_stat_{name}", [P, 4, TILES, WT], F32))
            by_head = lambda a: a.rearrange("p (h n) -> p h n", h=WT)
        with nc.Block() as block:
            @block.sync
            def _(sp):
                for b, (col, width, *_) in enumerate(jobs):
                    if b >= SLOTS:
                        sp.wait_ge(products_ready, ends[b - SLOTS])
                    src = (p.dram[col].rearrange("(k p) n -> p k n", p=P) if isinstance(col, str)
                           else w_view[:, :, col:col + width])
                    sp.dma_start(weight[:, b % SLOTS, :, 0:width], src).then_inc(weight_loaded[b % SLOTS], 16)

            @block.tensor
            def _(pe):
                u = 0
                for b, job in enumerate(jobs):
                    pe.wait_ge(weight_loaded[b % SLOTS], 16 * (b // SLOTS + 1))
                    for rows, n, operands, _ in units(job):
                        if u >= 8:
                            pe.wait_ge(copied, u - 7)
                        for k in range(KT):
                            lhsT, rhs = operands(k, weight[:, b % SLOTS])
                            last = nc.tensor.matmul(p.psum[0:rows, u % 8, 0:n], lhsT, rhs,
                                                    start=(k == 0), stop=(k == KT - 1))
                        last.then_inc(products_ready, 1)
                        u += 1

            @block.scalar
            def _(act):
                if norm is not None:
                    act.wait_ge(means_ready, 1)
                    nc.scalar.activation(stat[:, 2], stat[:, 1], ACT.Sqrt).then_inc(roots_ready, 1)
                u = silus = 0
                for b, job in enumerate(jobs):
                    for rows, n, _, dst in units(job):
                        j, in_tile = divmod(u - first_unit(b), units_by_tile(b))
                        if in_tile == 0 and sharing(b) is not None:
                            act.wait_ge(finished, finished_by(sharing(b), j))
                        act.wait_ge(products_ready, u + 1)
                        src = p.psum[0:rows, u % 8, 0:n]
                        if len(dst.shape) == 3:
                            src = src.rearrange("p (a b) -> p a b", a=dst.shape[1])
                        nc.scalar.activation(dst, src, job[2]).then_inc(copied, 1)
                        u += 1
                        if b in silu and in_tile == units_by_tile(b) - 1:
                            out, factor = silu[b]
                            act.wait_ge(finished, finished_by(b, j))
                            nc.scalar.activation(out[:, j, :], out[:, j, :], ACT.Silu).then_inc(silu_done, 1)
                            silus += 1
                            if factor != 1:
                                act.wait_ge(silu_done, silus)
                                nc.scalar.mul(out[:, j, :], out[:, j, :], factor)

            @block.vector
            def _(dve):
                made = [0]

                def then(instruction):
                    made[0] += 1
                    instruction.then_inc(chain, 1)
                    dve.wait_ge(chain, made[0])

                if norm is not None:
                    for t in range(TILES):
                        then(nc.vector.tensor_tensor(squares[:, t % 2, :], norm[:, t, :], norm[:, t, :], ALU.mult))
                        then(nc.vector.tensor_reduce(stat[:, 0, t, :], by_head(squares[:, t % 2, :]), AX.X, ALU.add))
                    nc.vector.tensor_scalar(stat[:, 1], stat[:, 0], 1.0 / P, EPS, ALU.mult, ALU.add).then_inc(means_ready, 1)
                    dve.wait_ge(roots_ready, 1)
                    then(nc.vector.reciprocal(stat[:, 3], stat[:, 2]))
                    for t in range(TILES):
                        wide = stat[:, 3, t, :].unsqueeze(2).broadcast_to([P, WT, P])
                        nc.vector.tensor_tensor(by_head(norm[:, t, :]), by_head(norm[:, t, :]), wide, ALU.mult).then_inc(normed, 1)
                for b in sorted(finish):
                    for j in range(WT):
                        dve.wait_ge(copied, first_unit(b) + units_by_tile(b) * (j + 1))
                        if b in store and stores_before(b):
                            dve.wait_ge(stored[j], 16 * stores_before(b))
                        finish[b](then, j).then_inc(finished, 1)

            @block.gpsimd
            def _(pool):
                for dst, of in loads:
                    nc.gpsimd.dma_start(dst, of).then_inc(side_loaded, 16)
                if norm is not None:
                    for b in range(2):
                        for t in range(TILES):
                            pool.wait_ge(copied, first_unit(b) + t + 1)
                            if b == 0:
                                pool.wait_ge(normed, t + 1)
                            else:
                                pool.wait_ge(gated, t + 1)
                            nc.gpsimd.tensor_tensor(norm[:, t, :], norm[:, t, :], jobs[b][3][:, t, :], ALU.mult).then_inc(gated, 1)
                for b in sorted(store):
                    for j in range(WT):
                        if b in finish:
                            pool.wait_ge(finished, finished_by(b, j))
                        else:
                            pool.wait_ge(copied, first_unit(b) + units_by_tile(b) * (j + 1))
                        nc.gpsimd.dma_start(*store[b](j)).then_inc(stored[j], 16)
                if save is not None:
                    b, saved_dram = save
                    for i in range(ends[b] - first_unit(b)):
                        pool.wait_ge(copied, first_unit(b) + i + 1)
                        nc.gpsimd.dma_start(saved_dram[:, i, :], jobs[b][3][:, i, :]).then_inc(saved, 16)
                    pool.wait_ge(saved, 16 * (ends[b] - first_unit(b)))
                if loads:
                    pool.wait_ge(side_loaded, 16 * len(loads))
                if store:
                    for j in range(WT):
                        pool.wait_ge(stored[j], 16 * len(store))


def conv3(nc, then, dst, src, taps):
    before, here, after = taps
    then(nc.vector.tensor_scalar(dst, src, here, None, ALU.mult))
    for a, n in ((0, CTX), (CTX, LAT)):
        out = dst[:, a + 1:a + n]
        then(nc.vector.scalar_tensor_tensor(out, src[:, a:a + n - 1], before, out, ALU.mult, ALU.add))
    out = dst[:, 0:CTX - 1]
    then(nc.vector.scalar_tensor_tensor(out, src[:, 1:CTX], after, out, ALU.mult, ALU.add))
    out = dst[:, CTX:TOK - 1]
    return nc.vector.scalar_tensor_tensor(out, src[:, CTX + 1:TOK], after, out, ALU.mult, ALU.add)


def stage_gate_rows(p, gate_i, gate_f, rows, carry):
    nc = p.nc
    p.begin_stage()
    chain = p.semaphore("dve_chain")
    biased = p.semaphore("gate_biased")
    soft = p.semaphore("gate_soft")
    logs_ready = p.semaphore("gate_logs_ready")
    exps_ready = p.semaphore("gate_exps_ready")
    R = GATE_ROWS
    with ExitStack() as local:
        sb = lambda name, shape: local.enter_context(nc.sbuf_tensor(name, shape, F32))
        soft_t = sb("gate_soft_t", [R, TOK])
        decay = sb("gate_decay", [R, TOK])
        peak = sb("gate_peak", [R, TOK])
        carry_on = sb("gate_carry_on", [R, TOK])
        small = sb("gate_small", [R, 3, TILES])
        chunked = lambda a: a.rearrange("r (c t) -> r c t", t=M_CHUNK)
        with nc.Block() as block:
            @block.scalar
            def _(act):
                act.wait_ge(biased, 1)
                nc.scalar.activation(soft_t[:, :], gate_f[:, :], ACT.Abs).then_inc(soft, 1)
                act.wait_ge(soft, 1)
                nc.scalar.activation(soft_t[:, :], soft_t[:, :], ACT.Exp, scale=-1.0).then_inc(soft, 1)
                act.wait_ge(soft, 2)
                nc.scalar.activation(soft_t[:, :], soft_t[:, :], ACT.Ln, bias=1.0).then_inc(soft, 1)
                act.wait_ge(logs_ready, 1)
                for name in ("query_scale", "floor", "key_scale"):
                    nc.scalar.activation(rows[name], rows[name], ACT.Exp,
                                                         scale=-1.0 if name == "floor" else 1.0).then_inc(exps_ready, 1)
                nc.scalar.activation(carry[:, :], carry[:, :], ACT.Exp).then_inc(exps_ready, 1)

            @block.vector
            def _(dve):
                made = [0]

                def then(instruction):
                    made[0] += 1
                    instruction.then_inc(chain, 1)
                    dve.wait_ge(chain, made[0])

                then(nc.vector.memset(carry_on[:, :], 1.0))
                then(nc.vector.memset(chunked(carry_on[0:32, :])[:, :, 0], 0.0))
                then(nc.vector.memset(chunked(carry_on[32:R, :])[:, :, M_CHUNK - 1], 0.0))
                then(nc.vector.tensor_scalar(gate_i[:, :], gate_i[:, :], p.param("gate_b_i", 0, R), None, ALU.add))
                nc.vector.tensor_scalar(gate_f[:, :], gate_f[:, :], p.param("gate_b_f", 0, R), None, ALU.add).then_inc(biased, 1)
                dve.wait_ge(biased, 1)
                dve.wait_ge(soft, 1)
                then(nc.vector.tensor_scalar(gate_f[:, :], gate_f[:, :], 0.0, None, ALU.min))
                dve.wait_ge(soft, 3)
                then(nc.vector.tensor_tensor(gate_f[:, :], gate_f[:, :], soft_t[:, :], ALU.subtract))
                fwd, bwd = slice(0, 32), slice(32, R)
                then(nc.vector.tensor_tensor_scan(decay[fwd, :], carry_on[fwd, :], gate_f[fwd, :], 0.0, ALU.mult, ALU.add))
                then(nc.vector.tensor_tensor_scan(decay[bwd, ::-1], carry_on[bwd, ::-1], gate_f[bwd, ::-1], 0.0, ALU.mult, ALU.add))
                then(nc.vector.tensor_tensor_scan(peak[fwd, :], gate_f[fwd, :], gate_i[fwd, :], 0.0, ALU.add, ALU.max))
                then(nc.vector.tensor_tensor_scan(peak[bwd, 0:CTX][:, ::-1], gate_f[bwd, 0:CTX][:, ::-1],
                                                  gate_i[bwd, 0:CTX][:, ::-1], 0.0, ALU.add, ALU.max))
                then(nc.vector.tensor_tensor_scan(peak[bwd, CTX:TOK][:, ::-1], gate_f[bwd, CTX:TOK][:, ::-1],
                                                  gate_i[bwd, CTX:TOK][:, ::-1], peak[bwd, 0:1], ALU.add, ALU.max))
                before, at_end, whole = small[:, 0, :], small[:, 1, :], small[:, 2, :]
                then(nc.vector.memset(small[:, :, :], 0.0))
                peaks, decays = chunked(peak[:, :]), chunked(decay[:, :])
                then(nc.vector.tensor_copy(before[fwd, 1:TILES], peaks[fwd, 0:TILES - 1, M_CHUNK - 1]))
                then(nc.vector.tensor_copy(before[bwd, 0:1], peaks[bwd, 1:2, 0]))
                then(nc.vector.tensor_copy(before[bwd, CTX_TILES:TILES - 1], peaks[bwd, CTX_TILES + 1:TILES, 0]))
                then(nc.vector.tensor_copy(before[bwd, TILES - 1:TILES], peaks[bwd, 0:1, 0]))
                for rws, at in ((fwd, M_CHUNK - 1), (bwd, 0)):
                    then(nc.vector.tensor_copy(at_end[rws, :], peaks[rws, :, at]))
                    then(nc.vector.tensor_copy(whole[rws, :], decays[rws, :, at]))
                wide = lambda a: a.unsqueeze(2).broadcast_to([R, TILES, M_CHUNK])
                then(nc.vector.tensor_tensor(rows["query_log"], decay[:, :], peak[:, :], ALU.subtract))
                then(nc.vector.tensor_tensor(rows["key_log"], gate_i[:, :], decay[:, :], ALU.subtract))
                then(nc.vector.tensor_copy(rows["floor"], peak[:, :]))
                then(nc.vector.tensor_tensor(chunked(rows["query_scale"]), chunked(rows["query_log"]), wide(before), ALU.add))
                then(nc.vector.tensor_tensor(whole, whole, at_end, ALU.subtract))
                then(nc.vector.tensor_tensor(chunked(rows["key_scale"]), chunked(rows["key_log"]), wide(whole), ALU.add))
                nc.vector.tensor_tensor(carry[:, :], whole, before, ALU.add).then_inc(logs_ready, 1)


def stage_gate_columns(p, rows, carry, sel, cols, carry_wide):
    nc = p.nc
    R = GATE_ROWS
    p.begin_stage()
    turned = p.semaphore("gate_turned")
    copied = p.semaphore("gate_columns_copied")
    kinds = ("key_log", "query_scale", "floor", "key_scale")
    with nc.Block() as block:
        @block.tensor
        def _(pe):
            for n, name in enumerate(kinds):
                for c in range(TILES):
                    last = nc.tensor.transpose(p.psum[:, n, c * R:(c + 1) * R], rows[name][:, c * P:(c + 1) * P],
                                               p.const("ident")[0:R, 0:R])
                last.then_inc(turned, 1)
            for r in range(2 * M_HEADS):
                last = nc.tensor.matmul(p.psum[:, 4, r * TILES:(r + 1) * TILES], sel[0:R, r * P:(r + 1) * P],
                                        carry[:, :], start=True, stop=True)
            last.then_inc(turned, 1)

        @block.vector
        def _(dve):
            for n in range(4):
                dve.wait_ge(turned, n + 1)
                nc.vector.tensor_copy(cols[:, n], p.psum[:, n, 0:TILES * R].rearrange("p (c r) -> p c r", r=R)).then_inc(copied, 1)
            dve.wait_ge(turned, 5)
            nc.vector.tensor_copy(carry_wide[:, :, :],
                                              p.psum[:, 4, 0:8 * TILES].rearrange("p (r c) -> p r c", c=TILES)).then_inc(copied, 1)


def stage_turn(p, kT, k_tok):
    nc = p.nc
    p.begin_stage()
    turned = p.semaphore("turn_turned")
    copied = p.semaphore("turn_copied")
    with nc.Block() as block:
        @block.tensor
        def _(pe):
            for i in range(TILES):
                if i >= 8:
                    pe.wait_ge(copied, i - 7)
                for h in range(WT):
                    last = nc.tensor.transpose(p.psum[:, i % 8, h * P:(h + 1) * P], kT[:, h, i * P:(i + 1) * P],
                                               p.const("ident"))
                last.then_inc(turned, 1)

        @block.scalar
        def _(act):
            for i in range(TILES):
                act.wait_ge(turned, i + 1)
                nc.scalar.copy(k_tok[:, i, :, :], p.psum[:, i % 8, :].rearrange("p (h n) -> p h n", h=WT)).then_inc(copied, 1)


def scan_order(direction, chunks, ctx_chunks):
    if direction == 0:
        return list(range(chunks))
    return list(range(ctx_chunks))[::-1] + list(range(ctx_chunks, chunks))[::-1]


def stage_mlstm_scan(p, qT, kT, k_tok, v_aug, rows, cols, carry_wide, sel, caps, y):
    nc = p.nc
    H, C = M_HEADS, M_CHUNK
    names = ("weights_logs_ready", "scores_ready", "capped", "weights_exp", "weighted", "inside_ready",
             "across_ready", "keys_scaled", "update_ready", "state_decayed", "state_ready", "y_ready")
    p.begin_stage()
    sig = {n: p.semaphore("m_" + n) for n in names}
    chain = p.semaphore("dve_chain")
    cleared = p.semaphore("m_cleared")
    steps = [(d, c) for pair in zip(scan_order(0, TILES, CTX_TILES), scan_order(1, TILES, CTX_TILES))
             for d, c in enumerate(pair)]
    N = len(steps)
    logs, scores, inside, across, update = 0, 1, (2, 4), (4, 6), (6, 8)
    two = lambda banks: p.psum[:, banks[0]:banks[1], 0:2 * (P + 1)].rearrange("p b (h n) -> p b h n", h=2)
    col = lambda n, c, d: cols[:, n, c, 32 * d:32 * d + H]
    with ExitStack() as local:
        sb = lambda name, shape: local.enter_context(nc.sbuf_tensor("m_" + name, shape, F32))
        state = sb("state", [P, 2, H, P + 1])
        decayed = sb("decayed", [P, 2, H, P + 1])
        capped = sb("capped", [P, 2, H, C])
        weight = sb("weight", [P, 2, H, C])
        keys = sb("keys", [P, 2, H, P])
        num = sb("num", [P, 2, H, P + 1])
        den = sb("den", [P, 2, 3, H])
        with nc.Block() as block:
            @block.tensor
            def _(pe):
                def spread_logs(i):
                    d, c = steps[i]
                    if i:
                        pe.wait_ge(sig["capped"], H * i)
                    for h in range(H):
                        r = d * H + h
                        last = nc.tensor.matmul(p.psum[:, logs, h * C:(h + 1) * C],
                                                sel[0:GATE_ROWS, r * P:(r + 1) * P], rows["query_log"][:, c * C:(c + 1) * C],
                                                start=True, stop=True)
                    last.then_inc(sig["weights_logs_ready"], 1)

                pe.wait_ge(cleared, 1)
                spread_logs(0)
                for i, (d, c) in enumerate(steps):
                    tokens = slice(c * C, (c + 1) * C)
                    if i:
                        pe.wait_ge(sig["weighted"], i)
                    for h in range(H):
                        last = nc.tensor.matmul(p.psum[:, scores, h * C:(h + 1) * C], kT[:, h, tokens],
                                                qT[:, h, tokens], start=True, stop=True)
                    last.then_inc(sig["scores_ready"], 1)
                    if i + 1 < len(steps):
                        spread_logs(i + 1)
                    if i >= 2:
                        pe.wait_ge(sig["state_ready"], i - 1)
                    if i:
                        pe.wait_ge(sig["y_ready"], i)
                    for h in range(H):
                        last = nc.tensor.matmul(p.psum[:, across[0] + h // 2, (h % 2) * (P + 1):(h % 2 + 1) * (P + 1)],
                                                qT[:, h, tokens], state[:, d, h, :], start=True, stop=True)
                    last.then_inc(sig["across_ready"], 1)
                    pe.wait_ge(sig["weighted"], i + 1)
                    for h in range(H):
                        last = nc.tensor.matmul(p.psum[:, inside[0] + h // 2, (h % 2) * (P + 1):(h % 2 + 1) * (P + 1)],
                                                weight[:, i % 2, h, :], v_aug[:, c, h, :], start=True, stop=True)
                    last.then_inc(sig["inside_ready"], 1)
                    pe.wait_ge(sig["keys_scaled"], i + 1)
                    if i:
                        pe.wait_ge(sig["state_ready"], i)
                    for h in range(H):
                        last = nc.tensor.matmul(p.psum[:, update[0] + h // 2, (h % 2) * (P + 1):(h % 2 + 1) * (P + 1)],
                                                keys[:, i % 2, h, :], v_aug[:, c, h, :], start=True, stop=True)
                    last.then_inc(sig["update_ready"], 1)

            @block.scalar
            def _(act):
                for i, (d, c) in enumerate(steps):
                    act.wait_ge(sig["capped"], H * (i + 1))
                    if i >= 2:
                        act.wait_ge(sig["inside_ready"], i - 1)
                    nc.scalar.activation(weight[:, i % 2], capped[:, i % 2], ACT.Exp).then_inc(sig["weights_exp"], 1)

            @block.gpsimd
            def _(pool):
                for i, (d, c) in enumerate(steps):
                    if i >= 2:
                        pool.wait_ge(sig["update_ready"], i - 1)
                    nc.gpsimd.tensor_tensor(
                        keys[:, i % 2], k_tok[:, c], col(3, c, d).unsqueeze(2).broadcast_to([P, H, P]), ALU.mult).then_inc(sig["keys_scaled"], 1)
                    if i == 0:
                        pool.wait_ge(cleared, 1)
                    if i >= 2:
                        pool.wait_ge(sig["state_ready"], i - 1)
                    nc.gpsimd.tensor_tensor(
                        decayed[:, d], state[:, d],
                        carry_wide[:, d * H:(d + 1) * H, c].unsqueeze(2).broadcast_to([P, H, P + 1]), ALU.mult).then_inc(sig["state_decayed"], 1)

            @block.vector
            def _(dve):
                made = [0]

                def then(instruction):
                    made[0] += 1
                    instruction.then_inc(chain, 1)
                    dve.wait_ge(chain, made[0])

                def cap_logs(i):
                    d, c = steps[i]
                    dve.wait_ge(sig["weights_logs_ready"], i + 1)
                    if i >= 2:
                        dve.wait_ge(sig["weights_exp"], i - 1)
                    for h in range(H):
                        nc.vector.scalar_tensor_tensor(
                            capped[:, i % 2, h, :], p.psum[:, logs, h * C:(h + 1) * C], cols[:, 0, c, 32 * d + h:32 * d + h + 1],
                            caps[:, d * P:(d + 1) * P], ALU.add, ALU.min).then_inc(sig["capped"], 1)

                nc.vector.memset(state[:, :, :, :], 0.0).then_inc(cleared, 1)
                cap_logs(0)
                for i, (d, c) in enumerate(steps):
                    b = i % 2
                    if i + 1 < len(steps):
                        cap_logs(i + 1)
                    dve.wait_ge(sig["scores_ready"], i + 1)
                    dve.wait_ge(sig["weights_exp"], i + 1)
                    nc.vector.tensor_tensor(
                        weight[:, b], weight[:, b], p.psum[:, scores, :].rearrange("p (h n) -> p h n", h=H), ALU.mult).then_inc(sig["weighted"], 1)
                    four = num[:, b].rearrange("p (b h) n -> p b h n", b=2)
                    dve.wait_ge(sig["across_ready"], i + 1)
                    then(nc.vector.tensor_tensor(
                        four, two(across), col(1, c, d).rearrange("p (b h) -> p b h", b=2).unsqueeze(3).broadcast_to([P, 2, 2, P + 1]), ALU.mult))
                    dve.wait_ge(sig["inside_ready"], i + 1)
                    then(nc.vector.tensor_tensor(four, four, two(inside), ALU.add))
                    then(nc.vector.tensor_scalar(den[:, b, 0, :], num[:, b, :, P], -1.0, None, ALU.mult))
                    then(nc.vector.tensor_tensor(den[:, b, 0, :], den[:, b, 0, :], num[:, b, :, P], ALU.max))
                    then(nc.vector.tensor_tensor(den[:, b, 1, :], den[:, b, 0, :], col(2, c, d), ALU.max))
                    then(nc.vector.reciprocal(den[:, b, 2, :], den[:, b, 1, :]))
                    inv = den[:, b, 2, :].unsqueeze(2).broadcast_to([P, H, P])
                    y_c = y[:, c, :].rearrange("p (h n) -> p h n", h=H)
                    first = all(cc != c for _, cc in steps[:i])
                    if first:
                        nc.vector.tensor_tensor(y_c, num[:, b, :, 0:P], inv, ALU.mult).then_inc(sig["y_ready"], 1)
                    else:
                        then(nc.vector.tensor_tensor(num[:, b, :, 0:P], num[:, b, :, 0:P], inv, ALU.mult))
                        nc.vector.tensor_tensor(y_c, y_c, num[:, b, :, 0:P], ALU.add).then_inc(sig["y_ready"], 1)
                    dve.wait_ge(sig["update_ready"], i + 1)
                    dve.wait_ge(sig["state_decayed"], i + 1)
                    nc.vector.tensor_tensor(
                        state[:, d].rearrange("p (b h) n -> p b h n", b=2),
                        decayed[:, d].rearrange("p (b h) n -> p b h n", b=2), two(update), ALU.add).then_inc(sig["state_ready"], 1)


def stage_heads_rmsnorm(p, y, gate, gate_dram, tiles, heads_eps):
    nc = p.nc
    H = WT
    p.begin_stage()
    squares = p.semaphore("hn_squares")
    sums = p.semaphore("hn_sums")
    roots = p.semaphore("hn_roots")
    done = p.semaphore("hn_done")
    gate_loaded = p.semaphore("hn_gate_loaded")
    with ExitStack() as local:
        sq = local.enter_context(nc.sbuf_tensor(f"hn_squares_t{len(tiles)}", [P, 2, W], F32))
        st = local.enter_context(nc.sbuf_tensor(f"hn_stat{len(tiles)}", [P, TILES, 3, H], F32))
        with nc.Block() as block:
            @block.sync
            def _(sp):
                sp.dma_start(gate, gate_dram).then_inc(gate_loaded, 16)

            @block.scalar
            def _(act):
                for i, t in enumerate(tiles):
                    if i >= 2:
                        act.wait_ge(sums, 2 * i - 2)
                    nc.scalar.activation(sq[:, i % 2, :], y[:, t, :], ACT.Square).then_inc(squares, 1)
                for i, t in enumerate(tiles):
                    act.wait_ge(sums, 2 * i + 2)
                    nc.scalar.activation(st[:, i, 1, :], st[:, i, 1, :], ACT.Sqrt).then_inc(roots, 1)

            @block.gpsimd
            def _(pool):
                pool.wait_ge(gate_loaded, 16)
                for i, t in enumerate(tiles):
                    pool.wait_ge(squares, i + 1)
                    nc.gpsimd.tensor_tensor(y[:, t, :], y[:, t, :], gate[:, t, :], ALU.mult).then_inc(done, 1)

            @block.vector
            def _(dve):
                for i, t in enumerate(tiles):
                    dve.wait_ge(squares, i + 1)
                    nc.vector.tensor_reduce(st[:, i, 0, :], sq[:, i % 2, :].rearrange("p (h n) -> p h n", h=H), AX.X, ALU.add).then_inc(sums, 1)
                    dve.wait_ge(sums, 2 * i + 1)
                    nc.vector.tensor_scalar(st[:, i, 1, :], st[:, i, 0, :], 1.0 / P, heads_eps, ALU.mult, ALU.add).then_inc(sums, 1)
                for i, t in enumerate(tiles):
                    dve.wait_ge(roots, i + 1)
                    nc.vector.reciprocal(st[:, i, 2, :], st[:, i, 1, :]).then_inc(sums, 1)
                    dve.wait_ge(sums, 2 * len(tiles) + 2 * i + 1)
                    dve.wait_ge(done, i + 1)
                    yt = y[:, t, :].rearrange("p (h n) -> p h n", h=H)
                    nc.vector.tensor_tensor(yt, yt, st[:, i, 2, :].unsqueeze(2).broadcast_to([P, H, P]), ALU.mult).then_inc(sums, 1)


def stage_turn_back(p, y, tiles, scale, shift, factor, mix, first, offset=0):
    nc = p.nc
    p.begin_stage()
    turned = p.semaphore("back_turned")
    copied = p.semaphore("back_copied")
    multiplied = p.semaphore("back_multiplied")
    stored = p.semaphore("back_stored")
    with ExitStack() as local:
        mixT = local.enter_context(nc.sbuf_tensor(f"back_mixT{first}_{len(tiles)}", [P, WT, TOK], F32))
        with nc.Block() as block:
            @block.tensor
            def _(pe):
                for i, t in enumerate(tiles):
                    if i >= 8:
                        pe.wait_ge(copied, WT * (i - 7))
                    for h in range(WT):
                        last = nc.tensor.transpose(p.psum[:, i % 8, h * P:(h + 1) * P], y[:, t, h * P:(h + 1) * P],
                                                   p.const("ident"))
                    last.then_inc(turned, 1)

            @block.scalar
            def _(act):
                for i, t in enumerate(tiles):
                    act.wait_ge(turned, i + 1)
                    for h in range(WT):
                        nc.scalar.activation(mixT[:, h, offset + t * P:offset + (t + 1) * P],
                                                         p.psum[:, i % 8, h * P:(h + 1) * P], ACT.Identity,
                                                         scale=scale(h), bias=shift(h) if shift else 0.0).then_inc(copied, 1)

            @block.gpsimd
            def _(pool):
                if factor is not None:
                    for i, t in enumerate(tiles):
                        pool.wait_ge(copied, WT * (i + 1))
                        out = mixT[:, :, t * P:(t + 1) * P]
                        nc.gpsimd.tensor_tensor(out, out, factor[:, :, t * P:(t + 1) * P], ALU.mult).then_inc(multiplied, 1)

            @block.sync
            def _(sp):
                sp.wait_ge(copied, WT * len(tiles))
                if factor is not None:
                    sp.wait_ge(multiplied, len(tiles))
                at = offset + tiles[0] * P
                sp.dma_start(mix[first:first + WT, :, at:TOK].rearrange("k p t -> p k t"), mixT[:, :, at:TOK]).then_inc(stored, 16)
                sp.wait_ge(stored, 16)


def mlstm_branch(p, free, hT, mix):
    nc = p.nc
    w_in = p.dram["l0_w_in"]
    with ExitStack() as outer:
        so = lambda name, shape: outer.enter_context(nc.sbuf_tensor(name, shape, F32))
        y = so("m_y", [P, TILES, W])
        with ExitStack() as inner:
            si = lambda name, shape: inner.enter_context(nc.sbuf_tensor(name, shape, F32))
            qT, kT = (free[:, i * WT * TOK:(i + 1) * WT * TOK].rearrange("p (j t) -> p j t", j=WT) for i in range(2))
            v_aug = si("m_v", [P, TILES, M_HEADS, P + 1])
            query_log = si("m_query_log", [GATE_ROWS, TOK])
            masks = si("m_masks", [P, 2 * P + 8 * P])
            cols = si("m_cols", [P, 4, TILES, GATE_ROWS])
            carry_wide = si("m_carry_wide", [P, 2 * M_HEADS, TILES])
            caps, sel = masks[:, 0:2 * P], masks[:, 2 * P:]
            with ExitStack() as gates:
                sg = lambda name, shape: gates.enter_context(nc.sbuf_tensor(name, shape, F32))
                gate_rows = sg("m_gates", [GATE_ROWS, 2, TOK])
                with ExitStack() as raws:
                    raw = raws.enter_context(nc.sbuf_tensor("m_raw", [P, WT, TOK], F32))
                    conv = lambda out, which: (lambda then, j: conv3(
                        nc, then, out[:, j, :], raw[:, j, :], [p.param("conv_w", 8 * tap + WT * which + j) for tap in range(3)]))
                    stage_project(p, "m", hT, w_in, [
                        (0, W, ACT.Copy, raw, False, GROUPS), (W, W, ACT.Copy, raw, False, GROUPS),
                        (2 * W, W, ACT.Copy, v_aug[:, :, :, 0:P], True, (0, TILES)),
                        ("gate_i", GATE_ROWS, ACT.Copy, gate_rows[:, 0], False, GROUPS),
                        ("gate_f", GATE_ROWS, ACT.Copy, gate_rows[:, 1], False, GROUPS)],
                        finish={0: conv(qT, 0), 1: conv(kT, 1)}, silu={0: (qT, 1), 1: (kT, float(P) ** -0.5)},
                        loads=[(masks[:, :], p.dram["const_mlstm"])])
                with nc.Block() as block:
                    @block.gpsimd
                    def _(pool):
                        nc.gpsimd.memset(v_aug[:, :, :, P:P + 1], 1.0)
                carry = sg("m_carry", [GATE_ROWS, TILES])
                row_buf = sg("m_rows", [GATE_ROWS, 4, TOK])
                rows = {n: row_buf[:, i, :] for i, n in enumerate(("key_log", "query_scale", "floor", "key_scale"))}
                rows["query_log"] = query_log[:, :]
                stage_gate_rows(p, gate_rows[:, 0], gate_rows[:, 1], rows, carry)
                stage_gate_columns(p, rows, carry, sel, cols, carry_wide)
            k_tok = si("m_k_tok", [P, TILES, M_HEADS, P])
            stage_turn(p, kT, k_tok)
            stage_mlstm_scan(p, qT, kT, k_tok, v_aug, rows, cols, carry_wide, sel, caps, y)
        gate_o, gate_z = so("m_o", [P, TILES, W]), so("m_z", [P, TILES, W])
        stage_project(p, "mo", hT, w_in, [
            (3 * W, W, ACT.Sigmoid, gate_o, True, (0, TILES)), (4 * W, W, ACT.Silu, gate_z, True, (0, TILES))], norm=y)
        stage_turn_back(p, y, range(TILES), lambda h: p.param("m_norm_g", h), None, None, mix, 0)


R_CHUNKS = TOK // R_CHUNK
R_PAIRS = R_HEADS // 2
R_LEVELS = 6
M_IN = 5 * W + 4 * M_HEADS


R_MASKS = 2 * 2 * R_CHUNK + R_CHUNK + R_LEVELS * 2 * P + 2 * P


def const_rwkv():
    C = R_CHUNK
    s, t = np.arange(C)[:, None], np.arange(C)[None]
    out = []
    for d in range(2):
        before = (s < t) if d == 0 else (s > t)
        upto = (s <= t) if d == 0 else (s >= t)
        cols = [before, upto, upto, before, before.T]
        out.append(np.tile(np.concatenate(cols, axis=1), (2, 1)))
        cols = []
        for n in range(R_LEVELS):
            added = before & ((s >> (n + 1)) == (t >> (n + 1))) & ((s >> n) != (t >> n))
            cols += [added, added.T]
        cols += [s == t, np.ones((C, C))]
        out += [np.kron(np.eye(2), m) for m in cols]
    return np.concatenate(out, axis=1).astype(np.float32)


def const_spread():
    out = np.zeros((2 * TILES, TILES, P), np.float32)
    for i in range(TILES):
        for h in range(2):
            out[2 * i + h, i, R_DIM * h:R_DIM * (h + 1)] = 1
    return out.reshape(2 * TILES, TOK)


def stage_shift_taps(p, taps):
    nc = p.nc
    p.begin_stage()
    made = p.semaphore("taps_made")
    at = PARAMS["r_mu"][0]
    with nc.Block() as block:
        @block.vector
        def _(dve):
            mu = p.params[:, at:at + 12]
            nc.vector.tensor_scalar(taps[:, 0, :], mu, 0.5, None, ALU.mult).then_inc(made, 1)
            nc.vector.tensor_scalar(taps[:, 1, :], mu, -1.0, 1.0, ALU.mult, ALU.add).then_inc(made, 1)


def token_shift(nc, raw, outs, taps, which):
    def finish(then, j):
        n = which * WT + j
        for i, (rows, out) in enumerate(outs):
            side, here = taps[rows, 0, n:n + 1], taps[rows, 1, n:n + 1]
            last = conv3(nc, then, out[:, j, :], raw[rows, j, :], [side, here, side])
            if i < len(outs) - 1:
                then(last)
        return last

    return finish


def lora_products(nc, p, up, down, d, j, bank):
    for n, (at, width) in enumerate(GROUPS):
        last = nc.tensor.matmul(p.psum[:, bank + n, 0:width], up[64 * d:64 * d + 64, j * P:(j + 1) * P],
                                down[64 * d:64 * d + 64, at:at + width], start=True, stop=True)
    return last


def stage_rwkv_prepare(p, d, r_dram, kr_dram, kk_dram, down, up, mix_k, queries, keys, chunk_decay, squares):
    nc = p.nc
    p.begin_stage()
    chain = p.semaphore("dve_chain")
    lora_ready = p.semaphore("rp_lora_ready")
    lora_read = p.semaphore("rp_lora_read")
    logs_ready = p.semaphore("rp_logs_ready")
    exps_ready = p.semaphore("rp_exps_ready")
    squares_ready = p.semaphore("rp_squares_ready")
    norms_ready = p.semaphore("rp_norms_ready")
    roots_ready = p.semaphore("rp_roots_ready")
    inverse_ready = p.semaphore("rp_inverse_ready")
    inverse_turned = p.semaphore("rp_inverse_turned")
    inverse_copied = p.semaphore("rp_inverse_copied")
    inverse_spread = p.semaphore("rp_inverse_spread")
    spread_loaded = p.semaphore("rp_spread_loaded")
    raw_keys_ready = p.semaphore("rp_raw_keys_ready")
    pair_done = p.semaphore("rp_pair_done")
    r_loaded, kr_loaded = p.semaphores("rp_r_loaded", 2), p.semaphores("rp_kr_loaded", 2)
    kk_ready = p.semaphore("rp_kk_ready")
    kk_moved = p.semaphores("rp_kk_moved", 2)
    half_e = -float(np.exp(-0.5))
    with ExitStack() as local:
        sb = lambda name, shape: local.enter_context(nc.sbuf_tensor(f"rp_{name}{d}", shape, F32))
        log_w, rate, decay = sb("log_w", [P, TOK]), sb("rate", [P, TOK]), sb("decay", [P, TOK])
        kk_buffers, norm, grown = sb("kk", [P, 2, TOK]), sb("norm", [P, TOK]), sb("grown", [P, TOK])
        carry_on = sb("carry_on", [P, TOK])
        r_in, kr_in = sb("r_in", [P, 2, TOK]), sb("kr_in", [P, 2, TOK])
        if d == 0:
            norms, inverse_rows, spread = sb("norms", [P, 3, 2 * TILES]), sb("inverse_rows", [2 * TILES, P]), sb("spread", [2 * TILES, TOK])
        chunked = lambda a: a.rearrange("p (c t) -> p c t", t=R_CHUNK)
        order = slice(None) if d == 0 else slice(None, None, -1)
        first, last_of_chunk = (0, R_CHUNK - 1) if d == 0 else (R_CHUNK - 1, 0)
        with nc.Block() as block:
            @block.sync
            def _(sp):
                if d == 0:
                    sp.dma_start(spread[:, :], p.dram["const_spread"]).then_inc(spread_loaded, 16)
                for j in range(R_PAIRS):
                    if j >= 2:
                        sp.wait_ge(pair_done, j - 1)
                    sp.dma_start(r_in[:, j % 2, :], r_dram[j]).then_inc(r_loaded[j % 2], 16)
                    sp.dma_start(kr_in[:, j % 2, :], kr_dram[j]).then_inc(kr_loaded[j % 2], 16)
                    if d == 1:
                        sp.dma_start(kk_buffers[:, j % 2, :], kk_dram[j]).then_inc(kk_moved[j % 2], 16)

            @block.gpsimd
            def _(pool):
                if d == 0:
                    for j in range(R_PAIRS):
                        pool.wait_ge(kk_ready, j + 1)
                        nc.gpsimd.dma_start(kk_dram[j], kk_buffers[:, j % 2, :]).then_inc(kk_moved[j % 2], 16)
                    for slot in range(2):
                        pool.wait_ge(kk_moved[slot], 16 * R_PAIRS // 2)

            @block.tensor
            def _(pe):
                def sum_squares(j):
                    pe.wait_ge(squares_ready, j + 1)
                    for t in range(TILES):
                        last = nc.tensor.matmul(p.psum[:, 6, 2 * t:2 * t + 2], squares[:, t * P:(t + 1) * P],
                                                p.const("head_ones")[:, 0:P:R_DIM], start=True, stop=True)
                    last.then_inc(norms_ready, 1)

                if d == 0:
                    sum_squares(0)
                for j in range(R_PAIRS):
                    if j:
                        pe.wait_ge(lora_read, 6 * j)
                    lora_products(nc, p, up[:, 0], down[:, 0], d, j, 0)
                    lora_products(nc, p, up[:, 1], down[:, 1], d, j, 3).then_inc(lora_ready, 1)
                    if d == 1:
                        continue
                    pe.wait_ge(inverse_ready, j + 1)
                    nc.tensor.transpose(p.psum[0:2 * TILES, 7, 0:P], norms[:, 2, :], p.const("ident")).then_inc(inverse_turned, 1)
                    pe.wait_ge(lora_read, 6 * j + 3)
                    pe.wait_ge(spread_loaded, 16)
                    pe.wait_ge(inverse_copied, j + 1)
                    for t in range(TILES):
                        last = nc.tensor.matmul(p.psum[:, t // 4, (t % 4) * P:(t % 4 + 1) * P], spread[:, t * P:(t + 1) * P],
                                                inverse_rows[:, :], start=True, stop=True)
                    last.then_inc(inverse_spread, 1)
                    if j + 1 < R_PAIRS:
                        sum_squares(j + 1)
                    pe.wait_ge(kk_ready, j + 1)

            @block.scalar
            def _(act):
                def roots(j):
                    act.wait_ge(raw_keys_ready, j + 1)
                    nc.scalar.activation(squares[:, :], kk_buffers[:, j % 2, :], ACT.Square).then_inc(squares_ready, 1)
                    act.wait_ge(norms_ready, j + 1)
                    nc.scalar.activation(norms[:, 0, :], p.psum[:, 6, 0:2 * TILES], ACT.Sqrt).then_inc(roots_ready, 1)

                if d == 0:
                    roots(0)
                for j in range(R_PAIRS):
                    act.wait_ge(lora_ready, j + 1)
                    if j:
                        act.wait_ge(pair_done, j)
                    for n, (at, width) in enumerate(GROUPS):
                        nc.scalar.activation(log_w[:, at:at + width], p.psum[:, n, 0:width], ACT.Sigmoid,
                                             bias=p.param("r_w0", WT * d + j)).then_inc(lora_read, 1)
                    for n, (at, width) in enumerate(GROUPS):
                        nc.scalar.activation(rate[:, at:at + width], p.psum[:, 3 + n, 0:width], ACT.Sigmoid,
                                             bias=p.param("r_a0", WT * d + j)).then_inc(lora_read, 1)
                    if d == 0:
                        act.wait_ge(inverse_turned, j + 1)
                        nc.scalar.copy(inverse_rows[:, :], p.psum[0:2 * TILES, 7, 0:P]).then_inc(inverse_copied, 1)
                    act.wait_ge(logs_ready, j + 1)
                    nc.scalar.activation(log_w[:, :], log_w[:, :], ACT.Exp).then_inc(exps_ready, 1)
                    nc.scalar.activation(grown[:, :], decay[:, :], ACT.Exp).then_inc(exps_ready, 1)
                    act.wait_ge(exps_ready, 3 * j + 2)
                    nc.scalar.activation(decay[:, :], decay[:, :], ACT.Exp, scale=-1.0).then_inc(exps_ready, 1)
                    if d == 0 and j + 1 < R_PAIRS:
                        roots(j + 1)

            @block.vector
            def _(dve):
                made = [0]

                def then(instruction):
                    made[0] += 1
                    instruction.then_inc(chain, 1)
                    dve.wait_ge(chain, made[0])

                then(nc.vector.memset(carry_on[:, :], 1.0))
                then(nc.vector.memset(chunked(carry_on[:, :])[:, :, first], 0.0))

                def raw_keys(j):
                    dve.wait_ge(kr_loaded[j % 2], 16 * (j // 2 + 1))
                    if j >= 2:
                        dve.wait_ge(kk_moved[j % 2], 16 * (j // 2))
                    nc.vector.tensor_scalar(kk_buffers[:, j % 2, :], kr_in[:, j % 2, :], p.param("r_k_k", j), None,
                                            ALU.mult).then_inc(raw_keys_ready, 1)

                if d == 0:
                    raw_keys(0)
                for j in range(R_PAIRS):
                    dve.wait_ge(r_loaded[j % 2], 16 * (j // 2 + 1))
                    dve.wait_ge(kr_loaded[j % 2], 16 * (j // 2 + 1))
                    rT, krT = r_in[:, j % 2, :], kr_in[:, j % 2, :]
                    kk = kk_buffers[:, j % 2, :]
                    if d == 0:
                        dve.wait_ge(roots_ready, j + 1)
                        then(nc.vector.tensor_scalar(norms[:, 1, :], norms[:, 0, :], 1e-12, None, ALU.max))
                        nc.vector.reciprocal(norms[:, 2, :], norms[:, 1, :]).then_inc(inverse_ready, 1)
                    dve.wait_ge(lora_read, 6 * (j + 1))
                    then(nc.vector.tensor_scalar(log_w[:, :], log_w[:, :], half_e, None, ALU.mult))
                    then(nc.vector.tensor_tensor_scan(decay[:, order], carry_on[:, order], log_w[:, order], 0.0, ALU.mult, ALU.add))
                    nc.vector.tensor_tensor(log_w[:, :], decay[:, :], log_w[:, :], ALU.subtract).then_inc(logs_ready, 1)
                    if d == 0:
                        dve.wait_ge(inverse_spread, j + 1)
                        spread_inverse = p.psum[:, 0:3, :].rearrange("p b n -> p (b n)")[:, 0:TOK]
                        nc.vector.tensor_tensor(kk, kk, spread_inverse, ALU.mult).then_inc(kk_ready, 1)
                        if j + 1 < R_PAIRS:
                            raw_keys(j + 1)
                        dve.wait_ge(kk_ready, j + 1)
                    else:
                        dve.wait_ge(kk_moved[j % 2], 16 * (j // 2 + 1))
                    dve.wait_ge(exps_ready, 3 * (j + 1))
                    for q in range(2):
                        rows = slice(R_DIM * q, R_DIM * q + R_DIM)
                        nc.vector.tensor_tensor(queries[rows, j, :, q, :], chunked(kk[rows, :]), chunked(log_w[rows, :]), ALU.mult)
                        nc.vector.tensor_tensor(queries[rows, j, :, 1 - q, :], chunked(grown[rows, :]), chunked(rT[rows, :]), ALU.mult)
                    then(nc.vector.tensor_copy(chunk_decay[:, j, :], chunked(grown[:, :])[:, :, last_of_chunk]))
                    then(nc.vector.tensor_tensor(norm[:, :], kk, rate[:, :], ALU.mult))
                    for q in range(2):
                        rows = slice(R_DIM * q, R_DIM * q + R_DIM)
                        last = nc.vector.scalar_tensor_tensor(keys[rows, j, :, q, :], chunked(norm[rows, :]), -1.0, chunked(decay[rows, :]),
                                                              ALU.mult, ALU.mult)
                    then(last)
                    then(nc.vector.tensor_scalar(rate[:, :], rate[:, :], p.param("r_k_a", j), mix_k[:, j:j + 1], ALU.mult, ALU.add))
                    then(nc.vector.tensor_tensor(rate[:, :], rate[:, :], krT, ALU.mult))
                    for q in range(2):
                        rows = slice(R_DIM * q, R_DIM * q + R_DIM)
                        last = nc.vector.tensor_tensor(keys[rows, j, :, 1 - q, :], chunked(rate[rows, :]), chunked(decay[rows, :]), ALU.mult)
                    last.then_inc(pair_done, 1)
                    dve.wait_ge(pair_done, j + 1)


def stage_rwkv_scan(p, d, queries, keys, vT, chunk_decay, y):
    nc = p.nc
    C, J = R_CHUNK, R_PAIRS
    HALF = J * C
    LEVELS = R_LEVELS - 1
    steps = scan_order(d, R_CHUNKS, CTX // R_CHUNK)
    N = len(steps)
    p.begin_stage()
    sig = {n: p.semaphore("r_" + n) for n in (
        "products_ready", "inverse_ready", "half_ready", "half_copied", "whole_ready", "keys_turned", "keys_copied",
        "v_turned", "v_copied", "queries_turned", "queries_copied", "pulled_ready", "pulled_copied", "u_start_ready", "from_state_copied",
        "u_sums_ready", "u_ready", "outputs_ready", "y_copied", "state_ready")}
    chain = p.semaphore("dve_chain")
    masks_loaded = p.semaphore("r_masks_loaded")
    part = lambda q: slice(C * q, C * q + C)
    both = [(j, q) for j in range(J) for q in range(2)]
    with ExitStack() as local:
        sb = lambda name, shape: local.enter_context(nc.sbuf_tensor(f"r_{name}{d}", shape, F32))
        prod = sb("prod", [P, 2, 2, J, 2 * C])
        strict_t = sb("strict_t", [P, 2, J, P])
        inv = sb("inv", [P, 2, 2, J, P])
        half = sb("half", [P, 2, J, P])
        pulled = sb("pulled", [P, 2, J, C])
        q_tok, k_tok = sb("q_tok", [P, 2, J, P]), sb("k_tok", [P, 2, J, P])
        from_state = sb("from_state", [P, 2, J, P])
        uv = sb("uv", [P, 2, 2, J, C])
        state = sb("state", [P, J, C])
        own = sb("masks", [P, R_MASKS])
        product_mask = lambda q: own[:, 2 * C * q:2 * C * (q + 1)].unsqueeze(1).broadcast_to([P, J, 2 * C])
        column = lambda n: own[:, n * C:(n + 1) * C].unsqueeze(1)
        strict = column(4).broadcast_to([P, J, C])
        block_column = lambda n: own[:, 5 * C + n * P:5 * C + (n + 1) * P].unsqueeze(1)
        added = lambda n, z: block_column(2 * n + z).bitcast(U32).broadcast_to([P, J, P])
        identity = block_column(2 * R_LEVELS).broadcast_to([P, 2 * J, P])
        blocks = block_column(2 * R_LEVELS + 1).broadcast_to([P, J, P])
        bank = lambda lane, b: p.psum[:, 4 * lane + b, :]
        narrow = lambda a: a.rearrange("p (j n) -> p j n", n=C)
        paired = lambda a: a.rearrange("p (j n) -> p j n", n=P)
        with nc.Block() as block:
            @block.sync
            def _(sp):
                sp.dma_start(own[:, :], p.dram["const_rwkv"][:, d * R_MASKS:(d + 1) * R_MASKS]).then_inc(masks_loaded, 16)

            @block.tensor
            def _(pe):
                for i in range(0, N, 2):
                    def turn(lane, what, turned):
                        for j in range(J):
                            last = nc.tensor.transpose(bank(lane, 3)[:, j * P:(j + 1) * P], what(j, steps[i + lane]), p.const("ident"))
                        last.then_inc(turned, 1)

                    def between_levels(n):
                        for lane in range(2):
                            s = i + lane
                            if n == 0:
                                turn(lane, lambda j, c: keys[:, j, c, :, :].rearrange("p k t -> p (k t)"), sig["keys_turned"])
                            elif n == 1:
                                pe.wait_ge(sig["keys_copied"], s + 1)
                                turn(lane, lambda j, c: vT[:, j, c * C:c * C + 2 * C], sig["v_turned"])
                            elif n == 2:
                                pe.wait_ge(sig["v_copied"], s + 1)
                                turn(lane, lambda j, c: queries[:, j, c, :, :].rearrange("p k t -> p (k t)"), sig["queries_turned"])
                            elif n == 3:
                                pe.wait_ge(sig["queries_copied"], s + 1)
                                for j, q in both:
                                    last = nc.tensor.matmul(
                                        bank(lane, 3)[part(q), j * C:(j + 1) * C], prod[part(1 - q), lane, q, j, part(q)],
                                        uv[part(1 - q), lane, q, j, :], start=True, stop=True)
                                last.then_inc(sig["pulled_ready"], 1)

                    for lane in range(2):
                        s, c = i + lane, steps[i + lane]
                        if s >= 2:
                            pe.wait_ge(sig["state_ready"], s)
                            pe.wait_ge(sig["y_copied"], s - 1)
                        for j, q in both:
                            nc.tensor.matmul(bank(lane, q)[:, j * P:(j + 1) * P], keys[part(q), j, c, :, :],
                                             queries[part(q), j, c, :, :], start=True, stop=True)
                        for j, q in both:
                            last = nc.tensor.matmul(bank(lane, 2)[part(q), j * C:(j + 1) * C], queries[part(q), j, c, q, :],
                                                    keys[part(q), j, c, q, :], start=True, stop=True)
                        last.then_inc(sig["products_ready"], 1)
                    for n in range(LEVELS):
                        between_levels(n)
                        zs = (0, 1) if n < LEVELS - 1 else (0,)
                        for lane in range(2):
                            pe.wait_ge(sig["inverse_ready"], i * R_LEVELS + 2 * n + lane + 1)
                            for j in range(J):
                                last = nc.tensor.matmul(bank(lane, 0)[:, j * P:(j + 1) * P], strict_t[:, lane, j, :],
                                                        inv[:, lane, 0, j, :], start=True, stop=True)
                            last.then_inc(sig["half_ready"], 1)
                        for lane in range(2):
                            pe.wait_ge(sig["half_copied"], i * LEVELS + 2 * n + lane + 1)
                            for z in zs:
                                for j in range(J):
                                    h, other = half[:, lane, j, :], inv[:, lane, 1, j, :]
                                    last = nc.tensor.matmul(bank(lane, 1 + z)[:, j * P:(j + 1) * P],
                                                            *((other, h) if z == 0 else (h, other)), start=True, stop=True)
                            last.then_inc(sig["whole_ready"], 1)
                    for lane in range(2):
                        pe.wait_ge(sig["inverse_ready"], i * R_LEVELS + 2 * LEVELS + lane + 1)
                        for j in range(J):
                            last = nc.tensor.matmul(bank(lane, 2)[:, j * P:(j + 1) * P], q_tok[:, lane, j, :],
                                                    inv[:, lane, 0, j, :], start=True, stop=True)
                        last.then_inc(sig["u_start_ready"], 1)
                    u_sum = lambda lane, j: bank(lane, 0)[:, HALF + j * C:HALF + (j + 1) * C]
                    for lane in range(2):
                        pe.wait_ge(sig["pulled_copied"], i + lane + 1)
                        for j in range(J):
                            nc.tensor.matmul(u_sum(lane, j), inv[:, lane, 0, j, :], pulled[:, lane, j, :], start=(j == 0), stop=False)
                    for lane in range(2):
                        s, c = i + lane, steps[i + lane]
                        output = lambda j, q: bank(lane, 3 if q == 0 else 1)[part(c % 2), j * C:(j + 1) * C]
                        pe.wait_ge(sig["from_state_copied"], s + 1)
                        pe.wait_ge(sig["state_ready"], s + 1)
                        for j in range(J):
                            last = nc.tensor.matmul(u_sum(lane, j), from_state[:, lane, j, :], state[:, j, :], start=False,
                                                    stop=(j == J - 1))
                        last.then_inc(sig["u_sums_ready"], 1)
                        for j, q in both:
                            nc.tensor.matmul(output(j, q), queries[part(q), j, c, 1 - q, :], state[part(q), j, :], start=(j == 0), stop=False)
                        pe.wait_ge(sig["u_ready"], s + 1)
                        for j, q in both:
                            nc.tensor.matmul(bank(lane, 2)[part(q), HALF + j * C:HALF + (j + 1) * C], k_tok[:, lane, j, part(q)],
                                             uv[:, lane, q, j, :], start=True, stop=True)
                        for j, q in both:
                            last = nc.tensor.matmul(output(j, q), prod[:, lane, q, j, part(1 - q)], uv[:, lane, q, j, :],
                                                    start=False, stop=(j == J - 1))
                        last.then_inc(sig["outputs_ready"], 1)

            @block.scalar
            def _(act):
                for i in range(0, N, 2):
                    def between_levels(n):
                        for lane in range(2):
                            s = i + lane
                            if n == 0:
                                act.wait_ge(sig["keys_turned"], s + 1)
                                nc.scalar.copy(k_tok[:, lane], paired(bank(lane, 3))).then_inc(sig["keys_copied"], 1)
                            elif n == 1:
                                act.wait_ge(sig["v_turned"], s + 1)
                                for q in range(2):
                                    last = nc.scalar.copy(uv[part(1 - q), lane, q], paired(bank(lane, 3))[part(1 - q), :, part(q)])
                                last.then_inc(sig["v_copied"], 1)
                            elif n == 2:
                                act.wait_ge(sig["queries_turned"], s + 1)
                                nc.scalar.copy(q_tok[:, lane], paired(bank(lane, 3))).then_inc(sig["queries_copied"], 1)
                            elif n == 3:
                                act.wait_ge(sig["pulled_ready"], s + 1)
                                nc.scalar.copy(pulled[:, lane], narrow(bank(lane, 3)[:, 0:HALF])).then_inc(sig["pulled_copied"], 1)

                    for n in range(LEVELS):
                        between_levels(n)
                        for lane in range(2):
                            act.wait_ge(sig["half_ready"], i * LEVELS + 2 * n + lane + 1)
                            if n:
                                act.wait_ge(sig["whole_ready"], i * LEVELS + 2 * (n - 1) + lane + 1)
                            nc.scalar.copy(half[:, lane], paired(bank(lane, 0))).then_inc(sig["half_copied"], 1)
                    for lane in range(2):
                        s, c = i + lane, steps[i + lane]
                        if d == 0:
                            act.wait_ge(sig["outputs_ready"], s + 1)
                            for q in range(2):
                                out = y[part(c % 2), c // 2, :].rearrange("p (j q n) -> p q j n", q=2, n=C)[:, q]
                                last = nc.scalar.copy(out, narrow(bank(lane, 3 if q == 0 else 1)[part(c % 2), 0:HALF]))
                            last.then_inc(sig["y_copied"], 1)

            @block.vector
            def _(dve):
                made = [0]

                def then(instruction):
                    made[0] += 1
                    instruction.then_inc(chain, 1)
                    dve.wait_ge(chain, made[0])

                nc.vector.memset(state[:, :, :], 0.0).then_inc(sig["state_ready"], 1)
                then(nc.vector.memset(strict_t[:, :, :, :], 0.0))
                dve.wait_ge(masks_loaded, 16)
                for i in range(0, N, 2):
                    for lane in range(2):
                        then(nc.vector.tensor_copy(inv[:, lane].rearrange("p z j n -> p (z j) n"), identity))
                    for lane in range(2):
                        s = i + lane
                        dve.wait_ge(sig["products_ready"], s + 1)
                        if s >= 2:
                            dve.wait_ge(sig["outputs_ready"], s - 1)
                        for q in range(2):
                            nc.vector.tensor_tensor(prod[:, lane, q], paired(bank(lane, q)), product_mask(q), ALU.mult)
                            last = nc.vector.tensor_tensor(strict_t[part(q), lane, :, part(q)],
                                                           narrow(bank(lane, 2)[part(q), 0:HALF]), strict[part(q)], ALU.mult)
                        then(last)
                        for q in range(2):
                            nc.vector.copy_predicated(inv[part(q), lane, 0, :, part(q)], added(0, 0)[part(q), :, part(q)],
                                                      prod[part(q), lane, q, :, part(q)])
                        nc.vector.copy_predicated(inv[:, lane, 1], added(0, 1), strict_t[:, lane]).then_inc(sig["inverse_ready"], 1)
                    for n in range(LEVELS):
                        for lane in range(2):
                            dve.wait_ge(sig["whole_ready"], i * LEVELS + 2 * n + lane + 1)
                            for z in range(2 if n < LEVELS - 1 else 1):
                                last = nc.vector.copy_predicated(inv[:, lane, z], added(n + 1, z),
                                                                 paired(bank(lane, 1 + z)))
                            last.then_inc(sig["inverse_ready"], 1)
                    for lane in range(2):
                        dve.wait_ge(sig["u_start_ready"], i + lane + 1)
                        nc.vector.tensor_tensor(from_state[:, lane], paired(bank(lane, 2)), blocks, ALU.mult).then_inc(sig["from_state_copied"], 1)
                    for lane in range(2):
                        s, c = i + lane, steps[i + lane]
                        dve.wait_ge(sig["u_sums_ready"], s + 1)
                        for q in range(2):
                            last = nc.vector.tensor_copy(uv[part(q), lane, q], narrow(bank(lane, 0)[part(q), HALF:]))
                        last.then_inc(sig["u_ready"], 1)
                        dve.wait_ge(sig["outputs_ready"], s + 1)
                        then(nc.vector.tensor_tensor(state[:, :, :], state[:, :, :], narrow(bank(lane, 2)[:, HALF:]), ALU.add))
                        nc.vector.tensor_tensor(
                            state[:, :, :], state[:, :, :], chunk_decay[:, :, c].unsqueeze(2).broadcast_to([P, J, C]), ALU.mult).then_inc(sig["state_ready"], 1)
                        if d == 1:
                            for q in range(2):
                                out = y[part(c % 2), c // 2, :].rearrange("p (j q n) -> p q j n", q=2, n=C)[:, q]
                                last = nc.vector.tensor_tensor(out, out, narrow(bank(lane, 3 if q == 0 else 1)[part(c % 2), 0:HALF]), ALU.add)
                            last.then_inc(sig["y_copied"], 1)


def stage_rwkv_bonus(p, r_dram, kr_dram, vT, down, up, mix_k, bonus):
    nc = p.nc
    p.begin_stage()
    chain = p.semaphore("dve_chain")
    rates_ready = p.semaphore("rb_rates_ready")
    rates_read = p.semaphore("rb_rates_read")
    products_ready = p.semaphore("rb_products_ready")
    sums_ready = p.semaphore("rb_sums_ready")
    sums_read = p.semaphore("rb_sums_read")
    r_loaded, kr_loaded = p.semaphores("rp_r_loaded", 2), p.semaphores("rp_kr_loaded", 2)
    with ExitStack() as local:
        sb = lambda name, shape: local.enter_context(nc.sbuf_tensor(f"rb_{name}", shape, F32))
        rates = sb("rates", [P, 2, TOK])
        double = sb("double", [P, WT])
        r_in, kr_in = sb("r_in", [P, 2, TOK]), sb("kr_in", [P, 2, TOK])
        with nc.Block() as block:
            @block.sync
            def _(sp):
                for j in range(R_PAIRS):
                    if j >= 2:
                        sp.wait_ge(products_ready, j - 1)
                    sp.dma_start(r_in[:, j % 2, :], r_dram[j]).then_inc(r_loaded[j % 2], 16)
                    sp.dma_start(kr_in[:, j % 2, :], kr_dram[j]).then_inc(kr_loaded[j % 2], 16)

            @block.tensor
            def _(pe):
                for j in range(R_PAIRS):
                    if j:
                        pe.wait_ge(rates_read, 6 * j)
                    if j:
                        pe.wait_ge(sums_read, 3 * j)
                    lora_products(nc, p, up[:, 1], down[:, 1], 0, j, 0)
                    lora_products(nc, p, up[:, 1], down[:, 1], 1, j, 3).then_inc(rates_ready, 1)
                    pe.wait_ge(products_ready, j + 1)
                    for n, (at, width) in enumerate(GROUPS):
                        nc.tensor.matmul(p.psum[:, n, 0:width], p.const("head_ones"),
                                                         rates[:, 0, at:at + width], start=True, stop=True).then_inc(sums_ready, 1)

            @block.scalar
            def _(act):
                for j in range(R_PAIRS):
                    act.wait_ge(rates_ready, j + 1)
                    if j:
                        act.wait_ge(sums_ready, 3 * j)
                    for d in range(2):
                        for n, (at, width) in enumerate(GROUPS):
                            nc.scalar.activation(rates[:, d, at:at + width], p.psum[:, 3 * d + n, 0:width],
                                                                 ACT.Sigmoid, bias=p.param("r_a0", WT * d + j)).then_inc(rates_read, 1)

            @block.vector
            def _(dve):
                made = [0]

                def then(instruction):
                    made[0] += 1
                    instruction.then_inc(chain, 1)
                    dve.wait_ge(chain, made[0])

                then(nc.vector.tensor_scalar(double[:, :], mix_k[:, :], 2.0, None, ALU.mult))
                for j in range(R_PAIRS):
                    dve.wait_ge(rates_read, 6 * (j + 1))
                    r0 = rates[:, 0, :]
                    dve.wait_ge(r_loaded[j % 2], 16 * (j // 2 + 1))
                    dve.wait_ge(kr_loaded[j % 2], 16 * (j // 2 + 1))
                    then(nc.vector.tensor_tensor(r0, r0, rates[:, 1, :], ALU.add))
                    then(nc.vector.tensor_scalar(r0, r0, p.param("r_k_a", j), double[:, j:j + 1], ALU.mult, ALU.add))
                    then(nc.vector.tensor_tensor(r0, r0, kr_in[:, j % 2, :], ALU.mult))
                    nc.vector.scalar_tensor_tensor(r0, r0, p.param("r_r_k", j), r_in[:, j % 2, :], ALU.mult, ALU.mult).then_inc(products_ready, 1)
                    for n, (at, width) in enumerate(GROUPS):
                        dve.wait_ge(sums_ready, 3 * j + n + 1)
                        for rows, late in ((slice(0, R_DIM), R_CHUNK), (slice(R_DIM, P), 0)):
                            last = nc.vector.tensor_tensor(bonus[rows, j, at:at + width], p.psum[rows, n, 0:width],
                                                           vT[rows, j, late + at:late + at + width], ALU.mult)
                        last.then_inc(sums_read, 1)


def stage_rwkv_layernorm(p, y, bonus, factor, factor_dram):
    nc = p.nc
    H = R_HEADS
    p.begin_stage()
    turned = p.semaphore("rl_turned")
    added = p.semaphore("rl_added")
    centred = p.semaphore("rl_centred")
    squared = p.semaphore("rl_squared")
    sums = p.semaphore("rl_sums")
    roots = p.semaphore("rl_roots")
    chain = p.semaphore("dve_chain")
    factor_loaded = p.semaphore("rl_factor_loaded")
    with ExitStack() as local:
        sq = local.enter_context(nc.sbuf_tensor("rl_squares", [P, 2, W], F32))
        st = local.enter_context(nc.sbuf_tensor("rl_stat", [P, TILES, 4, H], F32))
        by_head = lambda a: a.rearrange("p (h n) -> p h n", h=H)
        wide = lambda a: a.unsqueeze(2).broadcast_to([P, H, R_DIM])
        with nc.Block() as block:
            @block.sync
            def _(sp):
                sp.dma_start(factor, factor_dram).then_inc(factor_loaded, 16)
                sp.wait_ge(factor_loaded, 16)

            @block.tensor
            def _(pe):
                for t in range(TILES):
                    if t >= 8:
                        pe.wait_ge(added, t - 7)
                    for j in range(WT):
                        last = nc.tensor.transpose(p.psum[:, t % 8, j * P:(j + 1) * P], bonus[:, j, t * P:(t + 1) * P], p.const("ident"))
                    last.then_inc(turned, 1)

            @block.scalar
            def _(act):
                for t in range(TILES):
                    act.wait_ge(centred, t + 1)
                    if t >= 2:
                        act.wait_ge(sums, t - 1)
                    nc.scalar.activation(sq[:, t % 2, :], y[:, t, :], ACT.Square).then_inc(squared, 1)
                act.wait_ge(sums, TILES)
                nc.scalar.activation(st[:, :, 2, :], st[:, :, 2, :], ACT.Sqrt).then_inc(roots, 1)

            @block.vector
            def _(dve):
                made = [0]

                def then(instruction):
                    made[0] += 1
                    instruction.then_inc(chain, 1)
                    dve.wait_ge(chain, made[0])

                for t in range(TILES + 1):
                    if t < TILES:
                        yt = by_head(y[:, t, :])
                        dve.wait_ge(turned, t + 1)
                        nc.vector.tensor_tensor(y[:, t, :], y[:, t, :], p.psum[:, t % 8, :], ALU.add).then_inc(added, 1)
                        dve.wait_ge(added, t + 1)
                        then(nc.vector.tensor_reduce(st[:, t, 0, :], yt, AX.X, ALU.add))
                        then(nc.vector.tensor_scalar(st[:, t, 1, :], st[:, t, 0, :], 1.0 / R_DIM, None, ALU.mult))
                        nc.vector.tensor_tensor(yt, yt, wide(st[:, t, 1, :]), ALU.subtract).then_inc(centred, 1)
                    if t:
                        dve.wait_ge(squared, t)
                        then(nc.vector.tensor_reduce(st[:, t - 1, 3, :], by_head(sq[:, (t - 1) % 2, :]), AX.X, ALU.add))
                        nc.vector.tensor_scalar(st[:, t - 1, 2, :], st[:, t - 1, 3, :], 1.0 / R_DIM, R_LN_EPS, ALU.mult, ALU.add).then_inc(sums, 1)
                dve.wait_ge(roots, 1)
                then(nc.vector.reciprocal(st[:, :, 3, :], st[:, :, 2, :]))
                for t in range(TILES):
                    yt = by_head(y[:, t, :])
                    nc.vector.tensor_tensor(yt, yt, wide(st[:, t, 3, :]), ALU.mult).then_inc(centred, 1)


def rwkv_branch(p, arena, hT, mix, spill):
    nc = p.nc
    w_in = p.dram["l0_w_in"]
    free = arena[:, KT * TOK:]
    operands = lambda a: a.rearrange("p (j c k t) -> p j c k t", j=R_PAIRS, c=R_CHUNKS, k=2)
    wide = lambda a: a.rearrange("p (j t) -> p j t", j=WT)
    with ExitStack() as outer:
        so = lambda name, shape: outer.enter_context(nc.sbuf_tensor(name, shape, F32))
        vT = so("r_vT", [P, WT, R_CHUNK + TOK])
        down, up = so("r_down", [P, 2, TOK]), so("r_up", [P, 2, W])
        taps, mix_k = so("r_taps", [P, 2, 12]), so("r_mix_k", [P, WT])
        chunk_decay = so("r_chunk_decay", [P, R_PAIRS, R_CHUNKS])
        raw, shifted = wide(free[:, 0:WT * TOK]), wide(free[:, WT * TOK:])
        stage_shift_taps(p, taps)
        spilled = lambda n: spill[n].rearrange("k p t -> p k t")
        every, even, odd = slice(0, P), slice(0, R_DIM), slice(R_DIM, P)
        parts = ([(every, shifted)], [(every, shifted)], [(even, vT[even, :, R_CHUNK:]), (odd, vT[odd, :, 0:TOK])])
        stage_project(
            p, "r", hT, w_in,
            [(M_IN + i * W, W, ACT.Silu if i == 3 else ACT.Copy, raw, False, GROUPS) for i in range(4)]
            + [(M_IN + 4 * W, P, ACT.Tanh, down[:, 0], False, GROUPS), (M_IN + 4 * W + P, P, ACT.Copy, down[:, 1], False, GROUPS)],
            finish={i: token_shift(nc, raw, outs, taps, i) for i, outs in enumerate(parts)},
            store={0: lambda j: (spill[1, j], shifted[:, j, :]), 1: lambda j: (spill[2, j], shifted[:, j, :]),
                   3: lambda j: (spill[0, j], raw[:, j, :])},
            loads=[(up[:, 0, :], p.dram["w_up"]), (up[:, 1, :], p.dram["a_up"])])
        with nc.Block() as block:
            @block.vector
            def _(dve):
                nc.vector.memset(vT[even, :, 0:R_CHUNK], 0.0)
                nc.vector.memset(vT[odd, :, TOK:], 0.0)
                at = PARAMS["r_k_a"][0]
                nc.vector.tensor_scalar(mix_k[:, :], p.params[:, at:at + WT], -1.0, 1.0, ALU.mult, ALU.add)
        y = so("r_y", [P, TILES, W])
        queries, keys = operands(arena[:, 0:KT * TOK]), operands(free)
        for d in range(2):
            stage_rwkv_prepare(p, d, spill[1], spill[2], spill[3], down, up, mix_k, queries, keys, chunk_decay,
                               y.rearrange("p t n -> p (t n)")[:, 0:TOK])
            stage_rwkv_scan(p, d, queries, keys, vT, chunk_decay, y)
        bonus, factor = wide(arena[:, 0:WT * TOK]), wide(free[:, 0:WT * TOK])
        stage_rwkv_bonus(p, spill[1], spill[2], vT, down, up, mix_k, bonus)
        stage_rwkv_layernorm(p, y, bonus, factor, spilled(0))
        stage_turn_back(p, y, range(TILES), lambda h: p.param("r_ln_w", h), lambda h: p.param("r_ln_b", h), factor, mix, WT)


LAT_GROUPS = ((256, 512, 0), (768, 512, 512))
LAT_TILES = range(CTX_TILES, TILES)
FILTER_HIDDEN, FILTER_POS, BANDS = 64, 33, 16


def stage_output(p, layer, arena, mix, gate_dram, x, tiles, x_out, stored, final_gain=None):
    nc = p.nc
    p.begin_stage()
    rows_loaded = p.semaphores("out_rows_loaded", KT)
    loaded = p.semaphore("out_loaded")
    x_loaded = p.semaphores("out_x_loaded", 2)
    products_ready = p.semaphore("out_products_ready")
    gated = p.semaphore("out_gated")
    summed = p.semaphore("out_summed")
    squares_ready = p.semaphore("out_squares_ready")
    roots_ready = p.semaphore("out_roots_ready")
    chain = p.semaphore("dve_chain")
    normed = p.semaphore("out_normed")
    mixT = arena[:, 0:KT * TOK].rearrange("p (k t) -> p k t", k=KT)
    at = tiles[0] * P
    with ExitStack() as local:
        sb = lambda name, shape: local.enter_context(nc.sbuf_tensor(f"out_{name}{layer}", shape, F32))
        weight = sb("weight", [P, KT, D])
        gate = sb("gate", [P, 2, D])
        xt = sb("x", [P, 2, D])
        res = sb("res", [P, 2, D])
        junk = sb("junk", [P, D])
        gain = sb("gain", [P, D])
        stat = sb("stat", [P, TILES, 4])
        assert len(tiles) % 2 == 0
        finished = normed if final_gain is not None else summed
        with nc.Block() as block:
            @block.sync
            def _(sp):
                for k in range(KT):
                    sp.dma_start(mixT[:, k, at:TOK], mix[k, :, at:TOK]).then_inc(rows_loaded[k], 16)
                    sp.dma_start(weight[:, k, :], p.dram[f"l{layer}_w_out"][k * P:(k + 1) * P, :]).then_inc(rows_loaded[k], 16)
                sp.dma_start(gate[:, :, :], gate_dram).then_inc(loaded, 16)
                if final_gain is not None:
                    sp.dma_start(gain[:, :], final_gain).then_inc(loaded, 16)
                for i, t in enumerate(tiles):
                    if i >= 2:
                        sp.wait_ge(finished, i - 1)
                    sp.dma_start(xt[:, i % 2, :], x(t)).then_inc(x_loaded[i % 2], 16)
                    if i:
                        sp.wait_ge(finished, i)
                        sp.dma_start(x_out(tiles[i - 1]), res[:, (i - 1) % 2, :]).then_inc(stored[(i - 1) % 2], 16)
                sp.wait_ge(finished, len(tiles))
                sp.dma_start(x_out(tiles[-1]), res[:, 1, :]).then_inc(stored[1], 16)
                sp.wait_ge(stored[0], 16 * len(tiles) // 2)
                sp.wait_ge(stored[1], 16 * len(tiles) // 2)

            @block.tensor
            def _(pe):
                for k in range(KT):
                    pe.wait_ge(rows_loaded[k], 32)
                    for i in range(4):
                        lhsT = mixT[:, k, tiles[i] * P:(tiles[i] + 1) * P]
                        for n in range(2):
                            last = nc.tensor.matmul(p.psum[:, 2 * i + n, :], lhsT, weight[:, k, n * BANK:(n + 1) * BANK],
                                                    start=(k == 0), stop=(k == KT - 1))
                        if k == KT - 1:
                            last.then_inc(products_ready, 1)
                for i, t in enumerate(tiles[4:], 4):
                    pe.wait_ge(gated, i - 3)
                    for k in range(KT):
                        lhsT = mixT[:, k, t * P:(t + 1) * P]
                        for n in range(2):
                            last = nc.tensor.matmul(p.psum[:, 2 * (i % 4) + n, :], lhsT, weight[:, k, n * BANK:(n + 1) * BANK],
                                                    start=(k == 0), stop=(k == KT - 1))
                    last.then_inc(products_ready, 1)

            @block.scalar
            def _(act):
                if final_gain is not None:
                    for i in range(len(tiles)):
                        act.wait_ge(summed, i + 1)
                        if i:
                            act.wait_ge(squares_ready, i)
                        nc.scalar.activation(junk[:, :], res[:, i % 2, :], ACT.Square,
                                                                accum_out=stat[:, i, 0:1]).then_inc(squares_ready, 1)
                        act.wait_ge(roots_ready, 2 * i + 1)
                        nc.scalar.activation(stat[:, i, 2:3], stat[:, i, 1:2], ACT.Sqrt).then_inc(roots_ready, 1)

            @block.vector
            def _(dve):
                made = [0]

                def then(instruction):
                    made[0] += 1
                    instruction.then_inc(chain, 1)
                    dve.wait_ge(chain, made[0])

                dve.wait_ge(loaded, 16 * (1 + (final_gain is not None)))
                for i, t in enumerate(tiles):
                    dve.wait_ge(products_ready, i + 1)
                    dve.wait_ge(x_loaded[i % 2], 16 * (i // 2 + 1))
                    if i >= 2:
                        dve.wait_ge(stored[i % 2], 16 * (i // 2))
                    out = res[:, i % 2, :]
                    nc.vector.tensor_tensor(
                        out, p.psum[:, 2 * (i % 4):2 * (i % 4) + 2, :].rearrange("p b n -> p (b n)"),
                        gate[:, 1 if t < CTX_TILES else 0, :], ALU.mult).then_inc(gated, 1)
                    dve.wait_ge(gated, i + 1)
                    nc.vector.tensor_tensor(out, out, xt[:, i % 2, :], ALU.add).then_inc(summed, 1)
                    if final_gain is not None:
                        dve.wait_ge(squares_ready, i + 1)
                        nc.vector.tensor_scalar(stat[:, i, 1:2], stat[:, i, 0:1], 1.0 / D, EPS, ALU.mult, ALU.add).then_inc(roots_ready, 1)
                        dve.wait_ge(roots_ready, 2 * i + 2)
                        then(nc.vector.reciprocal(stat[:, i, 3:4], stat[:, i, 2:3]))
                        nc.vector.scalar_tensor_tensor(out, out, stat[:, i, 3:4], gain[:, :], ALU.mult, ALU.mult).then_inc(normed, 1)


G_HEADS, G_CHUNK, G_LEVELS = 4, 128, 7
G_LAT_CHUNKS = LAT // G_CHUNK


def const_hgrn():
    s, t = np.arange(P)[:, None], np.arange(P)[None]
    out = []
    for d in range(2):
        before = (s < t) if d == 0 else (s > t)
        for n in range(G_LEVELS):
            out.append(before & ((s >> (n + 1)) == (t >> (n + 1))) & ((s >> n) != (t >> n)))
    out.append(s == t)
    return np.concatenate(out, axis=1).astype(np.float32)


def stage_lower_bound(p, bound):
    nc = p.nc
    p.begin_stage()
    chain = p.semaphore("dve_chain")
    exps = p.semaphore("lower_exps")
    raw = lambda i: p.params[:, PARAMS["lower"][0] + WT * i:PARAMS["lower"][0] + WT * (i + 1)]
    with ExitStack() as local:
        t = local.enter_context(nc.sbuf_tensor("lower_t", [P, 5, WT], F32))
        with nc.Block() as block:
            @block.scalar
            def _(act):
                act.wait_ge(chain, 3)
                nc.scalar.activation(t[:, 1:3, :], t[:, 1:3, :], ACT.Exp).then_inc(exps, 1)

            @block.vector
            def _(dve):
                made = [0]

                def then(instruction):
                    made[0] += 1
                    instruction.then_inc(chain, 1)
                    dve.wait_ge(chain, made[0])

                then(nc.vector.tensor_tensor(t[:, 0, :], raw(0), raw(1), ALU.max))
                for i in range(2):
                    then(nc.vector.tensor_tensor(t[:, 1 + i, :], raw(i), t[:, 0, :], ALU.subtract))
                dve.wait_ge(exps, 1)
                then(nc.vector.tensor_tensor(t[:, 3, :], t[:, 1, :], t[:, 2, :], ALU.add))
                then(nc.vector.reciprocal(t[:, 4, :], t[:, 3, :]))
                for i in range(2):
                    then(nc.vector.tensor_tensor(t[:, 1 + i, :], t[:, 1 + i, :], t[:, 4, :], ALU.mult))
                then(nc.vector.tensor_tensor(t[:, 3, :], t[:, 1, :], t[:, 2, :], ALU.add))
                then(nc.vector.tensor_tensor(bound[:, 0, :], t[:, 3, :], t[:, 1, :], ALU.subtract))
                then(nc.vector.tensor_scalar(bound[:, 1, :], bound[:, 0, :], -1.0, 1.0, ALU.mult, ALU.add))
                then(nc.vector.tensor_scalar(bound[:, 2, :], bound[:, 1, :], -1.0, None, ALU.mult))


def stage_hgrn(p, arena, qT, gates, v, bound, y):
    nc = p.nc
    H, C, L = G_HEADS, G_CHUNK, G_LEVELS
    units = [(d, h) for d in range(2) for h in range(H)]
    U = len(units)
    UP = L + 2
    EARLY = 2
    p.begin_stage()
    sig = {n: p.semaphore("g_" + n) for n in (
        "floored", "logs_ready", "decay_ready", "k_ready", "gaps_ready", "exps_ready", "keyed", "queried", "level_ready",
        "scores_ready", "merged", "across_copied", "keys_turned", "keys_copied", "update_ready", "state_ready", "outputs_ready", "y_copied",
        "pair_cleared")}
    chain = p.semaphore("dve_chain")
    masks_loaded = p.semaphore("g_masks_loaded")
    SLOT = L * LAT + LAT + TOK
    slot = lambda u: arena[:, (u % 2) * SLOT:(u % 2 + 1) * SLOT]
    level = lambda u, n: slot(u)[:, n * LAT:(n + 1) * LAT]
    q_decayed = lambda u: slot(u)[:, L * LAT:(L + 1) * LAT]
    k_decayed = lambda u: slot(u)[:, (L + 1) * LAT:]
    chunked = lambda a: a.rearrange("p (c t) -> p c t", t=C)

    def halves(a, n, d):
        v4 = a.rearrange("p (b k t) -> p b k t", k=2, t=1 << n)
        return v4[:, :, 1 - d, :], v4[:, :, d, :]

    with ExitStack() as local:
        sb = lambda name, shape: local.enter_context(nc.sbuf_tensor(f"g_{name}", shape, F32))
        decay = sb("decay", [P, TOK])
        carry_on = sb("carry_on", [P, TOK])
        k = sb("k", [P, 2, TOK])
        gap = arena[:, 2 * SLOT:2 * SLOT + TOK]
        pairs = sb("pairs", [P, 2, G_LAT_CHUNKS, C])
        ends = sb("ends", [P, 2, TILES])
        state = sb("state", [P, P])
        keys = sb("keys", [P, 2, P])
        masks = local.enter_context(nc.sbuf_tensor("g_masks", [P, (2 * L + 1) * P], mybir.dt.uint8))
        mask = lambda d, n: masks[:, (2 * L if n == L else d * L + n) * P:][:, 0:P].unsqueeze(1).broadcast_to([P, 4, P])
        with nc.Block() as block:
            @block.sync
            def _(sp):
                sp.dma_start(slot(1)[:, 0:(2 * L + 1) * P], p.dram["const_hgrn"]).then_inc(masks_loaded, 16)

            @block.scalar
            def _(act):
                def take_logs(u):
                    d, h = units[u]
                    act.wait_ge(sig["floored"], u + 1)
                    nc.scalar.activation(gates[d][:, h, :], gates[d][:, h, :], ACT.Ln,
                                         bias=bound[:, 0, h:h + 1]).then_inc(sig["logs_ready"], 1)

                def prepare(u, n):
                    d, h = units[u]
                    if n == 0:
                        act.wait_ge(sig["decay_ready"], u + 1)
                        at = C - 1 if d == 0 else 0
                        nc.scalar.activation(ends[:, u % 2, :], chunked(decay[:, :])[:, :, at], ACT.Exp).then_inc(sig["exps_ready"], 1)
                    if n <= L:
                        act.wait_ge(sig["gaps_ready"], (L + 1) * u + n + 1)
                    out = level(u, n) if n < L else k_decayed(u) if n == L else q_decayed(u)
                    src = decay[:, CTX:TOK] if n == L + 1 else gap[:, 0:TOK if n == L else LAT]
                    nc.scalar.activation(out, src, ACT.Exp).then_inc(sig["exps_ready"], 1)

                take_logs(0)
                for n in range(UP):
                    prepare(0, n)
                take_logs(1)
                for u, (d, h) in enumerate(units):
                    if u + 1 < U:
                        if u:
                            act.wait_ge(sig["outputs_ready"], u * G_LAT_CHUNKS)
                            act.wait_ge(sig["update_ready"], u * TILES)
                        for n in range(EARLY):
                            prepare(u + 1, n)
                    for i, c in enumerate(scan_order(d, TILES, CTX_TILES)):
                        act.wait_ge(sig["keys_turned"], u * TILES + i + 1)
                        if u or i >= 2:
                            act.wait_ge(sig["update_ready"], u * TILES + i - 1)
                        nc.scalar.copy(keys[:, i % 2, :], p.psum[:, 4 + i % 2, 0:P]).then_inc(sig["keys_copied"], 1)
                        if u + 1 < U and EARLY + i < UP:
                            prepare(u + 1, EARLY + i)
                        if u + 2 < U and i == 8:
                            take_logs(u + 2)

            @block.gpsimd
            def _(pool):
                def prepare(u, n):
                    d, h = units[u]
                    if n == 0:
                        pool.wait_ge(sig["k_ready"], u + 1)
                    pool.wait_ge(sig["exps_ready"], u * (UP + 1) + n + 2)
                    if n < L:
                        out, _ = halves(level(u, n), n, d)
                        q, _ = halves(qT[:, h, :], n, d)
                    elif n == L:
                        out, q = k_decayed(u), k[:, u % 2, :]
                    else:
                        out, q = q_decayed(u), qT[:, h, :]
                    nc.gpsimd.tensor_tensor(out, out, q, ALU.mult).then_inc(sig["queried"], 1)

                for u in range(U):
                    for n in range(UP):
                        prepare(u, n)

            @block.vector
            def _(dve):
                made = [0]

                def then(instruction):
                    made[0] += 1
                    instruction.then_inc(chain, 1)
                    dve.wait_ge(chain, made[0])

                def begin(u):
                    d, h = units[u]
                    gate = gates[d][:, h, :]
                    if u >= 2:
                        dve.wait_ge(sig["scores_ready"], 2 * (L + 1) * (u - 1))
                        dve.wait_ge(sig["queried"], UP * (u - 1))
                    nc.vector.tensor_scalar(k[:, u % 2, :], gate, bound[:, 2, h:h + 1], bound[:, 1, h:h + 1],
                                            ALU.mult, ALU.add).then_inc(sig["k_ready"], 1)
                    dve.wait_ge(sig["k_ready"], u + 1)
                    nc.vector.tensor_scalar(gate, gate, bound[:, 1, h:h + 1], 2.0 ** -62, ALU.mult, ALU.max).then_inc(sig["floored"], 1)

                def prepare(u, n):
                    d, h = units[u]
                    gate, b = gates[d][:, h, :], decay[:, :]
                    if n == 0:
                        if h == 0:
                            then(nc.vector.memset(carry_on[:, :], 1.0))
                            then(nc.vector.memset(chunked(carry_on[:, :])[:, :, 0 if d == 0 else C - 1], 0.0))
                        dve.wait_ge(sig["logs_ready"], u + 1)
                        order = slice(None) if d == 0 else slice(None, None, -1)
                        if u:
                            dve.wait_ge(sig["exps_ready"], u * (UP + 1))
                        nc.vector.tensor_tensor_scan(b[:, order], carry_on[:, order], gate[:, order], 0.0,
                                                                             ALU.mult, ALU.add).then_inc(sig["decay_ready"], 1)
                        dve.wait_ge(sig["decay_ready"], u + 1)
                    dve.wait_ge(sig["exps_ready"], u * (UP + 1) + n + 1)
                    if n < L:
                        bq, bk = halves(b[:, CTX:TOK], n, d)
                        gq, gk = halves(gap[:, 0:LAT], n, d)
                        at = (1 << n) - 1 if d == 0 else 0
                        anchor = bk[:, :, at:at + 1].broadcast_to(list(bk.shape))
                        nc.vector.tensor_tensor(gq, bq, anchor, ALU.subtract)
                        nc.vector.tensor_tensor(gk, anchor, bk, ALU.subtract).then_inc(sig["gaps_ready"], 1)
                    elif n == L:
                        at = C - 1 if d == 0 else 0
                        end = chunked(b)[:, :, at:at + 1].broadcast_to([P, TILES, C])
                        nc.vector.tensor_tensor(chunked(gap[:, :]), end, chunked(b), ALU.subtract).then_inc(sig["gaps_ready"], 1)

                def scale_keys(u, n):
                    d, h = units[u]
                    if n < L:
                        _, keyed = halves(level(u, n), n, d)
                        _, kk = halves(k[:, u % 2, CTX:TOK], n, d)
                        dve.wait_ge(sig["exps_ready"], u * (UP + 1) + n + 2)
                        nc.vector.tensor_tensor(keyed, keyed, kk, ALU.mult).then_inc(sig["keyed"], 1)

                dve.wait_ge(masks_loaded, 16)
                then(nc.vector.tensor_copy(masks[:, :], slot(1)[:, 0:(2 * L + 1) * P]))
                begin(0)
                for n in range(UP):
                    prepare(0, n)
                    scale_keys(0, n)
                begin(1)
                for u, (d, h) in enumerate(units):
                    if h < 2:
                        then(nc.vector.memset(pairs[:, u % 2], 0.0))
                    for n in range(UP):
                        if n <= L:
                            for g in range(2):
                                m = u * 2 * (L + 1) + 2 * n + g
                                dve.wait_ge(sig["scores_ready"], m + 1)
                                if m >= 2:
                                    dve.wait_ge(sig["merged"], m - 1)
                                nc.vector.copy_predicated(
                                    pairs[:, u % 2, 4 * g:4 * g + 4, :], mask(d, n), chunked(p.psum[:, m % 4, :])).then_inc(sig["merged"], 1)
                        if u + 1 < U and 1 <= n <= 2 * EARLY:
                            (prepare if n % 2 else scale_keys)(u + 1, (n - 1) // 2)
                    nc.vector.memset(state[:, :], 0.0).then_inc(sig["state_ready"], 1)
                    dve.wait_ge(sig["state_ready"], u * (TILES + 1) + 1)
                    done = 0
                    for i, c in enumerate(scan_order(d, TILES, CTX_TILES)):
                        if u + 1 < U and EARLY + i < UP:
                            prepare(u + 1, EARLY + i)
                        dve.wait_ge(sig["update_ready"], u * TILES + i + 1)
                        if c >= CTX_TILES:
                            dve.wait_ge(sig["outputs_ready"], u * G_LAT_CHUNKS + done + 1)
                            out, src = y[:, c - CTX_TILES, h * P:(h + 1) * P], p.psum[:, 6 + i % 2, 0:P]
                            if d == 0:
                                nc.vector.tensor_copy(out, src).then_inc(sig["y_copied"], 1)
                            else:
                                nc.vector.tensor_tensor(out, out, src, ALU.add).then_inc(sig["y_copied"], 1)
                            done += 1
                        nc.vector.scalar_tensor_tensor(
                            state[:, :], state[:, :], ends[:, u % 2, c:c + 1], p.psum[:, 4 + i % 2, P:2 * P], ALU.mult, ALU.add).then_inc(sig["state_ready"], 1)
                        dve.wait_ge(sig["state_ready"], u * (TILES + 1) + i + 2)
                        if u + 1 < U and EARLY + i < UP:
                            scale_keys(u + 1, EARLY + i)
                        if u + 2 < U and i == 7:
                            begin(u + 2)

            @block.tensor
            def _(pe):
                for u, (d, h) in enumerate(units):
                    for n in range(L + 1):
                        if n < L:
                            pe.wait_ge(sig["keyed"], u * L + n + 1)
                            pe.wait_ge(sig["queried"], u * UP + n + 1)
                        else:
                            pe.wait_ge(sig["k_ready"], u + 1)
                        for g in range(2):
                            m = u * 2 * (L + 1) + 2 * n + g
                            if m >= 4:
                                pe.wait_ge(sig["merged"], m - 3)
                            for c in range(4 * g, 4 * g + 4):
                                at = slice(c * C, (c + 1) * C)
                                left = level(u, n)[:, at] if n < L else k[:, u % 2, CTX:TOK][:, at]
                                right = level(u, n)[:, at] if n < L else qT[:, h, at]
                                last = nc.tensor.matmul(p.psum[:, m % 4, (c - 4 * g) * C:(c - 4 * g + 1) * C], left, right,
                                                        start=True, stop=True)
                            last.then_inc(sig["scores_ready"], 1)
                    pe.wait_ge(sig["merged"], (u + 1) * 2 * (L + 1))
                    pe.wait_ge(sig["queried"], (u + 1) * UP)
                    done = 0
                    for i, c in enumerate(scan_order(d, TILES, CTX_TILES)):
                        states = u * (TILES + 1) + i + 1
                        if states > 1:
                            pe.wait_ge(sig["state_ready"], states - 1)
                        nc.tensor.transpose(p.psum[:, 4 + i % 2, 0:P], k_decayed(u)[:, c * C:(c + 1) * C],
                                                                    p.const("ident")).then_inc(sig["keys_turned"], 1)
                        if c >= CTX_TILES:
                            lat = c - CTX_TILES
                            if u or done >= 2:
                                pe.wait_ge(sig["y_copied"], u * G_LAT_CHUNKS + done - 1)
                            nc.tensor.matmul(p.psum[:, 6 + i % 2, 0:P], pairs[:, u % 2, lat, :], v[:, c, h * P:(h + 1) * P],
                                             start=True, stop=False)
                            pe.wait_ge(sig["state_ready"], states)
                            nc.tensor.matmul(
                                p.psum[:, 6 + i % 2, 0:P], q_decayed(u)[:, lat * C:(lat + 1) * C], state[:, :], start=False, stop=True).then_inc(sig["outputs_ready"], 1)
                            done += 1
                        pe.wait_ge(sig["keys_copied"], u * TILES + i + 1)
                        nc.tensor.matmul(p.psum[:, 4 + i % 2, P:2 * P], keys[:, i % 2, :],
                                                                  v[:, c, h * P:(h + 1) * P], start=True, stop=True).then_inc(sig["update_ready"], 1)


def hgrn_branch(p, arena, hT, mix):
    nc = p.nc
    w_in = p.dram["l1_w_in"]
    with ExitStack() as outer:
        so = lambda name, shape: outer.enter_context(nc.sbuf_tensor(name, shape, F32))
        y = so("g_y", [P, G_LAT_CHUNKS, W])
        bound = so("g_bound", [P, 3, WT])
        with ExitStack() as inner:
            si = lambda name, shape: inner.enter_context(nc.sbuf_tensor(name, shape, F32))
            gates = [si(f"g_gates{d}", [P, WT, TOK]) for d in range(2)]
            v = si("g_v", [P, TILES, W])
            qT = si("g_qT", [P, WT, LAT])
            z_tok = arena[:, KT * TOK:][:, 0:G_LAT_CHUNKS * W].rearrange("p (t n) -> p t n", n=W)
            z_dram = p.scratch["z"]
            stage_lower_bound(p, bound)
            stage_project(p, "g", hT, w_in, [
                (2 * W, W, ACT.Sigmoid, gates[0], False, GROUPS), (3 * W, W, ACT.Sigmoid, gates[1], False, GROUPS),
                (W, W, ACT.Copy, v, True, (0, TILES)),
                (0, W, ACT.Copy, qT, False, LAT_GROUPS),
                (4 * W, W, ACT.Silu, z_tok, True, (CTX_TILES, TILES, CTX_TILES))], save=(4, z_dram))
            stage_hgrn(p, arena, qT, gates, v, bound, y)
        gate = arena[:, 0:G_LAT_CHUNKS * W].rearrange("p (t n) -> p t n", n=W)
        stage_heads_rmsnorm(p, y, gate, z_dram, range(G_LAT_CHUNKS), EPS)
        stage_turn_back(p, y, range(G_LAT_CHUNKS), lambda h: p.param("g_norm_g", h), None, None, mix, 0, CTX)


F_TILES = LAT // 2 // P


def const_hyena():
    f32 = np.float32
    pos = np.arange(LAT, dtype=f32)
    t = pos / f32(LAT)
    bands = np.linspace(1e-4, BANDS - 1, BANDS, dtype=f32)
    ang = (f32(2.0 * np.pi / LAT) * pos[:, None] * bands).astype(f32)
    z = np.concatenate([t[:, None], np.cos(ang), np.sin(ang)], axis=-1).astype(f32)
    top, low = np.log(1e-2) / 0.3, np.log(1e-2) / 1.5
    deltas = np.abs(np.linspace(low, top, W, dtype=f32))
    window = (np.exp(-t[:, None] * deltas) + f32(0.05)).astype(f32)
    order = np.concatenate([np.arange(0, LAT, 2), np.arange(1, LAT, 2)])
    turn = (order[:, None] * (2 * np.arange(LAT // 2)[None] + 1)) % (4 * LAT)
    cos, sin = (fn(np.pi * turn / (2 * LAT)).astype(f32) for fn in (np.cos, np.sin))
    down = np.stack([m.reshape(KT, P, F_TILES, P).transpose(2, 1, 0, 3).reshape(F_TILES, P, LAT) for m in (cos, sin)], axis=2)
    up = np.stack([m.T.reshape(F_TILES, P, LAT) for m in (cos, sin)], axis=2)
    return {"positions": np.ascontiguousarray(z[order].T), "window": window[order].reshape(KT, P, W),
            "transform": np.ascontiguousarray(down), "transform_back": np.ascontiguousarray(up)}


def stage_filters(p, sums, differences, magnitudes):
    nc = p.nc
    TWO_PI = 2 * np.pi
    HIGH = float(np.float32(np.round(TWO_PI * 4096) / 4096))
    MIDDLE = float(np.float32(TWO_PI - HIGH))
    ROUND = 1.5 * 2.0 ** 23
    PI = 3.14159250259
    F = FILTER_HIDDEN
    p.begin_stage()
    loaded = p.semaphore("f_loaded")
    window_loaded = p.semaphores("f_window_loaded", 2)
    product_ready = p.semaphore("f_product_ready")
    reduced = p.semaphore("f_reduced")
    hidden_ready = p.semaphore("f_hidden_ready")
    taps_ready = p.semaphore("f_taps_ready")
    windowed = p.semaphore("f_windowed")
    absolute = p.semaphore("f_absolute")
    summed = p.semaphore("f_summed")
    chain = p.semaphore("dve_chain")
    with ExitStack() as local:
        sb = lambda name, shape: local.enter_context(nc.sbuf_tensor(f"f_{name}", shape, F32))
        positions, w1, w2, w3 = sb("positions", [FILTER_POS, LAT]), sb("w1", [FILTER_POS, F]), sb("w2", [F, F]), sb("w3", [F, 2 * W])
        angle, turns, hidden = sb("angle", [F, LAT]), sb("turns", [F, LAT]), sb("hidden", [F, LAT])
        window = sb("window", [P, 2, W])
        taps = sb("taps", [P, 2, 2, W])
        size = sb("size", [P, 2, 2, W])
        with nc.Block() as block:
            @block.sync
            def _(sp):
                for dst, name in ((positions, "positions"), (w1, "l1_hyena_w1"), (w2, "l1_hyena_w2"), (w3, "l1_hyena_w3")):
                    sp.dma_start(dst[:, :], p.dram[name]).then_inc(loaded, 16)
                for t in range(KT):
                    if t >= 2:
                        sp.wait_ge(windowed, 2 * (t - 1))
                    sp.dma_start(window[:, t % 2, :], p.dram["window"][t]).then_inc(window_loaded[t % 2], 16)

            @block.tensor
            def _(pe):
                pe.wait_ge(loaded, 64)
                for layer in range(2):
                    if layer:
                        pe.wait_ge(hidden_ready, layer)
                    for n in range(2):
                        at = slice(n * BANK, (n + 1) * BANK)
                        last = nc.tensor.matmul(p.psum[0:F, n, :], (w1, w2)[layer][:, :], (positions, hidden)[layer][:, at],
                                                start=True, stop=True)
                    last.then_inc(product_ready, 1)
                pe.wait_ge(hidden_ready, 2)
                for t in range(KT):
                    if t >= 2:
                        pe.wait_ge(windowed, 2 * (t - 1))
                    for n in range(2):
                        nc.tensor.matmul(p.psum[:, 2 + 2 * (t % 2) + n, :], hidden[:, t * P:(t + 1) * P],
                                                         w3[:, n * W:(n + 1) * W], start=True, stop=True).then_inc(taps_ready, 1)

            @block.scalar
            def _(act):
                for layer in range(2):
                    act.wait_ge(reduced, layer + 1)
                    nc.scalar.activation(hidden[:, :], angle[:, :], ACT.Sin).then_inc(hidden_ready, 1)
                for t in range(KT):
                    act.wait_ge(windowed, 2 * (t + 1))
                    if t >= 2:
                        act.wait_ge(summed, 2 * (t - 1))
                    nc.scalar.activation(size[:, t % 2], taps[:, t % 2], ACT.Abs).then_inc(absolute, 1)

            @block.gpsimd
            def _(pool):
                for t in range(KT):
                    pool.wait_ge(absolute, t + 1)
                    for n in range(2):
                        if t + n:
                            pool.wait_ge(summed, 2 * t + n)
                        if t + n:
                            nc.gpsimd.tensor_tensor(magnitudes[:, :], magnitudes[:, :], size[:, t % 2, n], ALU.add).then_inc(summed, 1)
                        else:
                            nc.gpsimd.tensor_copy(magnitudes[:, :], size[:, 0, 0]).then_inc(summed, 1)

            @block.vector
            def _(dve):
                made = [0]

                def then(instruction):
                    made[0] += 1
                    instruction.then_inc(chain, 1)
                    dve.wait_ge(chain, made[0])

                for layer in range(2):
                    dve.wait_ge(product_ready, layer + 1)
                    if layer:
                        dve.wait_ge(hidden_ready, layer)
                    bias = p.param(("b1", "b2")[layer], 0, F)
                    then(nc.vector.tensor_scalar(angle[:, :], p.psum[0:F, 0:2, :].rearrange("p b n -> p (b n)"), bias, None, ALU.add))
                    then(nc.vector.tensor_scalar(turns[:, :], angle[:, :], 1 / TWO_PI, ROUND, ALU.mult, ALU.add))
                    then(nc.vector.tensor_scalar(turns[:, :], turns[:, :], ROUND, None, ALU.subtract))
                    then(nc.vector.scalar_tensor_tensor(angle[:, :], turns[:, :], -HIGH, angle[:, :], ALU.mult, ALU.add))
                    then(nc.vector.scalar_tensor_tensor(angle[:, :], turns[:, :], -MIDDLE, angle[:, :], ALU.mult, ALU.add))
                    nc.vector.tensor_scalar(angle[:, :], angle[:, :], -PI, PI, ALU.max, ALU.min).then_inc(reduced, 1)
                for t in range(KT):
                    dve.wait_ge(window_loaded[t % 2], 16 * (t // 2 + 1))
                    if t >= 2:
                        dve.wait_ge(absolute, t - 1)
                    for n in range(2):
                        dve.wait_ge(taps_ready, 2 * t + n + 1)
                        nc.vector.tensor_tensor(taps[:, t % 2, n], p.psum[:, 2 + 2 * (t % 2) + n, :],
                                                              window[:, t % 2, :], ALU.mult).then_inc(windowed, 1)
                    dve.wait_ge(windowed, 2 * (t + 1))
                    nc.vector.tensor_tensor(sums[:, t, :], taps[:, t % 2, 0], taps[:, t % 2, 1], ALU.add)
                    then(nc.vector.tensor_tensor(differences[:, t, :], taps[:, t % 2, 0], taps[:, t % 2, 1], ALU.subtract))


def conv_product(p, raw, uT, out, which):
    nc = p.nc
    dst = (uT, out, out)[which]

    def finish(then, j):
        n = which * WT + j
        before, here, after = (p.param("short_w", 3 * WT * tap + n) for tap in range(3))
        o, r = dst[:, j, :], raw[:, j, :]
        then(nc.vector.tensor_scalar(o, r, here, p.param("short_b", n), ALU.mult, ALU.add))
        then(nc.vector.scalar_tensor_tensor(o[:, 1:LAT], r[:, 0:LAT - 1], before, o[:, 1:LAT], ALU.mult, ALU.add))
        last = nc.vector.scalar_tensor_tensor(o[:, 0:LAT - 1], r[:, 1:LAT], after, o[:, 0:LAT - 1], ALU.mult, ALU.add)
        if which == 2:
            then(last)
            last = nc.vector.tensor_tensor(uT[:, j, :], uT[:, j, :], o, ALU.mult)
        return last

    return finish


def stage_turn_u(p, uT, u_tok, x0T, zT):
    nc = p.nc
    p.begin_stage()
    turned = p.semaphore("turn_turned")
    copied = p.semaphore("turn_copied")
    with nc.Block() as block:
        @block.tensor
        def _(pe):
            for t in range(KT):
                at = slice((t % 4) * P, (t % 4 + 1) * P)
                for j in range(WT):
                    by_parity = uT[:, j, :].rearrange("p (n e) -> p e n", e=2)
                    last = nc.tensor.transpose(p.psum[:, t, j * P:(j + 1) * P], by_parity[:, t // 4, at], p.const("ident"))
                last.then_inc(turned, 1)

        @block.scalar
        def _(act):
            for t in range(KT):
                act.wait_ge(turned, t + 1)
                nc.scalar.copy(u_tok[:, t, :], p.psum[:, t, :]).then_inc(copied, 1)

        @block.gpsimd
        def _(pool):
            nc.gpsimd.tensor_tensor(x0T[:, :, :], x0T[:, :, :], zT[:, :, :], ALU.mult)


def stage_transform(p, u_tok, sums, differences, real, imag, spectrum, whole):
    nc = p.nc
    p.begin_stage()
    loaded = p.semaphores("t_loaded", 2)
    sums_ready = p.semaphore("t_sums_ready")
    odd_copied = p.semaphore("t_odd_copied")
    combined = p.semaphore("t_combined")
    chain = p.semaphore("dve_chain")
    with ExitStack() as local:
        sb = lambda name, shape: local.enter_context(nc.sbuf_tensor(f"t_{name}", shape, F32))
        matrix = sb("matrix", [P, 2, 2, LAT])
        cross, odd = sb("cross", [P, 2, W]), sb("odd", [P, 2, W])
        with nc.Block() as block:
            @block.sync
            def _(sp):
                for f in range(F_TILES):
                    if f >= 2:
                        sp.wait_ge(sums_ready, 2 * (f - 1))
                    sp.dma_start(matrix[:, f % 2], p.dram["transform"][f]).then_inc(loaded[f % 2], 16)

            @block.tensor
            def _(pe):
                for f in range(F_TILES):
                    pe.wait_ge(loaded[f % 2], 16 * (f // 2 + 1))
                    for part, taps in ((0, sums), (1, differences)):
                        if f:
                            pe.wait_ge(combined, 2 * (f - 1) + part + 1)
                        for t in range(KT):
                            left = matrix[:, f % 2, part, t * P:(t + 1) * P]
                            for n, right in enumerate((u_tok, taps)):
                                last = nc.tensor.matmul(p.psum[:, 4 * part + 2 * (t // 4) + n, :], left, right[:, t, :],
                                                        start=(t % 4 == 0), stop=(t % 4 == 3))
                        last.then_inc(sums_ready, 1)

            @block.scalar
            def _(act):
                for m in range(2 * F_TILES):
                    act.wait_ge(sums_ready, m + 1)
                    if m:
                        act.wait_ge(combined, m)
                    nc.scalar.copy(odd[:, :, :], p.psum[:, 4 * (m % 2) + 2:4 * (m % 2) + 4, :]).then_inc(odd_copied, 1)

            @block.vector
            def _(dve):
                made = [0]

                def then(instruction):
                    made[0] += 1
                    instruction.then_inc(chain, 1)
                    dve.wait_ge(chain, made[0])

                for f in range(F_TILES):
                    for part in range(2):
                        dve.wait_ge(odd_copied, 2 * f + part + 1)
                        even = p.psum[:, 4 * part:4 * part + 2, :]
                        nc.vector.tensor_tensor(spectrum[:, part, 0], even, odd[:, :, :], ALU.add)
                        first, second = (even, odd[:, :, :]) if part == 0 else (odd[:, :, :], even)
                        nc.vector.tensor_tensor(spectrum[:, part, 1], first, second, ALU.subtract).then_inc(combined, 1)
                    dve.wait_ge(combined, 2 * f + 2)
                    u_cos, u_sin = (spectrum[:, part, :, 0] for part in range(2))
                    k_cos, k_sin = (spectrum[:, part, :, 1] for part in range(2))
                    nc.vector.tensor_tensor(whole[:, 0], u_cos, k_cos, ALU.mult)
                    nc.vector.tensor_tensor(whole[:, 1], u_cos, k_sin, ALU.mult)
                    then(nc.vector.tensor_tensor(cross[:, :, :], u_sin, k_sin, ALU.mult))
                    then(nc.vector.tensor_tensor(whole[:, 0], whole[:, 0], cross[:, :, :], ALU.subtract))
                    then(nc.vector.tensor_tensor(cross[:, :, :], u_sin, k_cos, ALU.mult))
                    then(nc.vector.tensor_tensor(whole[:, 1], whole[:, 1], cross[:, :, :], ALU.add))
                    for out, n, signs in ((real, 0, (ALU.add, ALU.subtract)), (imag, 1, (ALU.subtract, ALU.add))):
                        for parity in range(2):
                            last = nc.vector.tensor_tensor(out[:, f, parity, :], whole[:, n, 0], whole[:, n, 1], signs[parity])
                    then(last)


def stage_transform_back(p, real, imag, magnitudes, uT, x0T, mix):
    nc = p.nc
    p.begin_stage()
    loaded = p.semaphores("t_loaded", 2)
    norms_ready = p.semaphore("b_norms_ready")
    used = p.semaphore("b_used")
    products_ready = p.semaphore("b_products_ready")
    biased = p.semaphore("b_biased")
    done = p.semaphore("b_done")
    stored = p.semaphore("b_stored")
    chain = p.semaphore("dve_chain")
    with ExitStack() as local:
        matrix = local.enter_context(nc.sbuf_tensor("b_matrix", [P, 2, 2, LAT], F32))
        norm = local.enter_context(nc.sbuf_tensor("b_norm", [P, 2, WT], F32))
        with nc.Block() as block:
            @block.sync
            def _(sp):
                for f in range(F_TILES):
                    if f >= 2:
                        sp.wait_ge(used, f - 1)
                    sp.dma_start(matrix[:, f % 2], p.dram["transform_back"][f]).then_inc(loaded[f % 2], 16)
                sp.wait_ge(done, WT)
                sp.dma_start(mix[WT:2 * WT, :, CTX:TOK].rearrange("k p t -> p k t"), uT[:, :, :]).then_inc(stored, 16)
                sp.wait_ge(stored, 16)

            @block.tensor
            def _(pe):
                for j in range(WT):
                    last = nc.tensor.matmul(p.psum[:, 0, j:j + 1], magnitudes[:, j * P:(j + 1) * P], p.const("ones")[:, 0:1],
                                            start=True, stop=True)
                last.then_inc(norms_ready, 1)
                pe.wait_ge(norms_ready, 2)
                for f in range(F_TILES):
                    pe.wait_ge(loaded[f % 2], 16 * (f // 2 + 1))
                    for j in range(WT):
                        for part, spectrum in ((0, real), (1, imag)):
                            for parity in range(2):
                                last = nc.tensor.matmul(p.psum[:, 2 * j + parity, :], spectrum[:, f, parity, j * P:(j + 1) * P],
                                                        matrix[:, f % 2, part, parity * BANK:(parity + 1) * BANK],
                                                        start=(f == 0 and part == 0), stop=(f == F_TILES - 1 and part == 1))
                        if f == F_TILES - 1:
                            last.then_inc(products_ready, 1)
                    if f < F_TILES - 1:
                        last.then_inc(used, 1)

            @block.vector
            def _(dve):
                dve.wait_ge(norms_ready, 1)
                nc.vector.tensor_scalar(norm[:, 0, :], p.psum[:, 0, 0:WT], float(LAT), None, ALU.mult).then_inc(chain, 1)
                dve.wait_ge(chain, 1)
                nc.vector.reciprocal(norm[:, 1, :], norm[:, 0, :]).then_inc(norms_ready, 1)
                for j in range(WT):
                    nc.vector.tensor_scalar(uT[:, j, :], uT[:, j, :], p.param("y_bias", j), None, ALU.mult).then_inc(biased, 1)
                dve.wait_ge(norms_ready, 2)
                for j in range(WT):
                    dve.wait_ge(products_ready, j + 1)
                    dve.wait_ge(biased, j + 1)
                    by_parity = uT[:, j, :].rearrange("p (n e) -> p e n", e=2)
                    nc.vector.scalar_tensor_tensor(by_parity, p.psum[:, 2 * j:2 * j + 2, :], norm[:, 1, j:j + 1], by_parity,
                                                   ALU.mult, ALU.add).then_inc(chain, 1)
                    dve.wait_ge(chain, j + 2)
                    nc.vector.tensor_tensor(uT[:, j, :], uT[:, j, :], x0T[:, j, :], ALU.mult).then_inc(done, 1)


def hyena_branch(p, arena, hT, mix):
    nc = p.nc
    w_in = p.dram["l1_w_in"]
    free = arena[:, KT * TOK:]
    lat = lambda i: free[:, i * WT * LAT:(i + 1) * WT * LAT].rearrange("p (j t) -> p j t", j=WT)
    with ExitStack() as outer:
        so = lambda name, shape: outer.enter_context(nc.sbuf_tensor(name, shape, F32))
        uT, x0T, zT = (so(f"y_{n}T", [P, WT, LAT]) for n in ("u", "x0", "z"))
        raw, x1T = lat(0), lat(1)
        stage_project(
            p, "y", hT, w_in,
            [(5 * W + i * W, W, ACT.Copy, raw, False, LAT_GROUPS) for i in range(3)] + [(8 * W, W, ACT.Silu, zT, False, LAT_GROUPS)],
            finish={i: conv_product(p, raw, uT, out, i) for i, out in enumerate((None, x0T, x1T))})
        sums, differences = so("y_sums", [P, KT, W]), so("y_differences", [P, KT, W])
        magnitudes = so("y_magnitudes", [P, W])
        stage_filters(p, sums, differences, magnitudes)
        u_tok = so("y_u_tok", [P, KT, W])
        stage_turn_u(p, uT, u_tok, x0T, zT)
        real, imag = (free[:, i * KT * W:(i + 1) * KT * W].rearrange("p (f e n) -> p f e n", f=F_TILES, e=2)
                      for i in range(2))
        spectrum = zT.rearrange("p j (a n) -> p (j a) n", a=2).rearrange("p (c f u) n -> p c f u n", c=2, f=2)
        whole = free[:, 2 * KT * W:2 * KT * W + 4 * W].rearrange("p (c f n) -> p c f n", c=2, f=2)
        stage_transform(p, u_tok, sums, differences, real, imag, spectrum, whole)
        stage_transform_back(p, real, imag, magnitudes, uT, x0T, mix)


def grid_columns(a):
    columns_per_tile = P // GRID_H

    def rows(t):
        first = (t - CTX_TILES) * columns_per_tile
        return a.rearrange("(r c) n -> c r n", c=GRID_W)[first:first + columns_per_tile]

    return rows


def build_program(nc, dram, out):
    with ExitStack() as ctx:
        p = Program(nc, ctx, dram)
        arena = p.keep("arena", [P, 2 * KT * TOK])
        hT = arena[:, 0:KT * TOK].rearrange("p (k t) -> p k t", k=KT)
        free = arena[:, KT * TOK:]
        tile = lambda a: (lambda t: a[t * P:(t + 1) * P, :])
        mix, gate, x0, x1 = p.scratch["mix"], p.scratch["gate"], tile(dram["x_tok"]), tile(p.scratch["x1"])
        stage_copies(p, [(p.consts[:, :], dram["consts"]), (p.params[:, :], dram["params"])])
        stage_modulated_norm(p, 0, x0, gate[0], hT)
        mlstm_branch(p, free, hT, mix)
        rwkv_branch(p, arena, hT, mix, p.scratch["spill"])
        stage_output(p, 0, arena, mix, gate[0], x0, range(TILES), x1, p.x1_stored)
        stage_modulated_norm(p, 1, x1, gate[1], hT)
        hyena_branch(p, arena, hT, mix)
        hgrn_branch(p, arena, hT, mix)
        stage_output(p, 1, arena, mix, gate[1], grid_columns(p.scratch["x1"][CTX:TOK]), LAT_TILES, grid_columns(out),
                     p.out_stored, dram["final_gain"])


def host_arrays(inputs):
    a = {k: np.ascontiguousarray(v) for k, v in inputs.items()}
    f = np.float32

    def tiles(v):
        return v.reshape(-1, P).T

    def rows(v, n=P):
        out = np.zeros((P, 1), f)
        out[:v.size, 0] = v.reshape(-1)
        return out

    gate_b = a["l0_mlstm_gate_b"].reshape(2, 2, M_HEADS)
    gate_cols = np.zeros((D, 2, GATE_ROWS), f)
    gate_bias = np.zeros((2, P, 1), f)
    first = 5 * W
    for kind in range(2):
        for d in range(2):
            at = first + (d * 2 + kind) * M_HEADS
            gate_cols[:, kind, 32 * d:32 * d + M_HEADS] = a["l0_w_in"][:, at:at + M_HEADS]
            gate_bias[kind, 32 * d:32 * d + M_HEADS, 0] = gate_b[d, kind]
    parts = {
        "l0_norm_g": tiles(a["l0_norm_g"]), "l1_norm_g": tiles(a["l1_norm_g"]),
        "conv_w": tiles(a["l0_mlstm_conv_w"].reshape(-1)), "m_norm_g": tiles(a["l0_mlstm_norm_g"]),
        "r_mu": tiles(a["l0_rwkv_mu"].reshape(-1)), "r_w0": tiles(a["l0_rwkv_w0"].reshape(-1)),
        "r_a0": tiles(a["l0_rwkv_a0"].reshape(-1)), "r_k_k": tiles(a["l0_rwkv_k_k"]), "r_k_a": tiles(a["l0_rwkv_k_a"]),
        "r_r_k": tiles(a["l0_rwkv_r_k"].reshape(-1)), "r_ln_w": tiles(a["l0_rwkv_ln_w"]), "r_ln_b": tiles(a["l0_rwkv_ln_b"]),
        "lower": tiles(a["hgrn_lower_bounds"].reshape(-1)), "g_norm_g": tiles(a["l1_hgrn_norm_g"]),
        "short_w": tiles(a["l1_hyena_short_w"].reshape(-1)), "short_b": tiles(a["l1_hyena_short_b"]),
        "y_bias": tiles(a["l1_hyena_bias"]), "b1": rows(a["l1_hyena_b1"]), "b2": rows(a["l1_hyena_b2"]),
        "gate_b_i": gate_bias[0], "gate_b_f": gate_bias[1],
        "c": np.concatenate([a["c"].reshape(P, KT), a["c_ctx"].reshape(P, KT)], axis=1),
    }
    assert all(parts[n].shape[1] == PARAMS[n][1] for n in PARAMS)
    out = {
        "x_tok": np.concatenate([a["ctx"][0], a["x"][0]], axis=0),
        "params": np.ascontiguousarray(np.concatenate([parts[n] for n in PARAMS], axis=1)),
        "consts": const_common(), "const_mlstm": const_mlstm(), "const_rwkv": const_rwkv(),
        "w_up": a["l0_rwkv_w_up"].reshape(P, W), "a_up": a["l0_rwkv_a_up"].reshape(P, W),
        "gate_i": np.ascontiguousarray(gate_cols[:, 0]), "gate_f": np.ascontiguousarray(gate_cols[:, 1]),
        "mod_b0": np.stack([a["l0_mod_b"]] * 2), "mod_b1": np.stack([a["l1_mod_b"]] * 2),
    }
    out["const_hgrn"] = const_hgrn()
    out["const_spread"] = const_spread()
    out["final_gain"] = np.tile(a["final_norm_g"], (P, 1))
    out.update(const_hyena())
    for n in ("l1_hyena_w1", "l1_hyena_w2", "l1_hyena_w3", "l0_mod_w", "l1_mod_w", "l0_w_in", "l0_w_out", "l1_w_in", "l1_w_out"):
        out[n] = a[n]
    return out


def kernel(**inputs):
    import concourse.bacc as bacc
    from concourse.bass_utils import run_bass_kernel_spmd

    nc = bacc.Bacc("TRN2", target_bir_lowering=False, num_devices=1)
    arrays, dram = {}, {}
    for name, a in host_arrays(inputs).items():
        arrays[f"in_{name}"] = a
        dram[name] = nc.dram_tensor(f"in_{name}", a.shape, mybir.dt.from_np(a.dtype), kind="ExternalInput").ap()
    out = nc.dram_tensor("out_x", (LAT, D), F32, kind="ExternalOutput").ap()
    build_program(nc, dram, out)
    r = run_bass_kernel_spmd(nc, [arrays], core_ids=[0])
    return r.results[0]["out_x"].reshape(1, LAT, D)
```
